# Optimizing a Trainium2 kernel written in Bass

```python
import math
import jax, jax.numpy as jnp
from jax import lax
import numpy as np

D_MODEL = 1024
BATCH = 1
SEQ = 256
DEPTH = 2

D_FF = 2816
CONV_K = 4
SSM_EXPAND = 2
SSM_INNER = SSM_EXPAND * D_MODEL
SSM_HEAD_DIM = 64
SSM_HEADS = SSM_INNER // SSM_HEAD_DIM
SSM_GROUPS = 4
SSM_STATE = 128
SSM_CONV_DIM = SSM_INNER + 2 * SSM_GROUPS * SSM_STATE
SSM_CHUNK = 128
DN_HEADS = 8
DN_HEAD_K = 128
DN_HEAD_V = 128
DN_K_DIM = DN_HEADS * DN_HEAD_K
DN_V_DIM = DN_HEADS * DN_HEAD_V
DN_CONV_DIM = 2 * DN_K_DIM + DN_V_DIM
DN_CHUNK = 64
IN_SPLIT_SIZES = (SSM_INNER, SSM_CONV_DIM, SSM_HEADS,
                  DN_CONV_DIM, DN_V_DIM, DN_HEADS, DN_HEADS,
                  D_MODEL, D_MODEL)
IN_DIM = sum(IN_SPLIT_SIZES)
EPS = 1e-6


def rms_norm(x, w):
    xf = x.astype(jnp.float32)
    y = xf * lax.rsqrt(jnp.mean(xf * xf, axis=-1, keepdims=True) + EPS)
    return (y * w.astype(jnp.float32)).astype(x.dtype)

def l2_norm(x):
    xf = x.astype(jnp.float32)
    return xf * lax.rsqrt(jnp.sum(xf * xf, axis=-1, keepdims=True) + EPS)

def swiglu(x, w_in, w_out):
    gate, up = jnp.split(x @ w_in, 2, axis=-1)
    return (jax.nn.silu(gate) * up) @ w_out

def causal_depthwise_conv(x, w, bias=None):
    K, C = w.shape
    y = lax.conv_general_dilated(
        x, w[:, None, :].astype(x.dtype), window_strides=(1,), padding=[(K - 1, 0)],
        dimension_numbers=("NWC", "WIO", "NWC"), feature_group_count=C)
    if bias is not None:
        y = y + bias.astype(x.dtype)
    return y

def ssd_chunked(x, dt, a, Bm, Cm):
    b, S, H, P = x.shape
    G, N = Bm.shape[2], Bm.shape[3]
    hg = H // G
    L = SSM_CHUNK
    nc = S // L
    f32 = jnp.float32
    xdt = (x.astype(f32) * dt[..., None]).reshape(b, nc, L, G, hg, P)
    log_a = (dt * a).reshape(b, nc, L, G, hg)
    Bc = Bm.astype(f32).reshape(b, nc, L, G, N)
    Cc = Cm.astype(f32).reshape(b, nc, L, G, N)
    a_cum = jnp.cumsum(log_a, axis=2)
    causal = jnp.tril(jnp.ones((L, L), dtype=bool))[None, None, :, :, None, None]
    seg = a_cum[:, :, :, None] - a_cum[:, :, None, :]
    decay = jnp.where(causal, jnp.exp(jnp.where(causal, seg, 0.0)), 0.0)
    cb = jnp.einsum("bclgn,bcsgn->bclsg", Cc, Bc)
    y_diag = jnp.einsum("bclsg,bclsgh,bcsghp->bclghp", cb, decay, xdt)
    decay_to_end = jnp.exp(a_cum[:, :, -1:] - a_cum)
    chunk_states = jnp.einsum("bclgn,bclgh,bclghp->bcghpn", Bc, decay_to_end, xdt)
    chunk_decay = jnp.exp(a_cum[:, :, -1])

    def step(state, inp):
        cs, cd = inp
        return state * cd[..., None, None] + cs, state

    s0 = jnp.zeros((b, G, hg, P, N), f32)
    _, states_in = lax.scan(step, s0, (jnp.moveaxis(chunk_states, 1, 0), jnp.moveaxis(chunk_decay, 1, 0)))
    states_in = jnp.moveaxis(states_in, 0, 1)
    y_off = jnp.einsum("bclgn,bcghpn,bclgh->bclghp", Cc, states_in, jnp.exp(a_cum))
    return (y_diag + y_off).reshape(b, S, H, P)

def gated_delta_rule_chunked(q, k, v, g, beta):
    b, S, H, dk = q.shape
    dv = v.shape[-1]
    C = DN_CHUNK
    n = S // C
    f32 = jnp.float32

    def chunks(t):
        return jnp.moveaxis(t.astype(f32).reshape(b, n, C, *t.shape[2:]), 2, 3)

    q, k, v, g, beta = (chunks(t) for t in (q, k, v, g, beta))
    G = jnp.cumsum(g, axis=-1)
    incl = jnp.tril(jnp.ones((C, C), dtype=bool))
    strict = jnp.tril(jnp.ones((C, C), dtype=bool), -1)
    diff = G[..., :, None] - G[..., None, :]
    decay = jnp.where(incl, jnp.exp(jnp.where(incl, diff, 0.0)), 0.0)
    kb = k * beta[..., None]
    M = jnp.where(strict, jnp.einsum("bnhid,bnhjd->bnhij", kb, k) * decay, 0.0)
    eye = jnp.eye(C, dtype=f32)
    rhs = jnp.concatenate([v * beta[..., None], kb * jnp.exp(G)[..., None]], axis=-1)
    sol = lax.linalg.triangular_solve(eye + M, rhs, left_side=True, lower=True, unit_diagonal=True)
    u, w = sol[..., :dv], sol[..., dv:]
    a_qk = jnp.einsum("bnhid,bnhjd->bnhij", q, k) * decay
    q_dec = q * jnp.exp(G)[..., None]
    g_last = G[..., -1]
    k_dec = k * jnp.exp(g_last[..., None] - G)[..., None]

    def step(state, inp):
        q_c, a_c, u_c, w_c, k_c, gl = inp
        v_new = u_c - jnp.einsum("bhck,bhkv->bhcv", w_c, state)
        o = jnp.einsum("bhck,bhkv->bhcv", q_c, state) + jnp.einsum("bhij,bhjv->bhiv", a_c, v_new)
        state = state * jnp.exp(gl)[..., None, None] + jnp.einsum("bhck,bhcv->bhkv", k_c, v_new)
        return state, o

    xs = tuple(jnp.moveaxis(t, 1, 0) for t in (q_dec, a_qk, u, w, k_dec, g_last))
    s0 = jnp.zeros((b, H, dk, dv), f32)
    _, o = lax.scan(step, s0, xs)
    o = jnp.moveaxis(jnp.moveaxis(o, 0, 1), 2, 3)
    return o.reshape(b, S, H, dv)

def mamba2_branch(z, xbc, dt_raw, conv_w, conv_b, dt_bias, a_log, d_skip, norm_w):
    b, S, _ = xbc.shape
    f32 = jnp.float32
    xbc = jax.nn.silu(causal_depthwise_conv(xbc, conv_w, conv_b))
    xs, Bm, Cm = jnp.split(xbc, [SSM_INNER, SSM_INNER + SSM_GROUPS * SSM_STATE], axis=-1)
    xs = xs.reshape(b, S, SSM_HEADS, SSM_HEAD_DIM)
    Bm = Bm.reshape(b, S, SSM_GROUPS, SSM_STATE)
    Cm = Cm.reshape(b, S, SSM_GROUPS, SSM_STATE)
    dt = jax.nn.softplus(dt_raw.astype(f32) + dt_bias.astype(f32))
    a = -jnp.exp(a_log.astype(f32))
    y = ssd_chunked(xs, dt, a, Bm, Cm) + xs.astype(f32) * d_skip.astype(f32)[:, None]
    yg = (y.reshape(b, S, SSM_INNER) * jax.nn.silu(z.astype(f32))).reshape(b, S, SSM_GROUPS, -1)
    yg = yg * lax.rsqrt(jnp.mean(yg * yg, axis=-1, keepdims=True) + EPS)
    return (yg.reshape(b, S, SSM_INNER) * norm_w.astype(f32)).astype(z.dtype)

def deltanet_branch(qkv, z, b_raw, a_raw, conv_w, dt_bias, a_log, norm_w):
    b, S, _ = qkv.shape
    f32 = jnp.float32
    qkv = jax.nn.silu(causal_depthwise_conv(qkv, conv_w))
    q, k, v = jnp.split(qkv, [DN_K_DIM, 2 * DN_K_DIM], axis=-1)
    q = l2_norm(q.reshape(b, S, DN_HEADS, DN_HEAD_K)) * (DN_HEAD_K ** -0.5)
    k = l2_norm(k.reshape(b, S, DN_HEADS, DN_HEAD_K))
    v = v.reshape(b, S, DN_HEADS, DN_HEAD_V)
    beta = jax.nn.sigmoid(b_raw.astype(f32))
    g = -jnp.exp(a_log.astype(f32)) * jax.nn.softplus(a_raw.astype(f32) + dt_bias.astype(f32))
    o = gated_delta_rule_chunked(q, k, v, g, beta)
    o = o * lax.rsqrt(jnp.mean(o * o, axis=-1, keepdims=True) + EPS) * norm_w.astype(f32)
    o = o * jax.nn.silu(z.astype(f32).reshape(b, S, DN_HEADS, DN_HEAD_V))
    return o.reshape(b, S, DN_V_DIM).astype(z.dtype)

def first_inputs(seed: int = 0) -> dict:
    key = jax.random.key(seed)
    k = jax.random.split(key, 23)
    f32 = jnp.float32

    def dense(kk, shape, fan_in):
        return jax.random.normal(kk, shape, f32) * fan_in ** -0.5

    def gain(kk, shape):
        return 1.0 + 0.02 * jax.random.normal(kk, shape, f32)

    def dt_bias(kk, shape):
        u = jax.random.uniform(kk, shape, f32)
        dt = jnp.exp(u * (math.log(0.1) - math.log(1e-3)) + math.log(1e-3))
        return dt + jnp.log(-jnp.expm1(-dt))

    def a_log(kk, shape):
        return jnp.log(jax.random.uniform(kk, shape, f32, 1.0, 16.0))

    L = DEPTH
    return {
        "x": jax.random.normal(k[0], (BATCH, SEQ, D_MODEL), f32),
        "ffn1_norm": gain(k[1], (L, D_MODEL)),
        "ffn1_w_in": dense(k[2], (L, D_MODEL, 2 * D_FF), D_MODEL),
        "ffn1_w_out": dense(k[3], (L, D_FF, D_MODEL), D_FF),
        "mix_norm": gain(k[4], (L, D_MODEL)),
        "w_in": dense(k[5], (L, D_MODEL, IN_DIM), D_MODEL),
        "ssm_conv_w": dense(k[6], (L, CONV_K, SSM_CONV_DIM), CONV_K),
        "ssm_conv_b": 0.02 * jax.random.normal(k[7], (L, SSM_CONV_DIM), f32),
        "ssm_dt_bias": dt_bias(k[8], (L, SSM_HEADS)),
        "ssm_a_log": a_log(k[9], (L, SSM_HEADS)),
        "ssm_d": 1.0 + 0.1 * jax.random.normal(k[10], (L, SSM_HEADS), f32),
        "ssm_norm": gain(k[11], (L, SSM_INNER)),
        "ssm_w_branch": dense(k[12], (L, SSM_INNER, D_MODEL), SSM_INNER),
        "dn_conv_w": dense(k[13], (L, CONV_K, DN_CONV_DIM), CONV_K),
        "dn_dt_bias": dt_bias(k[14], (L, DN_HEADS)),
        "dn_a_log": a_log(k[15], (L, DN_HEADS)),
        "dn_norm": gain(k[16], (L, DN_HEAD_V)),
        "dn_w_branch": dense(k[17], (L, DN_V_DIM, D_MODEL), DN_V_DIM),
        "w_out": dense(k[18], (L, D_MODEL, D_MODEL), D_MODEL),
        "ffn2_norm": gain(k[19], (L, D_MODEL)),
        "ffn2_w_in": dense(k[20], (L, D_MODEL, 2 * D_FF), D_MODEL),
        "ffn2_w_out": dense(k[21], (L, D_FF, D_MODEL), D_FF),
        "final_norm": gain(k[22], (D_MODEL,)),
    }

def first_block(x, ffn1_norm, ffn1_w_in, ffn1_w_out, mix_norm, w_in, ssm_conv_w, ssm_conv_b,
              ssm_dt_bias, ssm_a_log, ssm_d, ssm_norm, ssm_w_branch, dn_conv_w, dn_dt_bias,
              dn_a_log, dn_norm, dn_w_branch, w_out, ffn2_norm, ffn2_w_in, ffn2_w_out, final_norm):
    split_points = [int(p) for p in np.cumsum(IN_SPLIT_SIZES)[:-1]]
    h = x
    for l in range(DEPTH):
        h = h + 0.5 * swiglu(rms_norm(h, ffn1_norm[l]), ffn1_w_in[l], ffn1_w_out[l])
        u = rms_norm(h, mix_norm[l])
        (z_s, xbc, dt_s, qkv, z_d, b_d, a_d, gate_s, gate_d) = jnp.split(u @ w_in[l], split_points, axis=-1)
        y_s = mamba2_branch(z_s, xbc, dt_s, ssm_conv_w[l], ssm_conv_b[l], ssm_dt_bias[l],
                            ssm_a_log[l], ssm_d[l], ssm_norm[l])
        y_d = deltanet_branch(qkv, z_d, b_d, a_d, dn_conv_w[l], dn_dt_bias[l],
                              dn_a_log[l], dn_norm[l])
        merged = (jax.nn.sigmoid(gate_s) * (y_s @ ssm_w_branch[l])
                  + jax.nn.sigmoid(gate_d) * (y_d @ dn_w_branch[l]))
        h = h + merged @ w_out[l]
        h = h + 0.5 * swiglu(rms_norm(h, ffn2_norm[l]), ffn2_w_in[l], ffn2_w_out[l])
    return rms_norm(h, final_norm)


HEAD_DIM = 64
N_HEADS_MOBA = 6
N_HEADS_MLA = 4
N_HEADS_FOX = 6
MOBA_BLOCK = 256
MOBA_TOPK = 3
MOBA_Q_BLOCK = 32
Q_BLOCK = 128
MLA_Q_RANK = 256
MLA_KV_RANK = 128
MLA_NOPE_DIM = 64
MLA_ROPE_DIM = 32
MLA_V_DIM = 64
MLA_QK_DIM = MLA_NOPE_DIM + MLA_ROPE_DIM
ROPE_THETA = 10000.0
T5_BUCKETS = 32
T5_MAX_DIST = 1024
CONV_WIDTH = 3
NORM_EPS = 1e-6
NEG_INF = -1e30

W_MOBA = N_HEADS_MOBA * HEAD_DIM
W_MLA = N_HEADS_MLA * MLA_V_DIM
W_FOX = N_HEADS_FOX * HEAD_DIM
MIX_WIDTH = W_MOBA + W_MLA + W_FOX
PROJ_SIZES = (W_MOBA, W_MOBA, W_MOBA, MLA_Q_RANK, MLA_KV_RANK, MLA_ROPE_DIM, W_FOX, W_FOX, W_FOX, N_HEADS_FOX)
PROJ_COLS = sum(PROJ_SIZES)


def rms_norm_2(x, g):
    xf = x.astype(jnp.float32)
    y = xf * lax.rsqrt(jnp.mean(xf * xf, axis=-1, keepdims=True) + NORM_EPS)
    return (y * g.astype(jnp.float32)).astype(x.dtype)

def split_heads(t, n, d):
    b, s, _ = t.shape
    return t.reshape(b, s, n, d).transpose(0, 2, 1, 3)

def merge_heads(t):
    b, h, s, d = t.shape
    return t.transpose(0, 2, 1, 3).reshape(b, s, h * d)

def rotary(t, pos):
    half = t.shape[-1] // 2
    inv = ROPE_THETA ** (-jnp.arange(half, dtype=jnp.float32) / half)
    ang = pos.astype(jnp.float32)[:, None] * inv[None, :]
    cos, sin = jnp.cos(ang), jnp.sin(ang)
    t1 = t[..., :half].astype(jnp.float32)
    t2 = t[..., half:].astype(jnp.float32)
    return jnp.concatenate([t1 * cos - t2 * sin, t1 * sin + t2 * cos], axis=-1).astype(t.dtype)

def t5_bucket(rel):
    n = jnp.maximum(rel, 0)
    exact = T5_BUCKETS // 2
    large = exact + (jnp.log(jnp.maximum(n, 1).astype(jnp.float32) / exact)
                     / math.log(T5_MAX_DIST / exact) * (T5_BUCKETS - exact)).astype(jnp.int32)
    return jnp.where(n < exact, n, jnp.minimum(large, T5_BUCKETS - 1))

def moba_attention(q, k, v, rel_bias):
    b, h, s, dh = q.shape
    nb = -(-s // MOBA_BLOCK)
    pad = nb * MOBA_BLOCK - s
    kp = jnp.pad(k, ((0, 0), (0, 0), (0, pad), (0, 0)))
    vp = jnp.pad(v, ((0, 0), (0, 0), (0, pad), (0, 0)))
    k_blocks = kp.reshape(b, h, nb, MOBA_BLOCK, dh)
    v_blocks = vp.reshape(b, h, nb, MOBA_BLOCK, dh)
    k_mean = jnp.mean(k_blocks, axis=3)
    topk = min(MOBA_TOPK, nb)
    bias_tab = rel_bias.T
    scale = dh ** -0.5
    b_idx = jnp.arange(b)[:, None, None, None]
    h_idx = jnp.arange(h)[None, :, None, None]
    blk_pos = jnp.arange(MOBA_BLOCK)

    def chunk(c):
        q_start = c * MOBA_Q_BLOCK
        qc = lax.dynamic_slice_in_dim(q, q_start, MOBA_Q_BLOCK, axis=2)
        q_pos = q_start + jnp.arange(MOBA_Q_BLOCK)
        own = q_start // MOBA_BLOCK
        gate = jnp.einsum('bhqd,bhnd->bhqn', qc, k_mean).astype(jnp.float32)
        gate = jnp.where(jnp.arange(nb) < own, gate, NEG_INF)
        _, sel = lax.top_k(gate, topk)
        valid = jnp.arange(topk) < own
        k_sel = k_blocks[b_idx, h_idx, sel]
        v_sel = v_blocks[b_idx, h_idx, sel]
        k_pos_sel = sel[..., None] * MOBA_BLOCK + blk_pos
        s_sel = jnp.einsum('bhqd,bhqnkd->bhqnk', qc, k_sel).astype(jnp.float32) * scale
        s_sel = s_sel + bias_tab[h_idx[..., None], t5_bucket(q_pos[:, None, None] - k_pos_sel)]
        s_sel = jnp.where(valid[:, None], s_sel, NEG_INF)
        s_sel = s_sel.reshape(b, h, MOBA_Q_BLOCK, topk * MOBA_BLOCK)
        own_start = own * MOBA_BLOCK
        k_own = lax.dynamic_slice_in_dim(kp, own_start, MOBA_BLOCK, axis=2)
        v_own = lax.dynamic_slice_in_dim(vp, own_start, MOBA_BLOCK, axis=2)
        rel = q_pos[:, None] - (own_start + blk_pos)[None, :]
        s_own = jnp.einsum('bhqd,bhkd->bhqk', qc, k_own).astype(jnp.float32) * scale
        s_own = jnp.where(rel >= 0, s_own + bias_tab[:, t5_bucket(rel)], NEG_INF)
        p = jax.nn.softmax(jnp.concatenate([s_sel, s_own], axis=-1), axis=-1).astype(v.dtype)
        p_sel = p[..., :topk * MOBA_BLOCK].reshape(b, h, MOBA_Q_BLOCK, topk, MOBA_BLOCK)
        p_own = p[..., topk * MOBA_BLOCK:]
        return (jnp.einsum('bhqnk,bhqnkd->bhqd', p_sel, v_sel)
                + jnp.einsum('bhqk,bhkd->bhqd', p_own, v_own))

    outs = lax.map(chunk, jnp.arange(s // MOBA_Q_BLOCK))
    return outs.transpose(1, 2, 0, 3, 4).reshape(b, h, s, dh)

def causal_block_attention(q, k, v, scale, decay=None):
    b, h, s, _ = q.shape
    dv = v.shape[-1]
    k_pos = jnp.arange(s)

    def chunk(c):
        q_start = c * Q_BLOCK
        qc = lax.dynamic_slice_in_dim(q, q_start, Q_BLOCK, axis=2)
        q_pos = q_start + jnp.arange(Q_BLOCK)
        sc = jnp.einsum('bhqd,bhkd->bhqk', qc, k).astype(jnp.float32) * scale
        if decay is not None:
            dq = lax.dynamic_slice_in_dim(decay, q_start, Q_BLOCK, axis=2)
            sc = sc + dq[..., None] - decay[:, :, None, :]
        sc = jnp.where(k_pos[None, :] <= q_pos[:, None], sc, NEG_INF)
        p = jax.nn.softmax(sc, axis=-1).astype(v.dtype)
        return jnp.einsum('bhqk,bhkd->bhqd', p, v)

    outs = lax.map(chunk, jnp.arange(s // Q_BLOCK))
    return outs.transpose(1, 2, 0, 3, 4).reshape(b, h, s, dv)

def hybrid_mixer(h, rel_bias, w_in, b_f, q_norm, kv_norm, w_uq, w_ukv, w_o):
    b, s, _ = h.shape
    pos = jnp.arange(s)
    proj = h @ w_in
    (a_q, a_k, a_v, c_q, c_kv, k_r, f_q, f_k, f_v, f_g) = jnp.split(
        proj, np.cumsum(PROJ_SIZES)[:-1].tolist(), axis=-1)

    out_a = moba_attention(split_heads(a_q, N_HEADS_MOBA, HEAD_DIM),
                           split_heads(a_k, N_HEADS_MOBA, HEAD_DIM),
                           split_heads(a_v, N_HEADS_MOBA, HEAD_DIM), rel_bias)

    qb = split_heads(rms_norm_2(c_q, q_norm) @ w_uq, N_HEADS_MLA, MLA_QK_DIM)
    kv = split_heads(rms_norm_2(c_kv, kv_norm) @ w_ukv, N_HEADS_MLA, MLA_NOPE_DIM + MLA_V_DIM)
    k_nope, v_b = kv[..., :MLA_NOPE_DIM], kv[..., MLA_NOPE_DIM:]
    q_b = jnp.concatenate([qb[..., :MLA_NOPE_DIM], rotary(qb[..., MLA_NOPE_DIM:], pos)], axis=-1)
    k_rope = jnp.broadcast_to(rotary(k_r[:, None], pos), (b, N_HEADS_MLA, s, MLA_ROPE_DIM))
    k_b = jnp.concatenate([k_nope, k_rope], axis=-1)
    out_b = causal_block_attention(q_b, k_b, v_b, MLA_QK_DIM ** -0.5)

    log_f = jax.nn.log_sigmoid(f_g.astype(jnp.float32) + b_f.astype(jnp.float32))
    decay = jnp.cumsum(log_f, axis=1).transpose(0, 2, 1)
    out_c = causal_block_attention(split_heads(f_q, N_HEADS_FOX, HEAD_DIM),
                                   split_heads(f_k, N_HEADS_FOX, HEAD_DIM),
                                   split_heads(f_v, N_HEADS_FOX, HEAD_DIM),
                                   HEAD_DIM ** -0.5, decay)

    merged = jnp.concatenate([merge_heads(out_a), merge_heads(out_b), merge_heads(out_c)], axis=-1)
    return merged @ w_o

def conv_ffn(h, w_up, conv_w, conv_b, w_down):
    u = h @ w_up
    u = lax.conv_general_dilated(u, conv_w[:, None, :], window_strides=(1,),
                                 padding=[(CONV_WIDTH - 1, 0)],
                                 dimension_numbers=('NWC', 'WIO', 'NWC'),
                                 feature_group_count=u.shape[-1]) + conv_b
    g, val = jnp.split(u, 2, axis=-1)
    return (jax.nn.gelu(g, approximate=True) * val) @ w_down

def second_inputs(seed: int = 0) -> dict:
    key = jax.random.key(seed)
    ks = jax.random.split(key, 20)
    f32 = jnp.float32

    def nrm(k, shape, fan_in):
        return jax.random.normal(k, shape, f32) * (fan_in ** -0.5)

    def gain(k, shape):
        return 1.0 + 0.1 * jax.random.normal(k, shape, f32)

    L = DEPTH
    return {
        "x": jax.random.normal(ks[0], (BATCH, SEQ, D_MODEL), f32),
        "rel_bias": 0.5 * jax.random.normal(ks[1], (T5_BUCKETS, N_HEADS_MOBA), f32),
        "ln_mix_pre": gain(ks[2], (L, D_MODEL)),
        "ln_mix_post": gain(ks[3], (L, D_MODEL)),
        "ln_ffn_pre": gain(ks[4], (L, D_MODEL)),
        "ln_ffn_post": gain(ks[5], (L, D_MODEL)),
        "w_in": nrm(ks[6], (L, D_MODEL, PROJ_COLS), D_MODEL),
        "b_f": 2.0 + 0.5 * jax.random.normal(ks[7], (L, N_HEADS_FOX), f32),
        "q_norm": gain(ks[8], (L, MLA_Q_RANK)),
        "kv_norm": gain(ks[9], (L, MLA_KV_RANK)),
        "w_uq": nrm(ks[10], (L, MLA_Q_RANK, N_HEADS_MLA * MLA_QK_DIM), MLA_Q_RANK),
        "w_ukv": nrm(ks[11], (L, MLA_KV_RANK, N_HEADS_MLA * (MLA_NOPE_DIM + MLA_V_DIM)), MLA_KV_RANK),
        "w_o": nrm(ks[12], (L, MIX_WIDTH, D_MODEL), MIX_WIDTH),
        "w_up": nrm(ks[13], (L, D_MODEL, 2 * D_FF), D_MODEL),
        "conv_w": nrm(ks[14], (L, CONV_WIDTH, 2 * D_FF), CONV_WIDTH),
        "conv_b": 0.01 * jax.random.normal(ks[15], (L, 2 * D_FF), f32),
        "w_down": nrm(ks[16], (L, D_FF, D_MODEL), D_FF),
    }

def second_block(x, rel_bias, ln_mix_pre, ln_mix_post, ln_ffn_pre, ln_ffn_post, w_in, b_f,
              q_norm, kv_norm, w_uq, w_ukv, w_o, w_up, conv_w, conv_b, w_down):
    for l in range(DEPTH):
        h = rms_norm_2(x, ln_mix_pre[l])
        x = x + rms_norm_2(hybrid_mixer(h, rel_bias, w_in[l], b_f[l], q_norm[l], kv_norm[l],
                                      w_uq[l], w_ukv[l], w_o[l]), ln_mix_post[l])
        h = rms_norm_2(x, ln_ffn_pre[l])
        x = x + rms_norm_2(conv_ffn(h, w_up[l], conv_w[l], conv_b[l], w_down[l]), ln_ffn_post[l])
    return x


def setup_inputs(seed=0):
    out = dict(first_inputs(seed))
    for name, value in second_inputs(seed + 1).items():
        if name != "x":
            out[name + "_2"] = value
    return out


def reference(
    x, ffn1_norm, ffn1_w_in, ffn1_w_out, mix_norm, w_in, ssm_conv_w, ssm_conv_b, ssm_dt_bias,
    ssm_a_log, ssm_d, ssm_norm, ssm_w_branch, dn_conv_w, dn_dt_bias, dn_a_log, dn_norm,
    dn_w_branch, w_out, ffn2_norm, ffn2_w_in, ffn2_w_out, final_norm, rel_bias_2, ln_mix_pre_2,
    ln_mix_post_2, ln_ffn_pre_2, ln_ffn_post_2, w_in_2, b_f_2, q_norm_2, kv_norm_2, w_uq_2,
    w_ukv_2, w_o_2, w_up_2, conv_w_2, conv_b_2, w_down_2,
):
    x = first_block(
        x, ffn1_norm, ffn1_w_in, ffn1_w_out, mix_norm, w_in, ssm_conv_w, ssm_conv_b,
        ssm_dt_bias, ssm_a_log, ssm_d, ssm_norm, ssm_w_branch, dn_conv_w, dn_dt_bias, dn_a_log,
        dn_norm, dn_w_branch, w_out, ffn2_norm, ffn2_w_in, ffn2_w_out, final_norm,
    )
    return second_block(
        x, rel_bias_2, ln_mix_pre_2, ln_mix_post_2, ln_ffn_pre_2, ln_ffn_post_2, w_in_2, b_f_2,
        q_norm_2, kv_norm_2, w_uq_2, w_ukv_2, w_o_2, w_up_2, conv_w_2, conv_b_2, w_down_2,
    )


_drawn_inputs = setup_inputs


def setup_inputs(seed=0):
    import zlib

    import numpy as np

    out = dict(_drawn_inputs(seed))
    spreads = {}
    factors = {'dn_norm': 4.252, 'ffn2_norm': 3.655, 'conv_b_2': 4.938, 'ssm_norm': 3.075}
    for name, (base, spread) in spreads.items():
        noise = np.random.default_rng([zlib.crc32(name.encode()), seed]).standard_normal(out[name].shape)
        drawn = base * np.exp(spread * noise) if base else spread * noise
        out[name] = __import__('jax').numpy.asarray(drawn.astype(out[name].dtype))
    for name, factor in factors.items():
        out[name] = (out[name] * factor).astype(out[name].dtype)
    return out
```

```python
from contextlib import ExitStack, contextmanager

import numpy as np
import concourse.bass as bass
from concourse import mybir

F32 = mybir.dt.float32
F32R = mybir.dt.float32r
ALU = mybir.AluOpType
FN = mybir.ActivationFunctionType
AX_X = mybir.AxisListType.X

P = 128
S = 256
D = 1024
ND = D // P
L = 2
FF = 2816
NF = FF // P
EPS = 1e-6
NEG = -1e30
SI, SG, SH, SP, SN = 2048, 4, 32, 64, 128
HG = SH // SG
SCONV = SI + 2 * SG * SN
DH, DK = 8, 128
DC = 64
DCONV = 3 * DH * DK
COL_Z, COL_XBC = 0, SI
COL_DT = COL_XBC + SCONV
COL_QKV = COL_DT + SH
COL_ZD = COL_QKV + DCONV
COL_B = COL_ZD + DH * DK
COL_A = COL_B + DH
COL_GS = COL_A + DH
COL_GD = COL_GS + D
AH, MH, XH_, HD = 6, 4, 6, 64
QR, KVR, ROPE = 256, 128, 32
QKD = 96
COL2_KR = 3 * AH * HD + QR + KVR
COL2_F = COL2_KR + ROPE
COL2_FG = COL2_F + 3 * XH_ * HD
KC2 = 3

def table(widths):
    at, out = 0, {}
    for name, n in widths:
        out[name] = (at, n)
        at += n
    return out, at


PAR1, NPAR1 = table([("ffn1_norm", ND), ("mix_norm", ND), ("ffn2_norm", ND), ("ssm_cw", 4 * SCONV // P),
                     ("ssm_cb", SCONV // P), ("ssm_d", SI // P), ("ssm_norm", SI // P),
                     ("dn_cw", 4 * DCONV // P), ("dn_norm", 1), ("ssm_dtb", 1), ("ssm_alog", 1),
                     ("dn_dtb", 1), ("dn_alog", 1)])
PAR2, NPAR2 = table([("mix_pre", ND), ("mix_post", ND), ("ffn_pre", ND), ("ffn_post", ND), ("b_f", 1),
                     ("q_norm", QR // P), ("kv_norm", 1), ("cw", KC2 * 2 * NF), ("cb", 2 * NF)])
CON0, NCON0 = table([("ident", P), ("final_norm", ND)])
LEVELS = 6
CON1, NCON1 = table([("causal", P), ("incl", P), ("strict", P), ("level", LEVELS * P)])
CON2, NCON2 = table([("mask", S + P), ("rot", P), ("cos", S), ("sin", S)])
CONT, NCONT = table([("flip", P), ("bucket", S + P)])


class Count:

    def __init__(self, const=0, terms=()):
        self.const, self.terms = const, tuple(t for t in terms if t[2])

    def __add__(self, n):
        return Count(self.const + n, self.terms)

    def value(self):
        v = self.const
        for _, reg, k in self.terms:
            v = reg * k + v
        return v


class Sem:

    def __init__(self, prog, name, virtual=False):
        self.sem = None if virtual else prog.ctx.enter_context(prog.nc.semaphore(name))
        self.name, self.count = name, Count()
        prog.sems.append(self)

    def inc(self, ins, n=1):
        ins.then_inc(self.sem, n)
        return self.later(n)

    def later(self, n):
        self.count = self.count + n
        return (self, self.count)

    def mark(self, ago=0):
        return (self, self.count + (-ago))


class Engine:

    def __init__(self, prog, eng, name):
        self.eng, self.own = eng, Sem(prog, "done_" + name)
        self.idle = Sem(prog, "idle_" + name)
        prog.engines.append(self)

    def done(self, ins):
        return self.own.inc(ins)

    def wait(self, *marks):
        for sem, count in marks:
            self.eng.wait_ge(sem.sem, count.value())


    def settle(self):
        self.eng.sem_inc(self.idle.sem, 1)


class Program:
    def __init__(self, nc, ctx, passes):
        self.nc, self.ctx, self.passes = nc, ctx, passes
        self.sems, self.engines, self.loops, self.joined = [], [], 0, []
        self.PE = Engine(self, nc.tensor, "pe")
        self.ACT = Engine(self, nc.scalar, "act")
        self.DVE = Engine(self, nc.vector, "dve")
        self.POOL = Engine(self, nc.gpsimd, "pool")
        self.SP = Engine(self, nc.sync, "sp")

    @contextmanager
    def loop(self, trips):
        me = self.loops
        self.loops += 1
        start = [s.count for s in self.sems]
        step = self.passes.get(me, [0] * len(start))
        at = self.ring_places()
        for e in self.engines:
            e.settle()
        with self.nc.Fori(0, trips) as i:
            for s, c, k in zip(self.sems, start, step):
                s.count = Count(c.const, c.terms + ((me, i, k),))
            yield i
            took = [s.count.const - c.const for s, c in zip(self.sems, start)]
            self.passes[me] = took
            assert at == self.ring_places(), "a pass must leave every ring where it found it"
        for s, c, k in zip(self.sems, start, took):
            s.count = Count(c.const + k * trips, c.terms)

    def join(self):
        marks = [s.mark() for s in self.joined]
        for e in (self.PE, self.ACT, self.DVE, self.POOL):
            e.wait(*marks)


RAW, SPL, OUTB = 4, 2, 4
BLK = 1024


class Stream:

    def __init__(self, k):
        pr = self.prog = k.prog
        self.k = k
        self.raw = [k.sb(f"raw{i}", [P, BLK]) for i in range(RAW)]
        self.hi = [k.sb(f"w_hi{i}", [P, BLK], F32R) for i in range(SPL)]
        self.lo = [k.sb(f"w_lo{i}", [P, BLK], F32R) for i in range(SPL)]
        self.s_raw = [Sem(pr, f"raw{i}_landed") for i in range(RAW)]
        self.s_hi, self.s_lo, self.s_mm, self.s_ev = (Sem(pr, n) for n in ("w_hi", "w_lo", "w_mm", "out_read"))
        self.want = [Sem(pr, f"raw{i}_wanted", True) for i in range(RAW)]
        self.loads = Sem(pr, "loads", True)
        self.load_at = self.split_at = self.mm_at = self.out_at = 0
        self.put_off = []
        pr.ring_places = lambda: (self.load_at, self.split_at, self.mm_at, self.out_at)
        self.outs = Sem(pr, "outs", True)
        for sem, n in ((self.s_lo, RAW), (self.s_mm, SPL), (self.s_ev, OUTB)):
            pr.nc.gpsimd.sem_inc(sem.sem, n)
            sem.later(n)

    def load(self, parts):
        pr, s = self.prog, self.load_at
        pr.SP.wait((self.s_lo, self.loads.count + 1))
        for view, src in parts:
            self.s_raw[s].inc(pr.nc.sync.dma_start(view(self.raw[s]), src), 16)
        self.loads.later(1)
        self.load_at = (s + 1) % RAW

    def split(self, cols=BLK):
        pr, s, b = self.prog, self.split_at, self.split_at % SPL
        self.want[s].later(32)
        pr.ACT.wait((self.s_raw[s], self.want[s].count), (self.s_mm, self.s_hi.count + 1))
        self.s_hi.inc(pr.nc.scalar.copy(self.hi[b][:, 0:cols], self.raw[s][:, 0:cols]))
        pr.DVE.wait(self.s_hi.mark())
        self.s_lo.inc(pr.nc.vector.tensor_tensor(self.lo[b][:, 0:cols], self.raw[s][:, 0:cols],
                                                 self.hi[b][:, 0:cols].bitcast(F32), ALU.subtract))
        self.split_at = (s + 1) % RAW

    def block(self, parts, emit, after=(), nxt=BLK):
        pr, b = self.prog, self.mm_at % SPL
        self.load(parts)
        if nxt:
            self.split(nxt)
        self.flush()
        pr.PE.wait((self.s_lo, self.s_mm.count + (RAW - SPL + 1)), *after)
        self.s_mm.inc(emit(self.hi[b], self.lo[b]))
        self.mm_at = (b + 1) % SPL
        return self.s_mm.mark()

    def flush(self):
        put_off, self.put_off = self.put_off, []
        for issue in put_off:
            issue()

    def unit_parts(self, w, col, half, cols=None):
        rows = lambda a: w[:, half * 512 + a * 256:half * 512 + a * 256 + 256, :]
        if cols is None:
            return [((lambda r, a=a: r[:, a * 512:a * 512 + 512].rearrange("p (c n) -> p c n", c=2)),
                     rows(a)[:, :, bass.ds(col, 256)].rearrange("o (c p) n -> p (o c) n", p=P)) for a in range(2)]
        whole = w[:, half * 512:half * 512 + 512, :]
        return [((lambda r, a=a: r[:, :].rearrange("p (c n) -> p c n", c=4)[:, :, a * P:a * P + P]),
                 whole[:, :, cols[a]:cols[a] + P].rearrange("o (c p) n -> p (o c) n", p=P)) for a in range(2)]

    def unit(self, w, col, x, after=(), cols=None, last=BLK, extra=None):
        pr, nc = self.prog, self.prog.nc
        bank = self.k.bank(self.out_at)
        free = (self.s_ev, self.ev_due() + 1)
        for half in range(2):
            def emit(hi, lo, half=half):
                for t in range(2):
                    for c in range(4):
                        kc = 4 * half + c
                        wh = hi[:, c * 256 + t * P:c * 256 + t * P + P]
                        wl = lo[:, c * 256 + t * P:c * 256 + t * P + P]
                        out = bank[:, t * S:t * S + S]
                        xh, xl = x[0][:, kc, :], x[1][:, kc, :]
                        for n, (a, b) in enumerate(((wh, xh), (wh, xl), (wl, xh))):
                            ins = nc.tensor.matmul(out, a, b, start=(kc == 0 and t == 0 and n == 0),
                                                   stop=(kc == 7 and n == 2), skip_group_check=True)
                return extra(half, hi, lo, x) if extra else ins
            mark = self.block(self.unit_parts(w, col, half, cols), emit, (*after, free),
                              nxt=last if half else BLK)
        self.out_at = (self.out_at + 1) % OUTB
        self.outs.later(1)
        return bank, mark

    def row_block(self, w, row, x, first, final, after=(), nxt=BLK):
        nc, k = self.prog.nc, self.k

        def emit(hi, lo):
            for t in range(8):
                out = k.bank(4 + t // 2)[:, (t % 2) * S:(t % 2) * S + S]
                wh, wl = hi[:, t * P:t * P + P], lo[:, t * P:t * P + P]
                for n, (a, b) in enumerate(((wh, x[0]), (wh, x[1]), (wl, x[0]))):
                    ins = nc.tensor.matmul(out, a, b, start=(first and t % 2 == 0 and n == 0),
                                           stop=(final and n == 2), skip_group_check=True)
            return ins
        src = w[:, bass.ds(row, P), :].rearrange("o p n -> p (o n)")
        parts = [((lambda r, a=a: r[:, a * 512:a * 512 + 512]), src[:, a * 512:a * 512 + 512]) for a in range(2)]
        return self.block(parts, emit, after, nxt)

    def skip_banks(self, after):
        pr = self.prog
        pr.POOL.wait(after)
        pr.POOL.settle()
        self.s_ev.inc(pr.nc.gpsimd.memset(self.k.tick[:, 3:4], 0.0), OUTB)
        self.outs.later(OUTB - 1)
        self.out_at = (self.out_at + OUTB - 1) % OUTB

    def skip_banks_to_start(self):
        n = -self.out_at % OUTB
        if n:
            self.prog.POOL.settle()
            self.s_ev.inc(self.prog.nc.gpsimd.memset(self.k.tick[:, 3:4], 0.0), n)
            self.outs.later(n)
            self.out_at = 0

    def skip_blocks(self):
        pr, n = self.prog, -self.load_at % RAW
        if n:
            pr.POOL.settle()
            for i, s in enumerate((self.s_hi, self.s_lo, self.s_mm)):
                s.inc(pr.nc.gpsimd.memset(self.k.tick[:, i:i + 1], 0.0), n)
            self.loads.later(n)
            self.load_at = self.split_at = 0
            self.mm_at = (self.mm_at + n) % SPL

    def ev_due(self):
        return self.outs.count


class Kernel:
    def __init__(self, nc, ctx, passes):
        self.nc, self.ctx = nc, ctx
        self.prog = Program(nc, ctx, passes)
        self.PE, self.ACT, self.DVE, self.POOL, self.SP = (
            self.prog.PE, self.prog.ACT, self.prog.DVE, self.prog.POOL, self.prog.SP)
        self.psum = ctx.enter_context(nc.psum_tensor("psum", [P, 8, 512], F32))
        self.h = self.sb("h", [P, ND, S])
        self.xh = self.sb("x_hi", [P, 32, S], F32R)
        self.xl = self.sb("x_lo", [P, 32, S], F32R)
        self.tmp = self.sb("tmp", [P, ND, S])
        self.rs = self.sb("rs", [P, 2, S])
        self.ones = self.sb("ones", [P, P])
        self.eps = self.sb("eps", [P, 2])
        self.act_buf = self.sb("act", [P, 2 * S])
        self.tick = self.sb("tick", [P, 4])
        self.con0 = self.sb("con0", [P, NCON0])
        self.s_par = Sem(self.prog, "params_landed")
        self.st = Stream(self)
        self.s_hid = Sem(self.prog, "hidden_split")
        self.s_conv = Sem(self.prog, "conv_done")
        for sem in [e.own for e in self.prog.engines] + [self.s_hid, self.s_conv]:
            nc.gpsimd.sem_inc(sem.sem, 1)
            sem.later(1)
        self.prog.joined = [e.own for e in (self.PE, self.ACT, self.DVE, self.POOL)] + [
            self.s_hid, self.s_conv, self.st.s_hi, self.st.s_lo, self.st.s_mm, self.st.s_ev]

    def sb(self, name, shape, dt=F32, ctx=None):
        return (ctx or self.ctx).enter_context(self.nc.sbuf_tensor(name, shape, dt))

    def bank(self, i):
        return self.psum[:, i, :]

    def banks(self, i, n):
        return self.psum[:, i:i + n, :].rearrange("p b n -> p (b n)")

    def ident(self, n=P):
        return self.con0[0:n, 0:n]

    def inv_rms(self, src, chunks, width, bank, out, after=()):
        nc = self.nc
        self.ACT.wait(*after)
        self.PE.wait(*after)
        for c in range(0, chunks, 2):
            n = min(2, chunks - c)
            sq = self.ACT.done(nc.scalar.activation(self.tmp[:, c:c + n, :], src[:, c:c + n, :], FN.Square))
            self.PE.wait(sq)
            for j in range(c, c + n):
                ins = nc.tensor.matmul(bank[:, 0:S], self.ones[:, :], self.tmp[:, j, :],
                                       start=(j == 0), stop=(j == chunks - 1))
        summed = self.PE.done(ins)
        return self.inv_sqrt(bank[:, 0:S], out, width, summed), summed

    def inv_sqrt(self, src, out, width, after, scale=None):
        nc = self.nc
        self.ACT.wait(after)
        m = self.ACT.done(nc.scalar.activation(out, src, FN.Ln, scale=1.0 / width, bias=self.eps[:, 0:1]))
        self.ACT.wait(m)
        if scale is None:
            return self.ACT.done(nc.scalar.activation(out, out, FN.Exp, scale=-0.5))
        return self.ACT.done(nc.scalar.activation(out, out, FN.Exp, scale=-0.5, bias=scale))

    def norm_split(self, src, gain, chunks, width, dst, after=()):
        nc = self.nc
        rs, summed = self.inv_rms(src, chunks, width, self.bank(7), self.rs[:, 0, :], after)
        self.DVE.wait(rs, summed)
        for a in range(0, chunks, 2):
            n = min(2, chunks - a)
            for c in range(a, a + n):
                m = self.DVE.done(nc.vector.scalar_tensor_tensor(self.tmp[:, c, :], src[:, c, :], gain(c),
                                                                 self.rs[:, 0, :], ALU.mult, ALU.mult))
            self.ACT.wait(m)
            hi = self.ACT.done(nc.scalar.copy(self.xh[:, dst + a:dst + a + n, :], self.tmp[:, a:a + n, :]))
            if a >= 2 or chunks <= 2:
                self.lo_part(dst, a - 2 if chunks > 2 else a, 2 if chunks > 2 else n, before if chunks > 2 else hi)
            before = hi
        return self.lo_part(dst, chunks - 2, 2, before) if chunks > 2 else self.DVE.own.mark()

    def lo_part(self, dst, a, n, hi):
        self.DVE.wait(hi)
        return self.DVE.done(self.nc.vector.tensor_tensor(
            self.xl[:, dst + a:dst + a + n, :], self.tmp[:, a:a + n, :],
            self.xh[:, dst + a:dst + a + n, :].bitcast(F32), ALU.subtract))

    def split_x(self, src, dst, chunks, after):
        nc = self.nc
        self.ACT.wait(after)
        hi = self.ACT.done(nc.scalar.copy(self.xh[:, dst:dst + chunks, :], src))
        self.DVE.wait(hi, after)
        return self.DVE.done(nc.vector.tensor_tensor(self.xl[:, dst:dst + chunks, :], src,
                                                     self.xh[:, dst:dst + chunks, :].bitcast(F32), ALU.subtract))

    def x(self, a, n=None):
        return (self.xh[:, a:a + n, :], self.xl[:, a:a + n, :]) if n else (self.xh[:, a, :], self.xl[:, a, :])

    def down(self, w, l, after, last=BLK):
        row = lambda kc: (self.xh[:, bass.ds(8 + kc, 1), :].rearrange("p o s -> p (o s)"),
                          self.xl[:, bass.ds(8 + kc, 1), :].rearrange("p o s -> p (o s)"))
        wl = w[bass.ds(l, 1)]
        for kc in range(2):
            self.st.row_block(wl, kc * P, row(kc), kc == 0, False, after)
        with self.prog.loop((NF - 6) // 4) as i:
            for j in range(4):
                self.st.row_block(wl, i * (4 * P) + (2 + j) * P, row(i * 4 + (2 + j)), False, False)
        for kc in range(NF - 4, NF):
            m = self.st.row_block(wl, kc * P, row(kc), False, kc == NF - 1,
                                  nxt=last if kc == NF - 1 else BLK)
        return m

    def ffn(self, w_in, w_out, l, gain, conv=None, last=BLK):
        nc, st = self.nc, self.st
        self.prog.join()
        ready = self.norm_split(self.h[:, :, :], gain, ND, D, 0)
        act = self.act_buf
        hid = self.hid_buf
        wl = w_in[bass.ds(l, 1)]
        x = self.x(0, ND)

        def pair(i):
            g, gm = st.unit(wl, i * 256, x, after=(ready,))
            u, um = st.unit(wl, i * 256 + FF, x)
            def use():
                if conv is None:
                    self.ACT.wait(gm, self.hid_free())
                    a = self.ACT.done(nc.scalar.activation(act[:, :], g, FN.Silu))
                    self.DVE.wait(a, um, self.hid_free())
                    f = st.s_ev.inc(nc.vector.tensor_tensor(hid[:, :], act[:, :], u, ALU.mult), 2)
                else:
                    f = conv(i, g, gm, u, um)
                c = bass.ds(i * 2 + 8, 2)
                out_h = self.xh[:, c, :].rearrange("p c s -> p (c s)")
                out_l = self.xl[:, c, :].rearrange("p c s -> p (c s)")
                self.ACT.wait(f)
                hi = self.ACT.done(nc.scalar.copy(out_h, hid[:, :]))
                self.DVE.wait(hi, f)
                self.s_hid.inc(nc.vector.tensor_tensor(out_l, hid[:, :], out_h.bitcast(F32), ALU.subtract))
            st.put_off.append(use)

        with self.prog.loop(NF // 4) as i:
            pair(i * 2)
            pair(i * 2 + 1)
            st.flush()
        pair(NF // 2 - 1)
        st.flush()
        return self.down(w_out, l, (self.s_hid.mark(),), last)

    def hid_free(self):
        return self.s_hid.mark()

    def add_sum(self, scale, after):
        nc = self.nc
        self.DVE.wait(after)
        for b in range(4):
            hb = self.h[:, 2 * b:2 * b + 2, :].rearrange("p c s -> p (c s)")
            m = self.DVE.done(nc.vector.scalar_tensor_tensor(hb, self.bank(4 + b), scale, hb, ALU.mult, ALU.add))
        return m


def par1(core, name, i=0, n=1, rows=P):
    a, width = PAR1[name]
    assert i + n <= width
    return core.pv[0:rows, a + i:a + i + n]


def con1(core, name, i=0, n=P):
    a = CON1[name][0]
    return core.con1[:, a + i:a + i + n]


def wide(core, mask, n):
    return mask.unsqueeze(1).to_broadcast([P, n, P])

def conv_unit(core, bank, mark, c, taps, weight, bias, dst):
    nc = core.nc
    core.ACT.wait(mark, core.s_conv.mark())
    pad = core.pad_buf[:, :, 3:3 + S]
    m = core.st.s_ev.inc(nc.scalar.copy(pad, bank.rearrange("p (c s) -> p c s", c=2)))
    core.DVE.wait(m)
    acc = core.act_buf[:, :].rearrange("p (c s) -> p c s", c=2)
    core.DVE.wait(core.ACT.own.mark())
    for j in range(2):
        x = lambda k: core.pad_buf[:, j, 3 - (taps - 1) + k:3 - (taps - 1) + k + S]
        if bias is None:
            t = core.DVE.done(nc.vector.tensor_scalar(acc[:, j, :], x(0), weight(c, j, 0), None, ALU.mult))
        else:
            t = core.DVE.done(nc.vector.tensor_scalar(acc[:, j, :], x(0), weight(c, j, 0), bias(c, j),
                                                      ALU.mult, ALU.add))
        for k in range(1, taps):
            core.DVE.wait(t)
            ins = nc.vector.scalar_tensor_tensor(acc[:, j, :], x(k), weight(c, j, k), acc[:, j, :],
                                                 ALU.mult, ALU.add)
            t = core.DVE.done(ins) if (j, k) != (1, taps - 1) else core.s_conv.inc(ins)
    core.ACT.wait(t, core.DVE.own.mark())
    return core.ACT.done(nc.scalar.activation(dst[:, bass.ds(c, 2), :], acc, FN.Silu))


def project(core, w, col, units, x, use):
    assert units % 4 == 0
    with core.prog.loop(units // 4) as i:
        for j in range(4):
            bank, mark = core.st.unit(w, i * 1024 + (col + j * 256), x)
            core.st.put_off.append(lambda u=i * 4 + j, bank=bank, mark=mark: use(u, bank, mark))
        core.st.flush()


def act_unit(core, func, dst):
    def use(u, bank, mark):
        core.ACT.wait(mark)
        core.st.s_ev.inc(core.nc.scalar.activation(
            dst[:, bass.ds(u * 2, 2), :].rearrange("p c s -> p (c s)"), bank, func))
    return use


def softplus(core, x, scratch, rows, after):
    nc = core.nc
    core.ACT.wait(after)
    m = core.ACT.done(nc.scalar.activation(scratch, x, FN.Abs))
    core.ACT.wait(m)
    m = core.ACT.done(nc.scalar.activation(scratch, scratch, FN.Exp, scale=-1.0))
    core.ACT.wait(m)
    m = core.ACT.done(nc.scalar.activation(scratch, scratch, FN.Ln, bias=1.0))
    core.DVE.wait(m, after)
    return core.DVE.done(nc.vector.scalar_tensor_tensor(x, x, 0.0, scratch, ALU.max, ALU.add))


def spread_row(core, out, src, row, rows, after):
    core.PE.wait(*after)
    return core.nc.tensor.matmul(out, core.ident(rows)[:, row:row + 1].to_broadcast([rows, P]), src,
                                 start=True, stop=True, skip_group_check=True)


def small_params(core, bank, mark):
    nc, PE, ACT, DVE = core.nc, core.PE, core.ACT, core.DVE
    DVE.wait(mark)
    hs, hd = core.hs, core.hd
    dt, la, ac, te, sc = (hs[:, i, :] for i in range(5))
    beta, g, eg, bg, ed, scd = (hd[:, i, :] for i in range(6))
    m1 = DVE.done(nc.vector.tensor_scalar(dt, bank[0:SH, 0:S], par1(core, "ssm_dtb", rows=SH), None, ALU.add))
    m1 = softplus(core, dt, sc, SH, m1)
    na = ACT.done(nc.scalar.activation(core.nega[0:SH, 0:1], par1(core, "ssm_alog", rows=SH), FN.Exp))
    nd = ACT.done(nc.scalar.activation(core.nega[0:DH, 1:2], par1(core, "dn_alog", rows=DH), FN.Exp))
    DVE.wait(na, nd, m1)
    m = DVE.done(nc.vector.tensor_scalar(la, dt, core.nega[0:SH, 0:1], -1.0, ALU.mult, ALU.mult))
    DVE.wait(m)
    for t in range(2):
        c = slice(t * P, t * P + P)
        m = DVE.done(nc.vector.tensor_tensor_scan(ac[:, c], core.ones[0:SH, :], la[:, c], 0.0, ALU.mult, ALU.add))
    ACT.wait(m)
    for t in range(2):
        c = slice(t * P, t * P + P)
        m = ACT.done(nc.scalar.activation(te[:, c], ac[:, c], FN.Exp, scale=-1.0,
                                          bias=ac[:, t * P + P - 1:t * P + P]))
    ssm = m
    bank_b, bank_a = bank[0:DH, S:2 * S], core.bank(7)[0:DH, 0:S]
    ACT.wait(mark, m1)
    mb = ACT.done(nc.scalar.activation(beta, bank_b, FN.Sigmoid))
    DVE.wait(mark)
    m = DVE.done(nc.vector.tensor_scalar(g, bank_a, par1(core, "dn_dtb", rows=DH), None, ALU.add))
    m = softplus(core, g, scd, DH, m)
    DVE.wait(m)
    m = DVE.done(nc.vector.tensor_scalar(scd, g, core.nega[0:DH, 1:2], -1.0, ALU.mult, ALU.mult))
    DVE.wait(m)
    for c in range(S // DC):
        s = slice(c * DC, c * DC + DC)
        m = DVE.done(nc.vector.tensor_tensor_scan(g[:, s], core.ones[0:DH, 0:DC], scd[:, s], 0.0,
                                                  ALU.mult, ALU.add))
    ACT.wait(m)
    for c in range(S // DC):
        s = slice(c * DC, c * DC + DC)
        ACT.done(nc.scalar.activation(ed[:, s], g[:, s], FN.Exp, scale=-1.0,
                                      bias=g[:, c * DC + DC - 1:c * DC + DC]))
    me = ACT.done(nc.scalar.activation(eg, g, FN.Exp))
    DVE.wait(me, mb)
    m = DVE.done(nc.vector.tensor_tensor(bg, beta, eg, ALU.mult))
    PE.wait(m, ssm, me)
    PE.settle()
    out = core.bank(6)
    for n, a in enumerate((dt, ac, te)):
        for t in range(2):
            nc.tensor.transpose(out[:, (2 * n + t) * SH:(2 * n + t + 1) * SH], a[:, t * P:t * P + P],
                                core.ident(SH))
    for n, a in enumerate((g, beta, bg, ed)):
        for t in range(2):
            at = 6 * SH + (2 * n + t) * DH
            ins = nc.tensor.transpose(out[:, at:at + DH], a[:, t * P:t * P + P], core.ident(DH))
    m = PE.done(ins)
    DVE.wait(m)
    return DVE.done(nc.vector.tensor_copy(core.cols[:, :], out[:, 0:6 * SH + 8 * DH]))


def scol(core, what, t, h, n=1):
    at = (2 * ("dt", "ac", "te").index(what) + t) * SH + h
    return core.cols[:, at:at + n]


def dcol(core, what, t, h, n=1):
    at = 6 * SH + (2 * ("g", "beta", "bg", "ed").index(what) + t) * DH + h
    return core.cols[:, at:at + n]

def delta(core, cols_ready):
    nc, PE, ACT, DVE, POOL = core.nc, core.PE, core.ACT, core.DVE, core.POOL
    qkv = core.qkv
    for c in range(0, 2 * DH, 4):
        pair = core.banks(4, 2)
        ACT.wait(DVE.own.mark(), PE.own.mark())
        sq = ACT.done(nc.scalar.activation(core.tmp[:, 0:4, :], qkv[:, c:c + 4, :], FN.Square))
        PE.wait(sq, DVE.own.mark())
        for j in range(4):
            ins = nc.tensor.matmul(pair[:, j * S:j * S + S], core.ones[:, :], core.tmp[:, j, :],
                                   start=True, stop=True, skip_group_check=True)
        mm = PE.done(ins)
        inv = core.tmp[:, 4:8, :].rearrange("p c s -> p (c s)")
        m = core.inv_sqrt(pair, inv, 1.0, mm, core.eps[:, 1:2] if c < DH else None)
        DVE.wait(m)
        m = DVE.done(nc.vector.tensor_tensor(qkv[:, c:c + 4, :], qkv[:, c:c + 4, :], core.tmp[:, 4:8, :], ALU.mult))
    normed = m
    for h0 in range(0, DH, 4):
        o_ready = delta_heads(core, h0, normed, cols_ready)
    for c in range(0, DH, 4):
        pair = core.banks(4, 2)
        ACT.wait(o_ready, DVE.own.mark(), PE.own.mark())
        sq = ACT.done(nc.scalar.activation(core.tmp[:, 0:4, :], core.o[:, c:c + 4, :], FN.Square))
        PE.wait(sq, DVE.own.mark())
        for j in range(4):
            ins = nc.tensor.matmul(pair[:, j * S:j * S + S], core.ones[:, :], core.tmp[:, j, :],
                                   start=True, stop=True, skip_group_check=True)
        mm = PE.done(ins)
        inv = core.tmp[:, 4:8, :].rearrange("p c s -> p (c s)")
        m = core.inv_sqrt(pair, inv, DK, mm)
        DVE.wait(m)
        m = DVE.done(nc.vector.scalar_tensor_tensor(inv, core.o[:, c:c + 4, :].rearrange("p c s -> p (c s)"),
                                                    par1(core, "dn_norm"), inv, ALU.mult, ALU.mult))
        DVE.wait(m)
        m = DVE.done(nc.vector.tensor_tensor(inv, inv, core.zd[:, c:c + 4, :].rearrange("p c s -> p (c s)"),
                                             ALU.mult))
        core.split_x(core.tmp[:, 4:8, :], 24 + c, 4, m)


def delta_heads(core, h0, normed, cols_ready):
    nc, PE, ACT, DVE, POOL, d = core.nc, core.PE, core.ACT, core.DVE, core.POOL, core.dn
    prior = (PE.own.mark(), ACT.own.mark(), DVE.own.mark())
    q, k, v = (lambda h, n=n: core.qkv[:, n * DH + h0 + h, :] for n in range(3))
    PE.wait(normed, *prior)
    kt_p, vt_p = core.banks(0, 2), core.banks(2, 2)
    for h in range(4):
        for t in range(2):
            o = slice((2 * h + t) * P, (2 * h + t + 1) * P)
            nc.tensor.transpose(kt_p[:, o], k(h)[:, t * P:t * P + P], core.ident())
            ins = nc.tensor.transpose(vt_p[:, o], v(h)[:, t * P:t * P + P], core.ident())
    turned = PE.done(ins)
    g_p = core.banks(4, 2)
    for h in range(4):
        ins = spread_row(core, g_p[:, h * S:h * S + S], core.hd[:, 1, :], h0 + h, DH, (cols_ready,))
    spread = PE.done(ins)
    ACT.wait(spread, *prior)
    eg = ACT.done(nc.scalar.activation(d["eg"][:, :], g_p, FN.Exp))
    DVE.wait(eg, cols_ready, *prior)
    for h in range(4):
        for t in range(2):
            o = slice((2 * h + t) * P, (2 * h + t + 1) * P)
            m = DVE.done(nc.vector.tensor_scalar(d["dec"][:, o], g_p[:, o], dcol(core, "g", t, h0 + h), 0.0,
                                                 ALU.subtract, ALU.min))
    ACT.wait(m)
    dec = ACT.done(nc.scalar.activation(d["dec"][:, :], d["dec"][:, :], FN.Exp))
    DVE.wait(eg)
    qd = DVE.done(nc.vector.tensor_tensor(d["qd"][:, :], core.qkv[:, h0:h0 + 4, :].rearrange("p c s -> p (c s)"),
                                          d["eg"][:, :], ALU.mult))
    DVE.wait(turned)
    for h in range(4):
        for t in range(2):
            o = slice((2 * h + t) * P, (2 * h + t + 1) * P)
            DVE.done(nc.vector.tensor_scalar(d["kbg"][:, o], kt_p[:, o], dcol(core, "bg", t, h0 + h), None, ALU.mult))
            DVE.done(nc.vector.tensor_scalar(d["kdec"][:, o], kt_p[:, o], dcol(core, "ed", t, h0 + h), None, ALU.mult))
            rows = DVE.done(nc.vector.tensor_scalar(d["vb"][:, o], vt_p[:, o], dcol(core, "beta", t, h0 + h), None,
                                                    ALU.mult))
    kk_p, qk_p = core.banks(0, 2), core.banks(2, 2)
    PE.wait(rows)
    for h in range(4):
        for t in range(2):
            o, c = slice((2 * h + t) * P, (2 * h + t + 1) * P), slice(t * P, t * P + P)
            nc.tensor.matmul(kk_p[:, o], k(h)[:, c], k(h)[:, c], start=True, stop=True, skip_group_check=True)
            ins = nc.tensor.matmul(qk_p[:, o], k(h)[:, c], q(h)[:, c], start=True, stop=True,
                                   skip_group_check=True)
    mm = PE.done(ins)
    three = lambda a: a.rearrange("p (n j) -> p n j", n=8)
    DVE.wait(mm, dec)
    m = DVE.done(nc.vector.tensor_tensor(d["kk"][:, :], kk_p, d["dec"][:, :], ALU.mult))
    DVE.done(nc.vector.tensor_tensor(d["aqk"][:, :], qk_p, d["dec"][:, :], ALU.mult))
    DVE.wait(m)
    DVE.done(nc.vector.tensor_tensor(three(d["kk"][:, :]), three(d["kk"][:, :]), wide(core, con1(core, "strict"), 8), ALU.mult))
    DVE.wait(DVE.own.mark())
    lower = DVE.done(nc.vector.tensor_tensor(three(d["aqk"][:, :]), three(d["aqk"][:, :]), wide(core, con1(core, "incl"), 8), ALU.mult))
    DVE.wait(lower)
    DVE.done(nc.vector.tensor_copy(three(d["T"][:, :]), wide(core, core.ident(), 8)))
    m = DVE.done(nc.vector.tensor_copy(three(d["U"][:, :]), wide(core, core.ident(), 8)))
    p_p, t_p, u_p = core.banks(0, 2), core.banks(2, 2), core.banks(4, 2)
    mu = m
    for level in range(LEVELS):
        POOL.wait(lower, PE.own.mark())
        lm = POOL.done(nc.gpsimd.tensor_tensor(three(d["km"][:, :]), three(d["kk"][:, :]),
                                               wide(core, con1(core, "level", level * P), 8), ALU.mult))
        PE.wait(lm, mu, DVE.own.mark())
        for i in range(8):
            o = slice(i * P, i * P + P)
            ins = nc.tensor.matmul(p_p[:, o], d["km"][:, o], d["T"][:, o], start=True, stop=True, skip_group_check=True)
        mp = PE.done(ins)
        DVE.wait(mp)
        for h in range(4):
            for t in range(2):
                o = slice((2 * h + t) * P, (2 * h + t + 1) * P)
                m = DVE.done(nc.vector.tensor_scalar(d["P"][:, o], p_p[:, o], dcol(core, "beta", t, h0 + h), None,
                                                     ALU.mult))
        PE.wait(m)
        for i in range(8):
            o = slice(i * P, i * P + P)
            if level < LEVELS - 1:
                nc.tensor.matmul(t_p[:, o], d["U"][:, o], d["P"][:, o], start=True, stop=True, skip_group_check=True)
            ins = nc.tensor.matmul(u_p[:, o], d["P"][:, o], d["U"][:, o], start=True, stop=True, skip_group_check=True)
        mm = PE.done(ins)
        DVE.wait(mm)
        if level < LEVELS - 1:
            DVE.done(nc.vector.tensor_tensor(d["T"][:, :], d["T"][:, :], t_p, ALU.subtract))
        mu = DVE.done(nc.vector.tensor_tensor(d["U"][:, :], d["U"][:, :], u_p, ALU.subtract))
    un_p, wt_p = core.banks(0, 2), core.banks(2, 2)
    PE.wait(mu)
    for i in range(8):
        o = slice(i * P, i * P + P)
        nc.tensor.matmul(un_p[:, o], d["U"][:, o], d["vb"][:, o], start=True, stop=True, skip_group_check=True)
        ins = nc.tensor.matmul(wt_p[:, o], d["kbg"][:, o], d["U"][:, o], start=True, stop=True, skip_group_check=True)
    mm = PE.done(ins)
    DVE.wait(mm)
    un = DVE.done(nc.vector.tensor_copy(d["un"][:, :], un_p))
    ACT.wait(mm, un)
    wt = ACT.done(nc.scalar.copy(d["wt"][:, :], wt_p))
    state = DVE.done(nc.vector.memset(d["state"][:, :], 0.0))
    for c in range(S // DC):
        t, off = c // 2, (c % 2) * DC
        rows = slice(off, off + DC)
        ws_p, o_p, s_p = (core.bank(3 * (c % 2) + j) for j in range(3))
        hs = lambda h: slice((2 * h + t) * P, (2 * h + t + 1) * P)
        cs = lambda h: slice((2 * h + t) * P + off, (2 * h + t) * P + off + DC)
        PE.wait(state, wt, qd, un, ACT.own.mark())
        for h in range(4):
            nc.tensor.matmul(ws_p[rows, h * P:h * P + P], d["wt"][:, cs(h)], d["state"][:, h * P:h * P + P],
                             start=True, stop=True, skip_group_check=True)
        for h in range(4):
            ins = nc.tensor.matmul(o_p[:, h * DC:h * DC + DC], d["state"][:, h * P:h * P + P], d["qd"][:, cs(h)],
                                   start=(h == 0), stop=False, skip_group_check=True)
        mm = PE.done(ins)
        DVE.wait(mm)
        un_c = d["un"][rows, :].rearrange("p (h t v) -> p h t v", h=4, t=2)[:, :, t, :]
        vn = DVE.done(nc.vector.tensor_tensor(un_c, un_c, ws_p[rows, :].rearrange("p (h v) -> p h v", h=4),
                                              ALU.subtract))
        PE.wait(vn)
        for h in range(4):
            nc.tensor.matmul(s_p[:, h * P:h * P + P], d["kdec"][rows, hs(h)], d["un"][rows, hs(h)],
                             start=True, stop=True, skip_group_check=True)
        for h in range(4):
            ins = nc.tensor.matmul(o_p[:, h * DC:h * DC + DC], d["un"][rows, hs(h)], d["aqk"][rows, cs(h)],
                                   start=False, stop=True, skip_group_check=True)
        mm = PE.done(ins)
        DVE.wait(mm)
        for h in range(4):
            last = h * S + c * DC + DC - 1
            state = DVE.done(nc.vector.scalar_tensor_tensor(
                d["state"][:, h * P:h * P + P], d["state"][:, h * P:h * P + P], d["eg"][:, last:last + 1],
                s_p[:, h * P:h * P + P], ALU.mult, ALU.add))
        ACT.wait(mm)
        o_ready = ACT.done(nc.scalar.copy(core.o[:, h0:h0 + 4, c * DC:c * DC + DC],
                                          o_p[:, 0:4 * DC].rearrange("p (h s) -> p h s", h=4)))
    return o_ready

def ssm_group(core, g, cols_ready):
    nc, PE, ACT, DVE, POOL, b = core.nc, core.PE, core.ACT, core.DVE, core.POOL, core.sm
    prior = (PE.own.mark(), ACT.own.mark(), DVE.own.mark(), POOL.own.mark())
    nx = SI // P
    B, C = core.xbc[:, nx + g, :], core.xbc[:, nx + SG + g, :]
    ac_p = core.banks(0, 4)
    PE.wait(*prior, cols_ready)
    for h in range(HG):
        ins = spread_row(core, ac_p[:, h * S:h * S + S], core.hs[:, 2, :], g * HG + h, SH, ())
    spread = PE.done(ins)
    cb_p = core.bank(4)
    for t in range(2):
        c = slice(t * P, t * P + P)
        nc.tensor.matmul(cb_p[:, c], B[:, c], C[:, c], start=True, stop=True, skip_group_check=True)
    ins = nc.tensor.transpose(cb_p[:, 2 * P:3 * P], B[:, 0:P], core.ident())
    cbm = PE.done(ins)
    xt_p = core.banks(5, 2)
    for t in range(2):
        for c in range(4):
            ins = nc.tensor.transpose(xt_p[:, t * 512 + c * P:t * 512 + c * P + P],
                                      core.xbc[:, 4 * g + c, t * P:t * P + P], core.ident())
    turned = PE.done(ins)
    DVE.wait(spread, *prior)
    for h in range(HG):
        for t in range(2):
            o = slice(h * S + t * P, h * S + t * P + P)
            m = DVE.done(nc.vector.tensor_scalar(b["w"][:, o], ac_p[:, o], scol(core, "ac", t, g * HG + h), 0.0,
                                                 ALU.subtract, ALU.min))
    ACT.wait(m, *prior)
    dec = ACT.done(nc.scalar.activation(b["w"][:, :], b["w"][:, :], FN.Exp))
    ACT.wait(m)
    ea = ACT.done(nc.scalar.activation(b["cs"][:, :].rearrange("p (h l) -> p h l", h=HG),
                                       ac_p.rearrange("p (h s) -> p h s", h=HG)[:, :, P:S], FN.Exp))
    DVE.wait(cbm)
    cbs = DVE.done(nc.vector.tensor_tensor(b["cb"][:, :].rearrange("p (t l) -> p t l", t=2),
                                           cb_p[:, 0:2 * P].rearrange("p (t l) -> p t l", t=2),
                                           wide(core, con1(core, "causal"), 2), ALU.mult))
    bt = DVE.done(nc.vector.tensor_copy(b["bt"][:, :], cb_p[:, 2 * P:3 * P]))
    DVE.wait(turned)
    heads = lambda a: a.rearrange("p (h d) -> p h d", h=HG)
    over = lambda a: a.unsqueeze(2).to_broadcast([P, HG, SP])
    for t in range(2):
        c = slice(t * 512, t * 512 + 512)
        xd = DVE.done(nc.vector.tensor_tensor(heads(b["xd"][:, c]), heads(xt_p[:, c]),
                                              over(scol(core, "dt", t, g * HG, HG)), ALU.mult))
    DVE.wait(xd)
    xe = DVE.done(nc.vector.tensor_tensor(heads(b["xe"][:, :]), heads(b["xd"][:, 0:512]),
                                          over(scol(core, "te", 0, g * HG, HG)), ALU.mult))
    PE.wait(xe, bt)
    mm = PE.done(nc.tensor.matmul(core.bank(7), b["bt"][:, :], b["xe"][:, :], start=True, stop=True))
    ACT.wait(mm)
    state = ACT.done(nc.scalar.copy(b["state"][:, :], core.bank(7)))
    DVE.wait(ea, dec, cbs)
    cs = DVE.done(nc.vector.tensor_tensor(b["cs"][:, :].rearrange("p (h l) -> p h l", h=HG),
                                          b["cs"][:, :].rearrange("p (h l) -> p h l", h=HG),
                                          wide(core, C[:, P:S], HG), ALU.mult))
    w = DVE.done(nc.vector.tensor_tensor(b["w"][:, :].rearrange("p (h s) -> p h s", h=HG),
                                         b["w"][:, :].rearrange("p (h s) -> p h s", h=HG),
                                         b["cb"][:, :].unsqueeze(1).to_broadcast([P, HG, S]), ALU.mult))
    y_p = core.banks(5, 2)
    PE.wait(w, cs, state)
    for h in range(HG):
        rows = slice((h % 2) * SP, (h % 2) * SP + SP)
        for t in range(2):
            o = y_p[rows, (h // 2) * S + t * P:(h // 2) * S + t * P + P]
            ins = nc.tensor.matmul(o, b["xd"][:, t * 512 + h * SP:t * 512 + h * SP + SP],
                                   b["w"][:, h * S + t * P:h * S + t * P + P],
                                   start=True, stop=(t == 0), skip_group_check=True)
            if t == 1:
                ins = nc.tensor.matmul(o, b["state"][:, h * SP:h * SP + SP], b["cs"][:, h * P:h * P + P],
                                       start=False, stop=True, skip_group_check=True)
    mm = PE.done(ins)
    DVE.wait(mm)
    y = b["y"]
    for c in range(4):
        m = DVE.done(nc.vector.scalar_tensor_tensor(y[:, c, :], core.xbc[:, 4 * g + c, :],
                                                    par1(core, "ssm_d", 4 * g + c), y_p[:, c * S:c * S + S],
                                                    ALU.mult, ALU.add))
    DVE.wait(m)
    m = DVE.done(nc.vector.tensor_tensor(y[:, :, :], y[:, :, :], core.z[:, 4 * g:4 * g + 4, :], ALU.mult))
    rs, summed = core.inv_rms(y[:, :, :], 4, 512, core.bank(4), core.rs[:, 1, :], (m,))
    DVE.wait(rs, summed)
    for c in range(4):
        m = DVE.done(nc.vector.scalar_tensor_tensor(core.tmp[:, 4 + c, :], y[:, c, :],
                                                    par1(core, "ssm_norm", 4 * g + c), core.rs[:, 1, :],
                                                    ALU.mult, ALU.mult))
    core.split_x(core.tmp[:, 4:8, :], 8 + 4 * g, 4, m)


def branch(core, w, l, chunks, at, after, last=BLK):
    wl = w[bass.ds(l, 1)]
    one = lambda kc: (core.xh[:, bass.ds(at + kc, 1), :].rearrange("p o s -> p (o s)"),
                      core.xl[:, bass.ds(at + kc, 1), :].rearrange("p o s -> p (o s)"))
    st = core.st
    for kc in range(4):
        m = st.row_block(wl, kc * P, one(kc), kc == 0, False, after if kc == 0 else ())
    if chunks > 8:
        with core.prog.loop(chunks // 4 - 2) as i:
            for j in range(4):
                st.row_block(wl, i * (4 * P) + (4 + j) * P, one(i * 4 + (4 + j)), False, False)
    for kc in range(chunks - 4, chunks):
        m = st.row_block(wl, kc * P, one(kc), False, kc == chunks - 1,
                         nxt=last if kc == chunks - 1 else BLK)
    return m


def mixer1(core, io, l):
    nc, PE, ACT, DVE, POOL, st = core.nc, core.PE, core.ACT, core.DVE, core.POOL, core.st
    core.prog.join()
    w = io["w_in"][bass.ds(l, 1)]
    x = core.x(0, ND)
    u = core.norm_split(core.h[:, :, :], lambda c: par1(core, "mix_norm", c), ND, D, 0)
    PE.wait(u)
    POOL.settle()
    for j in range(2):
        m = POOL.done(nc.gpsimd.memset(core.pad_buf[:, j, 0:3], 0.0))
    ACT.wait(m)
    DVE.wait(m)
    bank, mark = st.unit(w, None, x, cols=(COL_DT, COL_B), extra=lambda *a: small_extra(core, *a))
    cols_ready = small_params(core, bank, mark)
    st.skip_banks(cols_ready)
    cw = lambda name: (lambda c, j, k: core.pv[:, bass.ds(c * 4 + (PAR1[name][0] + 4 * j + k), 1)])
    dw, sw = cw("dn_cw"), cw("ssm_cw")
    project(core, w, COL_QKV, DCONV // 256, x,
                 lambda i, bank, mark: conv_unit(core, bank, mark, i * 2, 4, dw, None, core.qkv))
    project(core, w, COL_ZD, DH * DK // 256, x, act_unit(core, FN.Silu, core.zd))
    with ExitStack() as inner:
        core.dn = buffers(core, inner, "dn", dict(eg=1024, dec=1024, qd=1024, kbg=1024, kdec=1024, vb=1024,
                                                  kk=1024, aqk=1024, km=1024, state=512))
        half = lambda n: core.tmp[:, 4 * n:4 * n + 4, :].rearrange("p c s -> p (c s)")
        core.dn["T"], core.dn["U"], core.dn["P"] = half(0), half(1), core.dn["dec"]
        core.dn["un"], core.dn["wt"], core.o = core.dn["P"], core.dn["T"], core.qkv
        core.prog.join()
        delta(core, cols_ready)
        core.prog.join()
    with ExitStack() as inner:
        core.z = core.sb("z", [P, SI // P, S], ctx=inner)
        core.sm = buffers(core, inner, "ssm", dict(w=2048, cs=1024, cb=256, bt=P, xd=1024, xe=512, state=512))
        core.sm["y"] = core.sm["w"][:, 0:4 * S].rearrange("p (c s) -> p c s", c=4)
        core.xbc = core.qkv
        bias = lambda c, j: core.pv[:, bass.ds(c + (PAR1["ssm_cb"][0] + j), 1)]
        project(core, w, COL_XBC, SCONV // 256, x,
                     lambda i, bank, mark: conv_unit(core, bank, mark, i * 2, 4, sw, bias, core.xbc))
        project(core, w, COL_Z, SI // 256, x, act_unit(core, FN.Silu, core.z))
        core.prog.join()
        for g in range(SG):
            ssm_group(core, g, cols_ready)
        core.prog.join()
    with ExitStack() as inner:
        gates = core.sb("gates", [P, 2 * ND, S], ctx=inner)
        project(core, w, COL_GS, 2 * D // 256, x, act_unit(core, FN.Sigmoid, gates))
        flat = lambda a: a.rearrange("p c s -> p (c s)")
        core.prog.join()
        m = branch(core, io["ssm_w_branch"], l, SI // P, 8, ())
        DVE.wait(m)
        for b in range(4):
            m = DVE.done(nc.vector.tensor_tensor(flat(core.tmp[:, 2 * b:2 * b + 2, :]), core.bank(4 + b),
                                                 flat(gates[:, 2 * b:2 * b + 2, :]), ALU.mult))
        m = branch(core, io["dn_w_branch"], l, DH, 24, (m,))
        DVE.wait(m)
        for b in range(4):
            gb = flat(gates[:, ND + 2 * b:ND + 2 * b + 2, :])
            m = DVE.done(nc.vector.tensor_tensor(gb, core.bank(4 + b), gb, ALU.mult))
        DVE.wait(m)
        m = DVE.done(nc.vector.tensor_tensor(flat(core.tmp[:, :, :]), flat(core.tmp[:, :, :]),
                                             flat(gates[:, ND:2 * ND, :]), ALU.add))
        m = core.split_x(core.tmp[:, :, :], 0, ND, m)
        m = branch(core, io["w_out"], l, ND, 0, (m,))
        core.add_sum(1.0, m)
        core.prog.join()


def small_extra(core, half, hi, lo, x):
    for c in range(4):
        kc = 4 * half + c
        wh, wl = (a[:, c * 256 + P + DH:c * 256 + 2 * P] for a in (hi, lo))
        for n, (a, b) in enumerate(((wh, x[0][:, kc, :]), (wh, x[1][:, kc, :]), (wl, x[0][:, kc, :]))):
            ins = core.nc.tensor.matmul(core.bank(7)[0:P - DH, 0:S], a, b, start=(kc == 0 and n == 0),
                                        stop=(kc == 7 and n == 2), skip_group_check=True)
    return ins


def layer1(core, io, l):
    nc = core.nc
    core.st.split()
    core.ACT.wait(core.DVE.own.mark(), core.ACT.own.mark())
    core.s_par.inc(nc.scalar.dma_start(core.pv[:, :], io["par1"][bass.ds(l, 1)].rearrange("o p n -> p (o n)")), 16)
    for e in (core.ACT, core.DVE):
        e.wait(core.s_par.mark())
    with ExitStack() as inner:
        core.hid_buf = core.sb("hid1", [P, 512], ctx=inner)
        m = core.ffn(io["ffn1_w_in"], io["ffn1_w_out"], l, lambda c: par1(core, "ffn1_norm", c))
        core.add_sum(0.5, m)
        core.prog.join()
    with ExitStack() as inner:
        core.qkv = core.sb("qkv", [P, 3 * DH, S], ctx=inner)
        core.pad_buf = core.sb("pad", [P, 2, 3 + S], ctx=inner)
        core.zd = core.sb("zd", [P, DH, S], ctx=inner)
        core.hs = core.sb("heads_ssm", [SH, 5, S], ctx=inner)
        core.hd = core.sb("heads_dn", [DH, 6, S], ctx=inner)
        core.cols = core.sb("cols", [P, 6 * SH + 8 * DH], ctx=inner)
        mixer1(core, io, l)
    with ExitStack() as inner:
        core.hid_buf = core.sb("hid2", [P, 512], ctx=inner)
        m = core.ffn(io["ffn2_w_in"], io["ffn2_w_out"], l, lambda c: par1(core, "ffn2_norm", c), last=0)
        core.add_sum(0.5, m)
        core.prog.join()
    core.st.skip_banks_to_start()
    core.st.skip_blocks()
    core.prog.join()


def buffers(core, ctx, stage, sizes):
    return {name: core.sb(stage + "_" + name, [P, n], ctx=ctx) for name, n in sizes.items()}


def par2(core, name, i=0, n=1, rows=P):
    a, width = PAR2[name]
    assert i + n <= width
    return core.pv2[0:rows, a + i:a + i + n]


def con2(core, name, rows=slice(0, P)):
    a, n = CON2[name]
    return core.con2[rows, a:a + n]


def moba_bias(core, io):
    nc, PE, ACT, DVE, SP = core.nc, core.PE, core.ACT, core.DVE, core.SP
    with ExitStack() as inner:
        cont = core.sb("con_t5", [P, NCONT], ctx=inner)
        relb = core.sb("rel_bias", [32, AH], ctx=inner)
        line = core.sb("bias_line", [AH, S + P], ctx=inner)
        slid = core.sb("bias_slid", [P, AH, S], ctx=inner)
        core.s_par.inc(nc.sync.dma_start(cont[:, :], io["con_t5"]), 16)
        core.s_par.inc(nc.sync.dma_start(relb[:, :], io["rel_bias"]), 16)
        flip = cont[:, CONT["flip"][0]:CONT["flip"][0] + P]
        onehot = cont[0:32, CONT["bucket"][0]:CONT["bucket"][0] + S + P]
        for e in (PE, DVE):
            e.wait(core.s_par.mark())
        mm = PE.done(nc.tensor.matmul(core.bank(0)[0:AH, 0:S + P], relb[:, :], onehot, start=True, stop=True))
        DVE.wait(mm)
        m = DVE.done(nc.vector.tensor_copy(line[:, :], core.bank(0)[0:AH, 0:S + P]))
        DVE.wait(m)
        m = DVE.done(nc.vector.memset(line[:, S:S + P], NEG))
        SP.wait(m)
        scratch = io["scratch"]
        core.s_par.inc(nc.sync.dma_start(scratch, line[:, :]), 16)
        SP.wait(core.s_par.mark())
        src = bass.AP(scratch.tensor, scratch.offset, [[1, P], [S + P, AH], [1, S]])
        core.s_par.inc(nc.sync.dma_start(slid[:, :, :], src), 16)
        PE.wait(core.s_par.mark(), m)
        for h in range(AH):
            ins = nc.tensor.matmul(core.bank(h // 2)[:, (h % 2) * S:(h % 2) * S + S], flip, slid[:, h, :],
                                   start=True, stop=True, skip_group_check=True)
        mm = PE.done(ins)
        ACT.wait(mm)
        for h in range(AH):
            b = core.bank(h // 2)[:, (h % 2) * S:(h % 2) * S + S]
            ACT.done(nc.scalar.copy(core.t5[:, h, 0:S], b))
            ACT.done(nc.scalar.copy(core.t5[:, h, S:S + P], b[:, P:S]))
        core.prog.join()


def units(core, w, cols, x, use):
    for n, col in enumerate(cols):
        bank, mark = core.st.unit(w, col, x)
        use(n, bank, mark)


def copy_unit(core, dst):
    def use(n, bank, mark):
        core.ACT.wait(mark)
        core.st.s_ev.inc(core.nc.scalar.copy(dst[:, 2 * n:2 * n + 2, :].rearrange("p c s -> p (c s)"), bank))
    return use


def mixer2(core, io, l):
    nc, PE, ACT, DVE, POOL, st = core.nc, core.PE, core.ACT, core.DVE, core.POOL, core.st
    core.prog.join()
    w = io["w_in_2"][bass.ds(l, 1)]
    x = core.x(0, ND)
    flat = lambda a: a.rearrange("p c s -> p (c s)")
    with ExitStack() as inner:
        sb = lambda name, shape: core.sb(name, shape, ctx=inner)
        pa, pf = sb("proj_a", [P, 12, S]), sb("proj_f", [P, 9, S])
        va, vf, vm = sb("v_moba", [P, 2, 3 * P]), sb("v_fox", [P, 2, 3 * P]), sb("v_mla", [P, 2, S])
        qm, km, kr = sb("q_mla", [P, MH, S]), sb("k_mla", [P, MH, S]), sb("k_rope", [P, 2, S])
        fg, dec = sb("forget", [P, 2 * XH_]), sb("decay", [XH_, 4, S])
        u = core.norm_split(core.h[:, :, :], lambda c: par2(core, "mix_pre", c), ND, D, 0)
        PE.wait(u)
        units(core, w, [256 * n for n in range(6)], x, copy_unit(core, pa))
        units(core, w, [COL2_F + 256 * n for n in range(4)], x, copy_unit(core, pf))
        bank, mark = st.unit(w, None, x, cols=(COL2_KR - 64, COL2_F + 8 * P), last=8 * XH_)
        ACT.wait(mark)
        ACT.done(nc.scalar.copy(kr[64:96, 0, :], bank[64:96, 0:S]))
        st.s_ev.inc(nc.scalar.copy(pf[:, 8, :], bank[:, S:2 * S]))

        def forget(hi, lo):
            for t in range(2):
                for kc in range(ND):
                    a, b = (v[:, kc, t * P:t * P + P] for v in x)
                    wh, wl = (v[:, kc * XH_:(kc + 1) * XH_] for v in (hi, lo))
                    for n, (p, q) in enumerate(((a, wh), (b, wh), (a, wl))):
                        ins = nc.tensor.matmul(core.bank(7)[:, t * XH_:t * XH_ + XH_], p, q,
                                               start=(kc == 0 and n == 0), stop=(kc == 7 and n == 2),
                                               skip_group_check=True)
            return ins
        parts = [((lambda r, a=a: r[:, a * 4 * XH_:(a + 1) * 4 * XH_].rearrange("p (c n) -> p c n", c=4)),
                  w[:, a * 512:a * 512 + 512, COL2_FG:COL2_FG + XH_].rearrange("o (c p) n -> p (o c) n", p=P))
                 for a in range(2)]
        mm = st.block(parts, forget, nxt=MH * QKD)
        DVE.wait(mm)
        fgm = DVE.done(nc.vector.tensor_copy(fg[:, :], core.bank(7)[:, 0:2 * XH_]))
        cq = core.norm_split(pa[:, 9:11, :], lambda c: par2(core, "q_norm", c), 2, QR, 8,
                             (ACT.own.mark(), st.s_ev.mark(), fgm))
        ckv = core.norm_split(pa[:, 11:12, :], lambda c: par2(core, "kv_norm", c), 1, KVR, 10,
                              (cq, st.s_ev.mark()))
        q_p = core.banks(4, 2)
        for kc in range(2):
            def up_q(hi, lo, kc=kc):
                a, b = core.x(8 + kc)
                for h in range(MH):
                    wh, wl = (v[:, h * QKD:(h + 1) * QKD] for v in (hi, lo))
                    for n, (p, q) in enumerate(((wh, a), (wh, b), (wl, a))):
                        ins = nc.tensor.matmul(q_p[0:QKD, h * S:h * S + S], p, q,
                                               start=(kc == 0 and h % 2 == 0 and n == 0),
                                               stop=(kc == 1 and n == 2), skip_group_check=True)
                return ins
            half = MH * QKD // 2
            parts = [((lambda r, a=a: r[:, a * half:(a + 1) * half]),
                      io["w_uq_2"][bass.ds(l, 1), kc * P:kc * P + P, a * half:(a + 1) * half].rearrange(
                          "o p n -> p (o n)")) for a in range(2)]
            mq = st.block(parts, up_q, (cq,), nxt=MH * QKD if kc == 0 else MH * P)
        k_p, v_p = core.banks(2, 2), core.bank(6)

        def up_kv(hi, lo):
            a, b = core.x(10)
            for h in range(MH):
                wh, wl = (v[:, h * P:(h + 1) * P] for v in (hi, lo))
                for n, (p, q) in enumerate(((wh, a), (wh, b), (wl, a))):
                    nc.tensor.matmul(k_p[:, h * S:h * S + S], p, q, start=(n == 0), stop=(n == 2),
                                     skip_group_check=True)
            for t in range(2):
                c = slice(t * P, t * P + P)
                wh, wl = (v[:, 0:MH * P].rearrange("p (h n) -> p h n", h=MH)[:, :, HD:P] for v in (hi, lo))
                for n, (p, q) in enumerate(((a[:, c], wh), (b[:, c], wh), (a[:, c], wl))):
                    ins = nc.tensor.matmul(v_p[:, t * S:t * S + S], p, q, start=(n == 0), stop=(n == 2),
                                           skip_group_check=True)
            return ins
        parts = [((lambda r, a=a: r[:, a * S:(a + 1) * S]),
                  io["w_ukv_2"][bass.ds(l, 1), :, a * S:(a + 1) * S].rearrange("o p n -> p (o n)"))
                 for a in range(2)]
        mkv = st.block(parts, up_kv, (ckv, st.s_ev.mark()), nxt=BLK)
        ACT.wait(mkv)
        ACT.done(nc.scalar.copy(km[0:HD, :, :], k_p[0:HD, :].rearrange("p (h s) -> p h s", h=MH)))
        ACT.done(nc.scalar.copy(flat(vm[:, :, :]), v_p))
        raw_q = ACT.done(nc.scalar.copy(qm[0:QKD, :, :], q_p[0:QKD, :].rearrange("p (h s) -> p h s", h=MH)))
        rr = slice(64, 96)
        PE.wait(raw_q)
        for n in range(2):
            nc.tensor.matmul(core.bank(4 + n)[0:QKD, :], con2(core, "rot", slice(0, QKD))[:, 0:QKD],
                             flat(qm[0:QKD, 2 * n:2 * n + 2, :]), start=True, stop=True)
        mr = PE.done(nc.tensor.matmul(core.bank(7)[rr, 0:S], con2(core, "rot", rr)[:, rr], kr[rr, 0, :],
                                      start=True, stop=True))
        DVE.wait(mr, raw_q)
        four = lambda a, rows: a.unsqueeze(1).to_broadcast([rows, MH, S])
        rq = core.tmp[0:QKD, 0:MH, :]
        m1 = DVE.done(nc.vector.tensor_tensor(rq, q_p[0:QKD, :].rearrange("p (h s) -> p h s", h=MH),
                                              four(con2(core, "sin", slice(0, QKD)), QKD), ALU.mult))
        m2 = DVE.done(nc.vector.tensor_tensor(qm[0:QKD, :, :], qm[0:QKD, :, :],
                                              four(con2(core, "cos", slice(0, QKD)), QKD), ALU.mult))
        m3 = DVE.done(nc.vector.tensor_tensor(kr[rr, 1, :], core.bank(7)[rr, 0:S], con2(core, "sin", rr), ALU.mult))
        m4 = DVE.done(nc.vector.tensor_tensor(kr[rr, 0, :], kr[rr, 0, :], con2(core, "cos", rr), ALU.mult))
        DVE.wait(m4)
        DVE.done(nc.vector.tensor_tensor(qm[0:QKD, :, :], qm[0:QKD, :, :], rq, ALU.add))
        for h in range(MH):
            mla = DVE.done(nc.vector.tensor_tensor(km[rr, h, :], kr[rr, 0, :], kr[rr, 1, :], ALU.add))
        PE.wait(fgm, mla)
        for t in range(2):
            ins = nc.tensor.transpose(core.bank(7)[0:XH_, t * P:t * P + P], fg[:, t * XH_:(t + 1) * XH_],
                                      core.ident())
        m = PE.done(ins)
        f, sc, cum, neg = (dec[:, i, :] for i in range(4))
        DVE.wait(m)
        m = DVE.done(nc.vector.tensor_scalar(f, core.bank(7)[0:XH_, 0:S], par2(core, "b_f", rows=XH_), None, ALU.add))
        ACT.wait(m)
        m = ACT.done(nc.scalar.activation(sc, f, FN.Abs))
        ACT.wait(m)
        m = ACT.done(nc.scalar.activation(sc, sc, FN.Exp, scale=-1.0))
        ACT.wait(m)
        m = ACT.done(nc.scalar.activation(sc, sc, FN.Ln, bias=1.0))
        DVE.wait(m)
        m = DVE.done(nc.vector.scalar_tensor_tensor(f, f, 0.0, sc, ALU.min, ALU.subtract))
        DVE.wait(m)
        m = DVE.done(nc.vector.tensor_tensor_scan(sc, core.one_row[:, :], f, 0.0, ALU.mult, ALU.add))
        DVE.wait(m)
        DVE.done(nc.vector.tensor_scalar(cum, sc, float(HD) ** 0.5, None, ALU.mult))
        m = DVE.done(nc.vector.tensor_scalar(neg, sc, -(float(HD) ** 0.5), None, ALU.mult))
        PE.wait(m, ACT.own.mark(), st.s_ev.mark(), mkv)
        for dst, src, c0, b0 in ((va, pa, 6, 0), (vf, pf, 6, 2)):
            for t in range(2):
                for c in range(3):
                    ins = nc.tensor.transpose(core.bank(b0 + t)[:, c * P:c * P + P],
                                              src[:, c0 + c, t * P:t * P + P], core.ident())
            mt = PE.done(ins)
            DVE.wait(mt)
            for t in range(2):
                vals = DVE.done(nc.vector.tensor_copy(dst[:, t, :], core.bank(b0 + t)[:, 0:3 * P]))
        core.prog.join()
        attend(core, inner, pa, pf, qm, km, va, vf, vm, cum, neg)
        core.prog.join()
        m = core.split_x(core.tmp[:, :, :], 0, ND, DVE.own.mark())
        m = branch2(core, io["w_o_2"], l, (m,))
        post(core, m, "mix_post", flat(pa[:, 0:ND, :]), pa)
        core.prog.join()


def attend(core, ctx, pa, pf, qm, km, va, vf, vm, cum, neg):
    nc, PE, ACT, DVE, POOL = core.nc, core.PE, core.ACT, core.DVE, core.POOL
    W = S + P
    sc = [core.sb(f"scores{i}", [P, 2, W], ctx=ctx) for i in range(2)]
    pt = core.sb("probs_t", [P, 2, W], ctx=ctx)
    st = [core.sb(f"softmax{i}", [P, 3, 4], ctx=ctx) for i in range(2)]
    pairs = ([("moba", c) for c in range(AH // 2)] + [("mla", c) for c in range(MH // 2)]
             + [("fox", c) for c in range(XH_ // 2)])
    done_sc, done_out = {}, {}

    def operands(kind, c, h):
        rows = slice(64 * h, 64 * h + 64)
        if kind == "mla":
            r = slice(0, QKD)
            return qm[r, 2 * c + h, :], km[r, 2 * c + h, :], lambda t: vm[:, t, (2 * c + h) * HD:(2 * c + h + 1) * HD]
        src, v = (pa, va) if kind == "moba" else (pf, vf)
        return src[rows, c, :], src[rows, 3 + c, :], lambda t: v[:, t, c * P + 64 * h:c * P + 64 * h + 64]

    def scores(n):
        kind, c = pairs[n]
        b = n % 2
        PE.wait(*done_sc.get(n - 2, ()))
        for h in range(2):
            q, k, _ = operands(kind, c, h)
            bank = core.bank(2 * b + h)
            for t, o, keys in ((1, 0, S), (0, S, P)):
                out = bank[:, o:o + keys]
                more = kind == "fox"
                ins = nc.tensor.matmul(out, q[:, t * P:t * P + P], k[:, 0:keys], start=True, stop=not more,
                                       skip_group_check=True)
                if more:
                    pick = core.ident(XH_)[:, 2 * c + h:2 * c + h + 1]
                    nc.tensor.matmul(out, cum[:, t * P:t * P + P], pick.to_broadcast([XH_, keys]), start=False,
                                     stop=False, skip_group_check=True)
                    ins = nc.tensor.matmul(out, pick.to_broadcast([XH_, P]), neg[:, 0:keys], start=False,
                                           stop=True, skip_group_check=True)
        mm = PE.done(ins)
        scale = float(QKD if kind == "mla" else HD) ** -0.5
        s, red = sc[b], st[b]
        DVE.wait(mm, *done_out.get(n - 2, ()))
        for h in range(2):
            bias = core.t5[:, 2 * c + h, :] if kind == "moba" else con2(core, "mask")
            m = DVE.done(nc.vector.scalar_tensor_tensor(s[:, h, :], core.bank(2 * b + h)[:, 0:W], scale, bias,
                                                        ALU.mult, ALU.add))
        DVE.wait(m)
        DVE.done(nc.vector.tensor_reduce(red[:, 0, 0:2], s[:, :, 0:S], AX_X, ALU.max))
        m = DVE.done(nc.vector.tensor_reduce(red[:, 0, 2:4], s[:, :, S:W], AX_X, ALU.max))
        DVE.wait(m)
        m = DVE.done(nc.vector.tensor_scalar(red[:, 0, :], red[:, 0, :], -1.0, None, ALU.mult))
        ACT.wait(m)
        for h in range(2):
            for t, o, keys in ((0, 0, S), (1, S, P)):
                a = 2 * t + h
                m = ACT.done(nc.scalar.activation(s[:, h, o:o + keys], s[:, h, o:o + keys], FN.Exp,
                                                  bias=red[:, 0, a:a + 1], accum_out=red[:, 1, a:a + 1]))
        DVE.wait(m)
        m = DVE.done(nc.vector.reciprocal(red[:, 2, :], red[:, 1, :]))
        DVE.wait(m)
        for h in range(2):
            for t, o, keys in ((0, 0, S), (1, S, P)):
                a = 2 * t + h
                m = DVE.done(nc.vector.tensor_scalar(s[:, h, o:o + keys], s[:, h, o:o + keys],
                                                     red[:, 2, a:a + 1], None, ALU.mult))
        done_sc[n] = (m,)

    def values(n):
        kind, c = pairs[n]
        b = n % 2
        s = sc[b]
        PE.wait(*done_sc[n], *done_out.get(n - 1, ()))
        for h in range(2):
            for i in range(3):
                ins = nc.tensor.transpose(core.bank(4 + h)[:, i * P:i * P + P], s[:, h, i * P:i * P + P],
                                          core.ident())
        mt = PE.done(ins)
        ACT.wait(mt)
        for h in range(2):
            m = ACT.done(nc.scalar.copy(pt[:, h, :], core.bank(4 + h)[:, 0:W]))
        PE.wait(m)
        out = core.bank(6 + b)
        for h in range(2):
            v = operands(kind, c, h)[2]
            rows = slice(64 * h, 64 * h + 64)
            for t in range(2):
                nc.tensor.matmul(out[rows, P:S], v(t), pt[:, h, t * P:t * P + P], start=(t == 0), stop=(t == 1),
                                 skip_group_check=True)
            ins = nc.tensor.matmul(out[rows, 0:P], v(0), pt[:, h, S:W], start=True, stop=True,
                                   skip_group_check=True)
        mm = PE.done(ins)
        DVE.wait(mm)
        m = DVE.done(nc.vector.tensor_copy(core.tmp[:, n, :], out[:, 0:S]))
        done_out[n] = (mm, m)

    for n in range(len(pairs) + 1):
        if n < len(pairs):
            scores(n)
        if n:
            values(n - 1)


def branch2(core, w, l, after):
    wl = w[bass.ds(l, 1)]
    for kc in range(ND):
        m = core.st.row_block(wl, kc * P, core.x(kc), kc == 0, kc == ND - 1, after if kc == 0 else ())
    return m


def post(core, after, gain, flat, y):
    nc, ACT, DVE = core.nc, core.ACT, core.DVE
    ACT.wait(after)
    m = ACT.done(nc.scalar.copy(flat, core.banks(4, 4)))
    rs, summed = core.inv_rms(y[:, 0:ND, :], ND, D, core.bank(0), core.rs[:, 0, :], (m, core.st.s_ev.mark()))
    DVE.wait(rs, m)
    for c in range(ND):
        m = DVE.done(nc.vector.scalar_tensor_tensor(y[:, c, :], y[:, c, :], par2(core, gain, c), core.rs[:, 0, :],
                                                    ALU.mult, ALU.mult))
    DVE.wait(m)
    return DVE.done(nc.vector.tensor_tensor(core.h[:, :, :], core.h[:, :, :], y[:, 0:ND, :], ALU.add))


def conv_pair(core, pads, up):
    nc, ACT, DVE, st = core.nc, core.ACT, core.DVE, core.st
    cw, cb = PAR2["cw"][0], PAR2["cb"][0]

    def use(i, g, gm, u, um):
        two = lambda a: a.rearrange("p (c s) -> p c s", c=2)
        ACT.wait(gm, core.hid_free())
        m1 = st.s_ev.inc(nc.scalar.copy(pads[:, 0:2, 2:2 + S], two(g)))
        ACT.wait(um)
        m2 = st.s_ev.inc(nc.scalar.copy(pads[:, 2:4, 2:2 + S], two(u)))
        acc = [two(core.act_buf[:, :])[:, j, :] for j in range(2)] + [up[:, j, :] for j in range(2)]
        for j in range(4):
            DVE.wait(m1 if j < 2 else m2)
            c = i * 2 + (j % 2 + (NF if j >= 2 else 0))
            wt = lambda k: core.pv2[:, bass.ds(c * KC2 + (cw + k), 1)]
            m = DVE.done(nc.vector.tensor_scalar(acc[j], pads[:, j, 0:S], wt(0), core.pv2[:, bass.ds(c + cb, 1)],
                                                 ALU.mult, ALU.add))
            for k in range(1, KC2):
                DVE.wait(m)
                m = DVE.done(nc.vector.scalar_tensor_tensor(acc[j], pads[:, j, k:k + S], wt(k), acc[j],
                                                            ALU.mult, ALU.add))
            if j == 1:
                ACT.wait(m)
                ge = ACT.done(nc.scalar.activation(core.act_buf[:, :], core.act_buf[:, :], FN.Gelu_apprx_tanh))
        DVE.wait(ge, m, core.hid_free())
        return DVE.done(nc.vector.tensor_tensor(core.hid_buf[:, :], core.act_buf[:, :],
                                                up[:, :, :].rearrange("p c s -> p (c s)"), ALU.mult))
    return use


def layer2(core, io, l):
    nc = core.nc
    core.st.split()
    core.ACT.wait(core.DVE.own.mark(), core.ACT.own.mark())
    core.s_par.inc(nc.scalar.dma_start(core.pv2[:, :], io["par2"][bass.ds(l, 1)].rearrange("o p n -> p (o n)")), 16)
    for e in (core.ACT, core.DVE):
        e.wait(core.s_par.mark())
    mixer2(core, io, l)
    with ExitStack() as inner:
        core.hid_buf = core.sb("hid3", [P, 512], ctx=inner)
        pads, up = core.sb("pads2", [P, 4, 2 + S], ctx=inner), core.sb("conv_up", [P, 2, S], ctx=inner)
        sums = core.sb("sums", [P, ND, S], ctx=inner)
        core.DVE.done(nc.vector.memset(pads[:, :, 0:2], 0.0))
        m = core.ffn(io["w_up_2"], io["w_down_2"], l, lambda c: par2(core, "ffn_pre", c),
                     conv=conv_pair(core, pads, up), last=0)
        post(core, m, "ffn_post", sums[:, :, :].rearrange("p c s -> p (c s)"), sums)
        core.prog.join()
    core.st.skip_banks_to_start()
    core.st.skip_blocks()
    core.prog.join()


def first_constants():
    j, i = np.arange(P)[:, None], np.arange(P)[None, :]
    same = (j // DC) == (i // DC)
    masks = [j <= i, (j <= i) & same, (j < i) & same]
    for level in range(LEVELS):
        s = 1 << level
        masks.append((j // (2 * s) == i // (2 * s)) & (j % (2 * s) < s) & (i % (2 * s) >= s))
    return np.concatenate(masks, axis=1).astype(np.float32)


def columns(a):
    return np.asarray(a).reshape(a.shape[0], -1, P).transpose(0, 2, 1)


def rows(a):
    a = np.asarray(a)
    out = np.zeros((a.shape[0], P, 1), a.dtype)
    out[:, :a.shape[1], 0] = a
    return out


def taps(a):
    a = np.asarray(a)
    return a.reshape(a.shape[0], a.shape[1], -1, P).transpose(0, 3, 2, 1).reshape(a.shape[0], P, -1)


def first_params(v):
    return np.ascontiguousarray(np.concatenate([
        columns(v["ffn1_norm"]), columns(v["mix_norm"]), columns(v["ffn2_norm"]), taps(v["ssm_conv_w"]),
        columns(v["ssm_conv_b"]), columns(np.repeat(np.asarray(v["ssm_d"]), SP, axis=1)), columns(v["ssm_norm"]),
        taps(v["dn_conv_w"]), columns(v["dn_norm"]), rows(v["ssm_dt_bias"]), rows(v["ssm_a_log"]),
        rows(v["dn_dt_bias"]), rows(v["dn_a_log"])], axis=2))


def second_constants():
    q, k = np.arange(P)[:, None], np.arange(P)[None, :]
    own = np.where(k <= q, 0.0, NEG)
    mask = np.concatenate([np.zeros((P, P)), own, own], axis=1)
    half = ROPE // 2
    rot, cos, sin = np.zeros((P, P)), np.ones((P, S), np.float32), np.zeros((P, S), np.float32)
    i = np.arange(half)
    rot[64 + half + i, 64 + i], rot[64 + i, 64 + half + i] = -1.0, 1.0
    inv = np.float32(10000.0) ** (-i.astype(np.float32) / np.float32(half))
    ang = (np.arange(S, dtype=np.float32)[None, :] * inv[:, None]).astype(np.float32)
    cos[64:96], sin[64:96] = np.tile(np.cos(ang), (2, 1)), np.tile(np.sin(ang), (2, 1))
    return np.concatenate([mask, rot, cos, sin], axis=1).astype(np.float32)


def bucket_constants():
    n = np.maximum(S - 1 - np.arange(S + P), 0)
    far = 16 + (np.log(np.maximum(n, 1).astype(np.float32) / np.float32(16)) / np.float32(np.log(64.0))
                * np.float32(16)).astype(np.int32)
    bucket = np.where(n < 16, n, np.minimum(far, 31))
    onehot = np.arange(P)[:, None] == bucket[None, :]
    return np.concatenate([np.eye(P)[::-1], onehot], axis=1).astype(np.float32)


def second_params(v):
    return np.ascontiguousarray(np.concatenate([
        columns(v["ln_mix_pre_2"]), columns(v["ln_mix_post_2"]), columns(v["ln_ffn_pre_2"]),
        columns(v["ln_ffn_post_2"]), rows(v["b_f_2"]), columns(v["q_norm_2"]), columns(v["kv_norm_2"]),
        taps(v["conv_w_2"]), columns(v["conv_b_2"])], axis=2))


WEIGHTS = ("ffn1_w_in", "ffn1_w_out", "w_in", "ssm_w_branch", "dn_w_branch", "w_out", "ffn2_w_in", "ffn2_w_out",
           "w_in_2", "w_uq_2", "w_ukv_2", "w_o_2", "w_up_2", "w_down_2")


def program(nc, io, out, passes):
    with ExitStack() as ctx:
        k = Kernel(nc, ctx, passes)
        PE, ACT, DVE, POOL, SP = k.PE, k.ACT, k.DVE, k.POOL, k.SP
        token = k.tmp[:, :, :].rearrange("p c s -> p (c s)").rearrange("p (t d) -> p t d", t=2)
        k.one_row = k.sb("one_row", [XH_, S])
        ones = POOL.done(nc.gpsimd.memset(k.ones[:, :], 1.0))
        POOL.done(nc.gpsimd.memset(k.one_row[:, :], 1.0))
        POOL.done(nc.gpsimd.memset(k.eps[:, 0:1], EPS))
        POOL.done(nc.gpsimd.memset(k.eps[:, 1:2], -0.5 * float(np.log(DK))))
        k.s_par.inc(nc.sync.dma_start(token, io["x"].rearrange("o (t p) d -> p (o t) d", p=P)), 16)
        k.s_par.inc(nc.sync.dma_start(k.con0[:, :], io["con0"]), 16)
        for e in (PE, ACT, DVE, POOL):
            e.wait(k.s_par.mark(), POOL.own.mark())
        for c in range(ND):
            for t in range(2):
                ins = nc.tensor.transpose(k.banks(0, 4)[:, c * S + t * P:c * S + t * P + P],
                                          token[:, t, c * P:c * P + P], k.ident())
        turned = PE.done(ins)
        DVE.wait(turned)
        DVE.done(nc.vector.tensor_copy(k.h[:, :, :].rearrange("p c s -> p (c s)"), k.banks(0, 4)))
        k.prog.join()
        with ExitStack() as part:
            k.con1, k.pv, k.nega = (k.sb(n, s, ctx=part) for n, s in (
                ("con1", [P, NCON1]), ("pv", [P, NPAR1]), ("nega", [P, 2])))
            k.s_par = Sem(k.prog, "par1_landed")
            k.s_par.inc(nc.sync.dma_start(k.con1[:, :], io["con1"]), 16)
            for e in (ACT, DVE, POOL):
                e.wait(k.s_par.mark())
            with k.prog.loop(L) as l:
                layer1(k, io, l)
        rs, summed = k.inv_rms(k.h[:, :, :], ND, D, k.bank(7), k.rs[:, 0, :])
        DVE.wait(rs, summed)
        for c in range(ND):
            g = k.con0[:, CON0["final_norm"][0] + c:CON0["final_norm"][0] + c + 1]
            DVE.done(nc.vector.scalar_tensor_tensor(k.h[:, c, :], k.h[:, c, :], g, k.rs[:, 0, :], ALU.mult, ALU.mult))
        k.prog.join()
        with ExitStack() as part:
            k.con2, k.pv2, k.t5 = (k.sb(n, s, ctx=part) for n, s in (
                ("con2", [P, NCON2]), ("pv2", [P, NPAR2]), ("t5_bias", [P, AH, S + P])))
            SP.wait(*[s.mark() for s in k.prog.joined])
            k.s_par = Sem(k.prog, "par2_landed")
            k.s_par.inc(nc.sync.dma_start(k.con2[:, :], io["con2"]), 16)
            moba_bias(k, io)
            for e in (PE, ACT, DVE, POOL):
                e.wait(k.s_par.mark())
            with k.prog.loop(L) as l:
                layer2(k, io, l)
        PE.wait(DVE.own.mark())
        for t in range(2):
            for c in range(ND):
                ins = nc.tensor.transpose(k.banks(0, 4)[:, t * D + c * P:t * D + c * P + P],
                                          k.h[:, c, t * P:t * P + P], k.ident())
        turned = PE.done(ins)
        DVE.wait(turned)
        m = DVE.done(nc.vector.tensor_copy(token.rearrange("p t d -> p (t d)"), k.banks(0, 4)))
        SP.wait(m)
        s_out = Sem(k.prog, "out_stored")
        s_out.inc(nc.sync.dma_start(out.rearrange("o (t p) d -> p (o t) d", p=P), token), 16)
        SP.wait(s_out.mark())


def kernel(**inputs):
    import concourse.bacc as bacc
    from concourse.bass_utils import run_bass_kernel_spmd as run

    v = {n: np.asarray(a) for n, a in inputs.items()}
    arrays = {n: np.ascontiguousarray(v[n]) for n in WEIGHTS}
    arrays["x"] = np.ascontiguousarray(v["x"])
    arrays["rel_bias"] = np.ascontiguousarray(v["rel_bias_2"])
    arrays["par1"], arrays["par2"] = first_params(v), second_params(v)
    arrays["con0"] = np.ascontiguousarray(np.concatenate(
        [np.eye(P, dtype=np.float32), v["final_norm"].reshape(ND, P).T], axis=1))
    arrays["con1"], arrays["con2"], arrays["con_t5"] = first_constants(), second_constants(), bucket_constants()
    passes = {}
    for _ in range(2):
        nc = bacc.Bacc("TRN2", target_bir_lowering=False, num_devices=1)
        io = {n: nc.dram_tensor("in_" + n, a.shape, F32, kind="ExternalInput").ap() for n, a in arrays.items()}
        io["scratch"] = nc.dram_tensor("bias_scratch", [AH, S + P], F32).ap()
        out = nc.dram_tensor("out", [1, S, D], F32, kind="ExternalOutput").ap()
        program(nc, io, out, passes)
    r = run(nc, [{"in_" + n: a for n, a in arrays.items()}], core_ids=[0])
    return r.results[0]["out"]
```

```python
from contextlib import ExitStack, contextmanager

import numpy as np
import concourse.bass as bass
from concourse import mybir

F32 = mybir.dt.float32
F32R = mybir.dt.float32r
ALU = mybir.AluOpType
FN = mybir.ActivationFunctionType
AX_X = mybir.AxisListType.X

P = 128
S = 256
D = 1024
ND = D // P
L = 2
FF = 2816
NF = FF // P
EPS = 1e-6
NEG = -1e30
SI, SG, SH, SP, SN = 2048, 4, 32, 64, 128
HG = SH // SG
SCONV = SI + 2 * SG * SN
DH, DK = 8, 128
DC = 64
DCONV = 3 * DH * DK
COL_Z, COL_XBC = 0, SI
COL_DT = COL_XBC + SCONV
COL_QKV = COL_DT + SH
COL_ZD = COL_QKV + DCONV
COL_B = COL_ZD + DH * DK
COL_A = COL_B + DH
COL_GS = COL_A + DH
COL_GD = COL_GS + D
AH, MH, XH_, HD = 6, 4, 6, 64
QR, KVR, ROPE = 256, 128, 32
QKD = 96
COL2_KR = 3 * AH * HD + QR + KVR
COL2_F = COL2_KR + ROPE
COL2_FG = COL2_F + 3 * XH_ * HD
KC2 = 3

def table(widths):
    at, out = 0, {}
    for name, n in widths:
        out[name] = (at, n)
        at += n
    return out, at


PAR1, NPAR1 = table([("ffn1_norm", ND), ("mix_norm", ND), ("ffn2_norm", ND), ("ssm_cw", 4 * SCONV // P),
                     ("ssm_cb", SCONV // P), ("ssm_d", SI // P), ("ssm_norm", SI // P),
                     ("dn_cw", 4 * DCONV // P), ("dn_norm", 1), ("ssm_dtb", 1), ("ssm_alog", 1),
                     ("dn_dtb", 1), ("dn_alog", 1)])
PAR2, NPAR2 = table([("mix_pre", ND), ("mix_post", ND), ("ffn_pre", ND), ("ffn_post", ND), ("b_f", 1),
                     ("q_norm", QR // P), ("kv_norm", 1), ("cw", KC2 * 2 * NF), ("cb", 2 * NF)])
CON0, NCON0 = table([("ident", P), ("final_norm", ND)])
LEVELS = 6
CON1, NCON1 = table([("causal", P), ("incl", P), ("strict", P), ("level", LEVELS * P)])
CON2, NCON2 = table([("mask", S + P), ("rot", P), ("cos", S), ("sin", S)])
CONT, NCONT = table([("flip", P), ("bucket", S + P)])


class Count:

    def __init__(self, const=0, terms=()):
        self.const, self.terms = const, tuple(t for t in terms if t[2])

    def __add__(self, n):
        return Count(self.const + n, self.terms)

    def value(self):
        v = self.const
        for _, reg, k in self.terms:
            v = reg * k + v
        return v


class Sem:

    def __init__(self, prog, name, virtual=False):
        self.sem = None if virtual else prog.ctx.enter_context(prog.nc.semaphore(name))
        self.name, self.count = name, Count()
        prog.sems.append(self)

    def inc(self, ins, n=1):
        ins.then_inc(self.sem, n)
        return self.later(n)

    def later(self, n):
        self.count = self.count + n
        return (self, self.count)

    def mark(self, ago=0):
        return (self, self.count + (-ago))


class Engine:

    def __init__(self, prog, eng, name):
        self.eng, self.own = eng, Sem(prog, "done_" + name)
        self.idle = Sem(prog, "idle_" + name)
        prog.engines.append(self)

    def done(self, ins):
        return self.own.inc(ins)

    def wait(self, *marks):
        for sem, count in marks:
            self.eng.wait_ge(sem.sem, count.value())


    def settle(self):
        self.eng.sem_inc(self.idle.sem, 1)


class Program:
    def __init__(self, nc, ctx, passes):
        self.nc, self.ctx, self.passes = nc, ctx, passes
        self.sems, self.engines, self.loops, self.joined = [], [], 0, []
        self.PE = Engine(self, nc.tensor, "pe")
        self.ACT = Engine(self, nc.scalar, "act")
        self.DVE = Engine(self, nc.vector, "dve")
        self.POOL = Engine(self, nc.gpsimd, "pool")
        self.SP = Engine(self, nc.sync, "sp")

    @contextmanager
    def loop(self, trips):
        me = self.loops
        self.loops += 1
        start = [s.count for s in self.sems]
        step = self.passes.get(me, [0] * len(start))
        at = self.ring_places()
        for e in self.engines:
            e.settle()
        with self.nc.Fori(0, trips) as i:
            for s, c, k in zip(self.sems, start, step):
                s.count = Count(c.const, c.terms + ((me, i, k),))
            yield i
            took = [s.count.const - c.const for s, c in zip(self.sems, start)]
            self.passes[me] = took
            assert at == self.ring_places(), "a pass must leave every ring where it found it"
        for s, c, k in zip(self.sems, start, took):
            s.count = Count(c.const + k * trips, c.terms)

    def join(self):
        marks = [s.mark() for s in self.joined]
        for e in (self.PE, self.ACT, self.DVE, self.POOL):
            e.wait(*marks)


RAW, SPL, OUTB = 4, 4, 4
AHEAD = 2
BLK = 1024


class Stream:

    def __init__(self, k):
        pr = self.prog = k.prog
        self.k = k
        self.raw = [k.sb(f"raw{i}", [P, BLK]) for i in range(RAW)]
        self.hi = [k.sb(f"w_hi{i}", [P, BLK], F32R) for i in range(SPL)]
        self.lo = [k.sb(f"w_lo{i}", [P, BLK], F32R) for i in range(SPL)]
        self.s_raw = [Sem(pr, f"raw{i}_landed") for i in range(RAW)]
        self.s_hi, self.s_mm, self.s_ev = (Sem(pr, n) for n in ("w_hi", "w_mm", "out_read"))
        self.s_lo = [Sem(pr, f"w_lo_{n}") for n in ("even", "odd")]
        self.want = [Sem(pr, f"raw{i}_wanted", True) for i in range(RAW)]
        self.loads = [Sem(pr, f"loads{i}", True) for i in range(2)]
        self.load_at = self.split_at = self.mm_at = self.out_at = 0
        self.put_off = []
        pr.ring_places = lambda: (self.load_at, self.split_at, self.mm_at, self.out_at)
        self.outs = Sem(pr, "outs", True)
        for sem, n in ((self.s_lo[0], RAW // 2), (self.s_lo[1], RAW // 2), (self.s_mm, SPL), (self.s_ev, OUTB)):
            pr.nc.gpsimd.sem_inc(sem.sem, n)
            sem.later(n)

    def load(self, parts):
        pr, s = self.prog, self.load_at
        pr.SP.wait((self.s_lo[s % 2], self.loads[s % 2].count + 1))
        pr.SP.settle()
        for view, src in parts:
            self.s_raw[s].inc(pr.nc.sync.dma_start(view(self.raw[s]), src), 16)
        self.loads[s % 2].later(1)
        self.load_at = (s + 1) % RAW

    def split(self):
        pr, s, b = self.prog, self.split_at, self.split_at % SPL
        self.want[s].later(32)
        pr.ACT.wait((self.s_raw[s], self.want[s].count), (self.s_mm, self.s_hi.count + 1))
        self.s_hi.inc(pr.nc.scalar.copy(self.hi[b][:, :], self.raw[s][:, :]))
        e = (pr.POOL, pr.DVE)[s % 2]
        e.wait(self.s_hi.mark())
        self.s_lo[s % 2].inc(e.eng.tensor_tensor(self.lo[b][:, :], self.raw[s][:, :],
                                                 self.hi[b][:, :].bitcast(F32), ALU.subtract))
        self.split_at = (s + 1) % RAW

    def block(self, parts, emit, after=(), ahead=True):
        pr, b = self.prog, self.mm_at
        odd = self.load_at % 2
        self.load(parts)
        made = (self.s_lo[odd], self.loads[odd].count + RAW // 2)
        if ahead:
            self.split()
        self.flush()
        pr.PE.wait(made, *after)
        self.s_mm.inc(emit(self.hi[b], self.lo[b]))
        self.mm_at = (b + 1) % SPL
        return self.s_mm.mark()

    def flush(self):
        put_off, self.put_off = self.put_off, []
        for stages in put_off:
            for _ in stages:
                self.put_off.append(stages)
                break

    def drain(self):
        while self.put_off:
            self.flush()

    def unit_parts(self, w, col, half, cols=None):
        rows = lambda a: w[:, half * 512 + a * 256:half * 512 + a * 256 + 256, :]
        if cols is None:
            return [((lambda r, a=a: r[:, a * 512:a * 512 + 512].rearrange("p (c n) -> p c n", c=2)),
                     rows(a)[:, :, bass.ds(col, 256)].rearrange("o (c p) n -> p (o c) n", p=P)) for a in range(2)]
        whole = w[:, half * 512:half * 512 + 512, :]
        return [((lambda r, a=a: r[:, :].rearrange("p (c n) -> p c n", c=4)[:, :, a * P:a * P + P]),
                 whole[:, :, cols[a]:cols[a] + P].rearrange("o (c p) n -> p (o c) n", p=P)) for a in range(2)]

    def unit(self, w, col, x, after=(), cols=None, extra=None):
        pr, nc = self.prog, self.prog.nc
        bank = self.k.bank(self.out_at)
        free = (self.s_ev, self.ev_due() + 1)
        for half in range(2):
            def emit(hi, lo, half=half):
                for t in range(2):
                    for c in range(4):
                        kc = 4 * half + c
                        wh = hi[:, c * 256 + t * P:c * 256 + t * P + P]
                        wl = lo[:, c * 256 + t * P:c * 256 + t * P + P]
                        out = bank[:, t * S:t * S + S]
                        xh, xl = x[0][:, kc, :], x[1][:, kc, :]
                        for n, (a, b) in enumerate(((wh, xh), (wh, xl), (wl, xh))):
                            ins = nc.tensor.matmul(out, a, b, start=(kc == 0 and t == 0 and n == 0),
                                                   stop=(kc == 7 and n == 2), skip_group_check=True)
                return extra(half, hi, lo, x) if extra else ins
            mark = self.block(self.unit_parts(w, col, half, cols), emit, (*after, free))
        self.out_at = (self.out_at + 1) % OUTB
        self.outs.later(1)
        return bank, mark

    def row_block(self, w, row, x, first, final, after=(), ahead=True):
        nc, k = self.prog.nc, self.k

        def emit(hi, lo):
            for t in range(8):
                out = k.bank(4 + t // 2)[:, (t % 2) * S:(t % 2) * S + S]
                wh, wl = hi[:, t * P:t * P + P], lo[:, t * P:t * P + P]
                for n, (a, b) in enumerate(((wh, x[0]), (wh, x[1]), (wl, x[0]))):
                    ins = nc.tensor.matmul(out, a, b, start=(first and t % 2 == 0 and n == 0),
                                           stop=(final and n == 2), skip_group_check=True)
            return ins
        src = w[:, bass.ds(row, P), :].rearrange("o p n -> p (o n)")
        parts = [((lambda r, a=a: r[:, a * 512:a * 512 + 512]), src[:, a * 512:a * 512 + 512]) for a in range(2)]
        return self.block(parts, emit, after, ahead)

    def skip_banks_to_start(self):
        n = -self.out_at % OUTB
        if n:
            self.prog.POOL.settle()
            self.s_ev.inc(self.prog.nc.gpsimd.memset(self.k.tick[:, 4:5], 0.0), n)
            self.outs.later(n)
            self.out_at = 0

    def skip_blocks(self):
        pr, n = self.prog, -self.load_at % RAW
        if n:
            pr.POOL.settle()
            odd = [(i + self.load_at) % 2 for i in range(n)].count(1)
            for i, (s, by) in enumerate(((self.s_hi, n), (self.s_mm, n), (self.s_lo[0], n - odd), (self.s_lo[1], odd))):
                if by:
                    s.inc(pr.nc.gpsimd.memset(self.k.tick[:, i:i + 1], 0.0), by)
            for i, by in enumerate((n - odd, odd)):
                self.loads[i].later(by)
            self.load_at = self.split_at = 0
            self.mm_at = (self.mm_at + n) % SPL

    def latest(self):
        return self.k.bank((self.out_at - 1) % OUTB), self.s_mm.mark()

    def ev_due(self):
        return self.outs.count


class Kernel:
    def __init__(self, nc, ctx, passes):
        self.nc, self.ctx = nc, ctx
        self.prog = Program(nc, ctx, passes)
        self.PE, self.ACT, self.DVE, self.POOL, self.SP = (
            self.prog.PE, self.prog.ACT, self.prog.DVE, self.prog.POOL, self.prog.SP)
        self.psum = ctx.enter_context(nc.psum_tensor("psum", [P, 8, 512], F32))
        self.h = self.sb("h", [P, ND, S])
        self.xh = self.sb("x_hi", [P, 32, S], F32R)
        self.xl = self.sb("x_lo", [P, 32, S], F32R)
        self.tmp = self.sb("tmp", [P, ND, S])
        self.rs = self.sb("rs", [P, 2, S])
        self.ones = self.sb("ones", [P, P])
        self.eps = self.sb("eps", [P, 2])
        self.act_buf = self.sb("act", [P, 2 * S])
        self.tick = self.sb("tick", [P, 5])
        self.con0 = self.sb("con0", [P, NCON0])
        self.s_par = Sem(self.prog, "params_landed")
        self.st = Stream(self)
        self.s_hid = Sem(self.prog, "hidden_split")
        self.s_conv = Sem(self.prog, "conv_done")
        for sem in [e.own for e in self.prog.engines] + [self.s_hid, self.s_conv]:
            nc.gpsimd.sem_inc(sem.sem, 1)
            sem.later(1)
        self.prog.joined = [e.own for e in (self.PE, self.ACT, self.DVE, self.POOL)] + [
            self.s_hid, self.s_conv, self.st.s_hi, *self.st.s_lo, self.st.s_mm, self.st.s_ev]

    def sb(self, name, shape, dt=F32, ctx=None):
        return (ctx or self.ctx).enter_context(self.nc.sbuf_tensor(name, shape, dt))

    def bank(self, i):
        return self.psum[:, i, :]

    def banks(self, i, n):
        return self.psum[:, i:i + n, :].rearrange("p b n -> p (b n)")

    def ident(self, n=P):
        return self.con0[0:n, 0:n]

    def inv_rms(self, src, chunks, width, bank, out, after=()):
        nc = self.nc
        self.ACT.wait(*after)
        self.PE.wait(*after)
        for c in range(0, chunks, 2):
            n = min(2, chunks - c)
            sq = self.ACT.done(nc.scalar.activation(self.tmp[:, c:c + n, :], src[:, c:c + n, :], FN.Square))
            self.PE.wait(sq)
            for j in range(c, c + n):
                ins = nc.tensor.matmul(bank[:, 0:S], self.ones[:, :], self.tmp[:, j, :],
                                       start=(j == 0), stop=(j == chunks - 1))
        summed = self.PE.done(ins)
        return self.inv_sqrt(bank[:, 0:S], out, width, summed), summed

    def inv_sqrt(self, src, out, width, after, scale=None):
        nc = self.nc
        self.ACT.wait(after)
        m = self.ACT.done(nc.scalar.activation(out, src, FN.Ln, scale=1.0 / width, bias=self.eps[:, 0:1]))
        self.ACT.wait(m)
        if scale is None:
            return self.ACT.done(nc.scalar.activation(out, out, FN.Exp, scale=-0.5))
        return self.ACT.done(nc.scalar.activation(out, out, FN.Exp, scale=-0.5, bias=scale))

    def norm_split(self, src, gain, chunks, width, dst, after=()):
        nc = self.nc
        rs, summed = self.inv_rms(src, chunks, width, self.bank(7), self.rs[:, 0, :], after)
        self.DVE.wait(rs, summed)
        for a in range(0, chunks, 2):
            n = min(2, chunks - a)
            for c in range(a, a + n):
                m = self.DVE.done(nc.vector.scalar_tensor_tensor(self.tmp[:, c, :], src[:, c, :], gain(c),
                                                                 self.rs[:, 0, :], ALU.mult, ALU.mult))
            self.ACT.wait(m)
            hi = self.ACT.done(nc.scalar.copy(self.xh[:, dst + a:dst + a + n, :], self.tmp[:, a:a + n, :]))
            if a >= 2 or chunks <= 2:
                self.lo_part(dst, a - 2 if chunks > 2 else a, 2 if chunks > 2 else n, before if chunks > 2 else hi)
            before = hi
        return self.lo_part(dst, chunks - 2, 2, before) if chunks > 2 else self.DVE.own.mark()

    def lo_part(self, dst, a, n, hi):
        self.DVE.wait(hi)
        return self.DVE.done(self.nc.vector.tensor_tensor(
            self.xl[:, dst + a:dst + a + n, :], self.tmp[:, a:a + n, :],
            self.xh[:, dst + a:dst + a + n, :].bitcast(F32), ALU.subtract))

    def split_x(self, src, dst, chunks, after):
        nc = self.nc
        self.ACT.wait(after)
        hi = self.ACT.done(nc.scalar.copy(self.xh[:, dst:dst + chunks, :], src))
        self.DVE.wait(hi, after)
        return self.DVE.done(nc.vector.tensor_tensor(self.xl[:, dst:dst + chunks, :], src,
                                                     self.xh[:, dst:dst + chunks, :].bitcast(F32), ALU.subtract))

    def x(self, a, n=None):
        return (self.xh[:, a:a + n, :], self.xl[:, a:a + n, :]) if n else (self.xh[:, a, :], self.xl[:, a, :])

    def down(self, w, l, after, last):
        row = lambda kc: (self.xh[:, bass.ds(8 + kc, 1), :].rearrange("p o s -> p (o s)"),
                          self.xl[:, bass.ds(8 + kc, 1), :].rearrange("p o s -> p (o s)"))
        wl = w[bass.ds(l, 1)]
        for kc in range(2):
            self.st.row_block(wl, kc * P, row(kc), kc == 0, False, after)
        self.st.drain()
        self.PE.wait(self.s_hid.mark())
        with self.prog.loop((NF - 6) // 4) as i:
            for j in range(4):
                self.st.row_block(wl, i * (4 * P) + (2 + j) * P, row(i * 4 + (2 + j)), False, False)
        for kc in range(NF - 4, NF):
            m = self.st.row_block(wl, kc * P, row(kc), False, kc == NF - 1,
                                  ahead=not (last and kc >= NF - AHEAD))
        return m

    def ffn(self, w_in, w_out, l, gain, conv=None, last=False):
        nc, st = self.nc, self.st
        self.prog.join()
        ready = self.norm_split(self.h[:, :, :], gain, ND, D, 0)
        act = self.act_buf
        hid = self.hid_buf
        wl = w_in[bass.ds(l, 1)]
        x = self.x(0, ND)

        def pair(i):
            g, gm = st.unit(wl, i * 256, x, after=(ready,))
            st.put_off.append(gate_chunks(i, g, gm))
            u, um = st.unit(wl, i * 256 + FF, x)
            st.put_off.append(value_chunks(i, u, um))

        def gate_chunks(i, g, gm):
            if conv:
                yield from conv(i, g, gm, 0, act)
                self.ACT.wait(self.DVE.own.mark(), self.s_conv.mark())
                self.ACT.done(nc.scalar.activation(act[:, :], act[:, :], FN.Gelu_apprx_tanh))
            else:
                self.ACT.wait(gm, self.hid_free())
                st.s_ev.inc(nc.scalar.activation(act[:, :], g, FN.Silu))
            yield

        def value_chunks(i, u, um):
            if conv:
                yield from conv(i, u, um, 2, self.up_buf)
                self.DVE.wait(self.ACT.own.mark(), self.DVE.own.mark(), self.s_conv.mark(), self.hid_free())
                f = self.DVE.done(nc.vector.tensor_tensor(hid[:, :], act[:, :], self.up_buf[:, :], ALU.mult))
            else:
                self.DVE.wait(st.s_ev.mark(), um, self.hid_free())
                f = st.s_ev.inc(nc.vector.tensor_tensor(hid[:, :], act[:, :], u, ALU.mult))
            c = bass.ds(i * 2 + 8, 2)
            out_h = self.xh[:, c, :].rearrange("p c s -> p (c s)")
            out_l = self.xl[:, c, :].rearrange("p c s -> p (c s)")
            self.ACT.wait(f)
            hi = self.ACT.done(nc.scalar.copy(out_h, hid[:, :]))
            self.DVE.wait(hi, f)
            self.s_hid.inc(nc.vector.tensor_tensor(out_l, hid[:, :], out_h.bitcast(F32), ALU.subtract))

        pair(0)
        st.put_off = []
        with self.prog.loop((NF // 2 - 1) // 2) as i:
            st.put_off = [value_chunks(i * 2, *st.latest())]
            pair(i * 2 + 1)
            pair(i * 2 + 2)
            st.put_off = []
        st.put_off = [value_chunks(NF // 2 - 1, *st.latest())]
        return self.down(w_out, l, (self.s_hid.mark(),), last)

    def hid_free(self):
        return self.s_hid.mark()

    def add_sum(self, scale, after):
        nc = self.nc
        self.DVE.wait(after)
        for b in range(4):
            hb = self.h[:, 2 * b:2 * b + 2, :].rearrange("p c s -> p (c s)")
            m = self.DVE.done(nc.vector.scalar_tensor_tensor(hb, self.bank(4 + b), scale, hb, ALU.mult, ALU.add))
        return m


def par1(core, name, i=0, n=1, rows=P):
    a, width = PAR1[name]
    assert i + n <= width
    return core.pv[0:rows, a + i:a + i + n]


def con1(core, name, i=0, n=P):
    a = CON1[name][0]
    return core.con1[:, a + i:a + i + n]


def wide(core, mask, n):
    return mask.unsqueeze(1).to_broadcast([P, n, P])

def conv_taps(core, bank, mark, taps, weight, bias, pad, acc, free):
    nc, ACT, DVE = core.nc, core.ACT, core.DVE
    two = bank.rearrange("p (c s) -> p c s", c=2)
    ACT.wait(mark, *free)
    padded = ACT.done(nc.scalar.copy(pad[:, :, taps - 1:taps - 1 + S], two))
    for j in range(2):
        ins = nc.scalar.activation(acc[:, j, :], two[:, j, :], FN.Identity, scale=weight(j, taps - 1),
                                   bias=bias(j) if bias else 0.0)
        m = ACT.done(ins) if j == 0 else core.st.s_ev.inc(ins)
    DVE.wait(padded, m)
    before = (), ()
    for k in range(taps - 1):
        now = []
        for j in range(2):
            DVE.wait(*before[j])
            ins = nc.vector.scalar_tensor_tensor(acc[:, j, :], pad[:, j, k:k + S], weight(j, k), acc[:, j, :],
                                                 ALU.mult, ALU.add)
            now.append(((DVE.done(ins) if (j, k) != (1, taps - 2) else core.s_conv.inc(ins)),))
        before = now
    return now[0][0], now[1][0]


def conv_unit(core, bank, mark, c, taps, weight, bias, dst):
    acc = core.act_buf[:, :].rearrange("p (c s) -> p c s", c=2)
    free = core.s_conv.mark(), core.ACT.own.mark()
    summed = conv_taps(core, bank, mark, taps, lambda j, k: weight(c, j, k),
                       (lambda j: bias(c, j)) if bias else None, core.pad_buf, acc, free)
    yield
    core.ACT.wait(*summed)
    core.ACT.done(core.nc.scalar.activation(dst[:, bass.ds(c, 2), :], acc, FN.Silu))


def project(core, w, col, units, x, use, peel=4):
    st = core.st
    assert (units - peel) % 4 == 0

    def unit(u, at):
        bank, mark = st.unit(w, at, x)
        st.put_off.append(use(u, bank, mark))
    for u in range(peel):
        unit(u, col + u * 256)
    if units > peel:
        st.put_off = []
        with core.prog.loop((units - peel) // 4) as i:
            st.put_off = [use(i * 4 + (peel - 1), *st.latest())]
            for j in range(4):
                unit(i * 4 + (peel + j), i * 1024 + (col + (peel + j) * 256))
            st.put_off = []
        st.put_off = [use(units - 1, *st.latest())]


def act_unit(core, func, dst):
    def use(u, bank, mark):
        core.ACT.wait(mark)
        core.st.s_ev.inc(core.nc.scalar.activation(
            dst[:, bass.ds(u * 2, 2), :].rearrange("p c s -> p (c s)"), bank, func))
        yield
    return use


def softplus(core, x, scratch, rows, after):
    nc = core.nc
    core.ACT.wait(after)
    m = core.ACT.done(nc.scalar.activation(scratch, x, FN.Abs))
    core.ACT.wait(m)
    m = core.ACT.done(nc.scalar.activation(scratch, scratch, FN.Exp, scale=-1.0))
    core.ACT.wait(m)
    m = core.ACT.done(nc.scalar.activation(scratch, scratch, FN.Ln, bias=1.0))
    yield
    core.DVE.wait(m, after)
    return core.DVE.done(nc.vector.scalar_tensor_tensor(x, x, 0.0, scratch, ALU.max, ALU.add))


def spread_row(core, out, src, row, rows, after):
    core.PE.wait(*after)
    return core.nc.tensor.matmul(out, core.ident(rows)[:, row:row + 1].to_broadcast([rows, P]), src,
                                 start=True, stop=True, skip_group_check=True)


def small_params(core, bank, mark, ready):
    nc, PE, ACT, DVE = core.nc, core.PE, core.ACT, core.DVE
    raw, raw_a = core.hd_raw[:, 0:2 * S], core.hd_raw[0:DH, 2 * S:3 * S]
    ACT.wait(mark)
    ACT.done(nc.scalar.copy(raw_a, core.bank(7)[0:DH, 0:S]))
    mark = core.st.s_ev.inc(nc.scalar.copy(raw, bank[0:SH, :]))
    own = ACT.own.mark()
    yield
    DVE.wait(mark, own)
    hs, hd = core.hs, core.hd
    dt, la, ac, te, sc = (hs[:, i, :] for i in range(5))
    beta, g, eg, bg, ed, scd = (hd[:, i, :] for i in range(6))
    m1 = DVE.done(nc.vector.tensor_scalar(dt, raw[:, 0:S], par1(core, "ssm_dtb", rows=SH), None, ALU.add))
    m1 = yield from softplus(core, dt, sc, SH, m1)
    na = ACT.done(nc.scalar.activation(core.nega[0:SH, 0:1], par1(core, "ssm_alog", rows=SH), FN.Exp))
    nd = ACT.done(nc.scalar.activation(core.nega[0:DH, 1:2], par1(core, "dn_alog", rows=DH), FN.Exp))
    DVE.wait(na, nd, m1)
    m = DVE.done(nc.vector.tensor_scalar(la, dt, core.nega[0:SH, 0:1], -1.0, ALU.mult, ALU.mult))
    DVE.wait(m)
    for t in range(2):
        c = slice(t * P, t * P + P)
        m = DVE.done(nc.vector.tensor_tensor_scan(ac[:, c], core.ones[0:SH, :], la[:, c], 0.0, ALU.mult, ALU.add))
    yield
    ACT.wait(m)
    for t in range(2):
        c = slice(t * P, t * P + P)
        m = ACT.done(nc.scalar.activation(te[:, c], ac[:, c], FN.Exp, scale=-1.0,
                                          bias=ac[:, t * P + P - 1:t * P + P]))
    ssm = m
    bank_b, bank_a = raw[0:DH, S:2 * S], raw_a
    ACT.wait(mark, m1)
    mb = ACT.done(nc.scalar.activation(beta, bank_b, FN.Sigmoid))
    DVE.wait(mark)
    m = DVE.done(nc.vector.tensor_scalar(g, bank_a, par1(core, "dn_dtb", rows=DH), None, ALU.add))
    m = yield from softplus(core, g, scd, DH, m)
    DVE.wait(m)
    m = DVE.done(nc.vector.tensor_scalar(scd, g, core.nega[0:DH, 1:2], -1.0, ALU.mult, ALU.mult))
    DVE.wait(m)
    for c in range(S // DC):
        s = slice(c * DC, c * DC + DC)
        m = DVE.done(nc.vector.tensor_tensor_scan(g[:, s], core.ones[0:DH, 0:DC], scd[:, s], 0.0,
                                                  ALU.mult, ALU.add))
    yield
    ACT.wait(m)
    for c in range(S // DC):
        s = slice(c * DC, c * DC + DC)
        ACT.done(nc.scalar.activation(ed[:, s], g[:, s], FN.Exp, scale=-1.0,
                                      bias=g[:, c * DC + DC - 1:c * DC + DC]))
    me = ACT.done(nc.scalar.activation(eg, g, FN.Exp))
    DVE.wait(me, mb)
    m = DVE.done(nc.vector.tensor_tensor(bg, beta, eg, ALU.mult))
    yield
    PE.wait(m, ssm, me)
    PE.settle()
    out = core.bank(6)
    for n, a in enumerate((dt, ac, te)):
        for t in range(2):
            nc.tensor.transpose(out[:, (2 * n + t) * SH:(2 * n + t + 1) * SH], a[:, t * P:t * P + P],
                                core.ident(SH))
    for n, a in enumerate((g, beta, bg, ed)):
        for t in range(2):
            at = 6 * SH + (2 * n + t) * DH
            ins = nc.tensor.transpose(out[:, at:at + DH], a[:, t * P:t * P + P], core.ident(DH))
    m = PE.done(ins)
    yield
    DVE.wait(m)
    ready.append(DVE.done(nc.vector.tensor_copy(core.cols[:, :], out[:, 0:6 * SH + 8 * DH])))


def scol(core, what, t, h, n=1):
    at = (2 * ("dt", "ac", "te").index(what) + t) * SH + h
    return core.cols[:, at:at + n]


def dcol(core, what, t, h, n=1):
    at = 6 * SH + (2 * ("g", "beta", "bg", "ed").index(what) + t) * DH + h
    return core.cols[:, at:at + n]

def side_by_side(*chains):
    chains = list(chains)
    while chains:
        for chain in list(chains):
            for _ in chain:
                break
            else:
                chains.remove(chain)


def delta(core, cols_ready):
    for h0 in range(0, DH, 4):
        side_by_side(*(delta_heads(core, h0 + 2 * side, side, cols_ready) for side in range(2)))


def delta_heads(core, h0, side, cols_ready):
    nc, PE, ACT, DVE, POOL = core.nc, core.PE, core.ACT, core.DVE, core.POOL
    W = 2 * S
    d = {name: a[:, side * W:side * W + W] for name, a in core.dn.items() if name != "state"}
    state = core.dn["state"][:, side * S:side * S + S]
    work = core.tmp[:, 4 * side:4 * side + 4, :]
    low, high = (work[:, 2 * i:2 * i + 2, :].rearrange("p c s -> p (c s)") for i in range(2))
    T, U, un, wt = low, high, d["dec"], low
    bank = lambda i: core.bank(4 * side + i)
    tile = lambda i: slice(i * P, i * P + P)
    four = lambda a: a.rearrange("p (n j) -> p n j", n=4)
    qkv = core.qkv
    q, k, v = (lambda h, n=n: qkv[:, n * DH + h0 + h, :] for n in range(3))
    two = lambda n: qkv[:, n * DH + h0:n * DH + h0 + 2, :]
    flat = lambda a: a.rearrange("p c s -> p (c s)")
    prior = (PE.own.mark(), ACT.own.mark(), DVE.own.mark(), POOL.own.mark())

    ACT.wait(*prior)
    for n in range(2):
        m = ACT.done(nc.scalar.activation(work[:, 2 * n:2 * n + 2, :], two(n), FN.Square))
    PE.wait(m, *prior)
    for n in range(4):
        ins = nc.tensor.matmul(bank(n // 2)[:, (n % 2) * S:(n % 2) * S + S], core.ones[:, :], work[:, n, :],
                               start=True, stop=True, skip_group_check=True)
    mm = PE.done(ins)
    yield
    for n, a in enumerate((low, high)):
        m = core.inv_sqrt(bank(n), a, 1.0, mm, None if n else core.eps[:, 1:2])
        DVE.wait(m, *prior)
        normed = DVE.done(nc.vector.tensor_tensor(flat(two(n)), flat(two(n)), a, ALU.mult))
    PE.wait(m, normed, cols_ready)
    for h in range(2):
        c = slice(h * S, h * S + S)
        spread_row(core, bank(2)[:, c], core.hd[:, 1, :], h0 + h, DH, ())
        spread_row(core, bank(3)[:, c], core.hd[:, 0, :], h0 + h, DH, ())
    spread = PE.done(nc.tensor.transpose(bank(0)[:, tile(0)], k(0)[:, 0:P], core.ident()))
    for h in range(2):
        for t in range(2):
            c = slice(t * P, t * P + P)
            if h or t:
                nc.tensor.transpose(bank(0)[:, tile(2 * h + t)], k(h)[:, c], core.ident())
            ins = nc.tensor.transpose(bank(1)[:, tile(2 * h + t)], v(h)[:, c], core.ident())
    turned = PE.done(ins)
    yield
    ACT.wait(spread)
    eg = ACT.done(nc.scalar.activation(d["eg"], bank(2), FN.Exp))
    DVE.wait(eg, cols_ready)
    column = lambda name, i: dcol(core, name, i % 2, h0 + i // 2)
    for i in range(4):
        m = DVE.done(nc.vector.tensor_scalar(d["dec"][:, tile(i)], bank(2)[:, tile(i)], column("g", i), 0.0,
                                             ALU.subtract, ALU.min))
    ACT.wait(m)
    dec = ACT.done(nc.scalar.activation(d["dec"], d["dec"], FN.Exp))
    qd = DVE.done(nc.vector.tensor_tensor(d["qd"], flat(two(0)), d["eg"], ALU.mult))
    DVE.wait(turned)
    for name, scale, src in (("kbg", "bg", 0), ("kdec", "ed", 0), ("vb", "beta", 1)):
        for i in range(4):
            rows = DVE.done(nc.vector.tensor_scalar(d[name][:, tile(i)], bank(src)[:, tile(i)], column(scale, i),
                                                    None, ALU.mult))
    yield
    PE.wait(rows)
    for i in range(4):
        h, c = i // 2, slice((i % 2) * P, (i % 2) * P + P)
        ins = nc.tensor.matmul(bank(0)[:, tile(i)], k(h)[:, c], k(h)[:, c], start=True, stop=True,
                               skip_group_check=True)
    kk = PE.done(ins)
    for i in range(4):
        h, c = i // 2, slice((i % 2) * P, (i % 2) * P + P)
        ins = nc.tensor.matmul(bank(1)[:, tile(i)], k(h)[:, c], q(h)[:, c], start=True, stop=True,
                               skip_group_check=True)
    qk = PE.done(ins)
    yield
    DVE.wait(kk, dec)
    m = DVE.done(nc.vector.tensor_tensor(d["kk"], bank(0), d["dec"], ALU.mult))
    DVE.wait(qk)
    aqk = DVE.done(nc.vector.tensor_tensor(d["aqk"], bank(1), d["dec"], ALU.mult))
    DVE.wait(m)
    kk = DVE.done(nc.vector.tensor_tensor(d["kk"], d["kk"], bank(3), ALU.mult))
    yield

    def level_blocks(level, read):
        POOL.wait(kk, *read)
        return POOL.done(nc.gpsimd.tensor_tensor(four(d["km"]), four(d["kk"]),
                                                 wide(core, con1(core, "level", level * P), 4), ALU.mult))
    m = level_blocks(0, ())
    POOL.wait(m)
    mu = POOL.done(nc.gpsimd.tensor_tensor(four(U), wide(core, core.ident(), 4), four(d["km"]), ALU.subtract))
    lm = level_blocks(1, (mu,))
    PE.wait(mu)
    for i in range(4):
        ins = nc.tensor.transpose(bank(2)[:, tile(i)], U[:, tile(i)], core.ident())
    mm = PE.done(ins)
    ACT.wait(mm, aqk)
    mt = ACT.done(nc.scalar.copy(T, bank(2)))
    yield
    for level in range(1, LEVELS):
        final = level == LEVELS - 1
        PE.wait(lm, mt)
        for i in range(4):
            ins = nc.tensor.matmul(bank(0)[:, tile(i)], d["km"][:, tile(i)], T[:, tile(i)], start=True, stop=True,
                                   skip_group_check=True)
        mp = PE.done(ins)
        if not final:
            lm = level_blocks(level + 1, (mp,))
        else:
            POOL.wait(aqk)
            aqk = POOL.done(nc.gpsimd.tensor_tensor(four(d["aqk"]), four(d["aqk"]),
                                                    wide(core, con1(core, "incl"), 4), ALU.mult))
        ACT.wait(mp, aqk if level == 1 else mp)
        m = ACT.done(nc.scalar.copy(d["dec"], bank(0)))
        yield
        PE.wait(m, mu)
        if not final:
            for i in range(4):
                ins = nc.tensor.matmul(bank(1)[:, tile(i)], U[:, tile(i)], d["dec"][:, tile(i)], start=True,
                                       stop=True, skip_group_check=True)
            mm = PE.done(ins)
            DVE.wait(mm)
            mt = DVE.done(nc.vector.tensor_tensor(T, T, bank(1), ALU.subtract))
        for i in range(4):
            ins = nc.tensor.matmul(bank(2)[:, tile(i)], d["dec"][:, tile(i)], U[:, tile(i)], start=True,
                                   stop=True, skip_group_check=True)
        mm = PE.done(ins)
        DVE.wait(mm)
        mu = DVE.done(nc.vector.tensor_tensor(U, U, bank(2), ALU.subtract))
        yield
    PE.wait(mu)
    for i in range(4):
        ins = nc.tensor.matmul(bank(0)[:, tile(i)], U[:, tile(i)], d["vb"][:, tile(i)], start=True, stop=True,
                               skip_group_check=True)
    mm = PE.done(ins)
    DVE.wait(mm)
    un_ready = DVE.done(nc.vector.tensor_copy(un, bank(0)))
    for i in range(4):
        ins = nc.tensor.matmul(bank(1)[:, tile(i)], d["kbg"][:, tile(i)], U[:, tile(i)], start=True, stop=True,
                               skip_group_check=True)
    mm = PE.done(ins)
    ACT.wait(mm)
    wt_ready = ACT.done(nc.scalar.copy(wt, bank(1)))
    yield
    new, st_ready, outs = un_ready, None, []
    for c in range(S // DC):
        t, off = c // 2, (c % 2) * DC
        rows = slice(off, off + DC)
        ws_p, s_p, o_p = bank(0)[:, 0:S], bank(0)[:, S:2 * S], bank(1 + c % 2)
        cs = lambda h: slice((2 * h + t) * P + off, (2 * h + t) * P + off + DC)
        hv = lambda h: slice(h * P, h * P + P)
        PE.wait(*(outs[c - 2:c - 1] if c >= 2 else (wt_ready,)))
        if c:
            PE.wait(st_ready)
            for h in range(2):
                ins = nc.tensor.matmul(ws_p[rows, hv(h)], wt[:, cs(h)], state[:, hv(h)], start=True, stop=True,
                                       skip_group_check=True)
            mm = PE.done(ins)
            for h in range(2):
                nc.tensor.matmul(o_p[:, h * DC:h * DC + DC], state[:, hv(h)], d["qd"][:, cs(h)],
                                 start=(h == 0), stop=False, skip_group_check=True)
            DVE.wait(mm)
            un_c = un[rows, :].rearrange("p (h t v) -> p h t v", h=2, t=2)[:, :, t, :]
            new = DVE.done(nc.vector.tensor_tensor(un_c, un_c, ws_p[rows, :].rearrange("p (h v) -> p h v", h=2),
                                                   ALU.subtract))
            yield
        PE.wait(new, aqk)
        if c < S // DC - 1:
            for h in range(2):
                ins = nc.tensor.matmul(s_p[:, hv(h)], d["kdec"][rows, tile(2 * h + t)], un[rows, tile(2 * h + t)],
                                       start=True, stop=True, skip_group_check=True)
            mm = PE.done(ins)
            DVE.wait(mm)
            for h in range(2):
                last = h * S + c * DC + DC - 1
                if c:
                    st_ready = DVE.done(nc.vector.scalar_tensor_tensor(
                        state[:, hv(h)], state[:, hv(h)], d["eg"][:, last:last + 1], s_p[:, hv(h)],
                        ALU.mult, ALU.add))
                else:
                    st_ready = DVE.done(nc.vector.tensor_copy(state[:, hv(h)], s_p[:, hv(h)]))
        for h in range(2):
            ins = nc.tensor.matmul(o_p[:, h * DC:h * DC + DC], un[rows, tile(2 * h + t)], d["aqk"][rows, cs(h)],
                                   start=(c == 0 and h == 0), stop=True, skip_group_check=True)
        mm = PE.done(ins)
        ACT.wait(mm, qd)
        outs.append(ACT.done(nc.scalar.copy(core.o[:, h0:h0 + 2, c * DC:c * DC + DC],
                                            o_p[:, 0:2 * DC].rearrange("p (h s) -> p h s", h=2))))
        yield
    ACT.wait(outs[-1])
    sq = ACT.done(nc.scalar.activation(work[:, 0:2, :], core.o[:, h0:h0 + 2, :], FN.Square))
    PE.wait(sq)
    for n in range(2):
        ins = nc.tensor.matmul(bank(3)[:, n * S:n * S + S], core.ones[:, :], work[:, n, :],
                               start=True, stop=True, skip_group_check=True)
    mm = PE.done(ins)
    yield
    m = core.inv_sqrt(bank(3), high, DK, mm)
    yield
    DVE.wait(m, outs[-1])
    m = DVE.done(nc.vector.scalar_tensor_tensor(high, flat(core.o[:, h0:h0 + 2, :]), par1(core, "dn_norm"), high,
                                                ALU.mult, ALU.mult))
    DVE.wait(m)
    m = DVE.done(nc.vector.tensor_tensor(high, high, flat(core.zd[:, h0:h0 + 2, :]), ALU.mult))
    yield
    core.split_x(work[:, 2:4, :], 24 + h0, 2, m)


def ssm(core, cols_ready):
    tail = ()
    for g in range(SG):
        done = []
        side_by_side(*(ssm_heads(core, g, side, cols_ready, done) for side in range(2)), *tail)
        tail = (ssm_tail(core, g, done),)
    side_by_side(*tail)


def ssm_heads(core, g, side, cols_ready, done):
    nc, PE, ACT, DVE, POOL = core.nc, core.PE, core.ACT, core.DVE, core.POOL
    n = HG // 2
    h0, c0 = g * HG + side * n, 4 * g + 2 * side
    b = {name: a[:, side * a.shape[1] // 2:(side + 1) * a.shape[1] // 2] for name, a in core.sm.items()}
    bank = lambda i: core.bank(4 * side + i)
    prior = (PE.own.mark(), ACT.own.mark(), DVE.own.mark())
    nx = SI // P
    B, C = core.xbc[:, nx + g, :], core.xbc[:, nx + SG + g, :]
    ac_p = core.banks(4 * side, 2)
    PE.wait(*prior, cols_ready)
    for h in range(n):
        ins = spread_row(core, ac_p[:, h * S:h * S + S], core.hs[:, 2, :], h0 + h, SH, ())
    spread = PE.done(ins)
    cb_p, xt_p = bank(2), bank(3)
    for t in range(2):
        c = slice(t * P, t * P + P)
        nc.tensor.matmul(cb_p[:, c], B[:, c], C[:, c], start=True, stop=True, skip_group_check=True)
    cbm = PE.done(nc.tensor.transpose(cb_p[:, 2 * P:3 * P], B[:, 0:P], core.ident()))
    for t in range(2):
        for c in range(2):
            ins = nc.tensor.transpose(xt_p[:, t * S + c * P:t * S + c * P + P],
                                      core.xbc[:, c0 + c, t * P:t * P + P], core.ident())
    turned = PE.done(ins)
    yield
    DVE.wait(spread, *prior)
    for h in range(n):
        for t in range(2):
            o = slice(h * S + t * P, h * S + t * P + P)
            m = DVE.done(nc.vector.tensor_scalar(b["w"][:, o], ac_p[:, o], scol(core, "ac", t, h0 + h), 0.0,
                                                 ALU.subtract, ALU.min))
    ACT.wait(m, *prior)
    heads = lambda a: a.rearrange("p (h s) -> p h s", h=n)
    ea = ACT.done(nc.scalar.activation(heads(b["cs"]), heads(ac_p)[:, :, P:S], FN.Exp))
    dec = ACT.done(nc.scalar.activation(b["w"], b["w"], FN.Exp))
    DVE.wait(turned)
    over = lambda a: a.unsqueeze(2).to_broadcast([P, n, SP])
    for t in range(2):
        c = slice(t * S, t * S + S)
        xd = DVE.done(nc.vector.tensor_tensor(heads(b["xd"][:, c]), heads(xt_p[:, c]),
                                              over(scol(core, "dt", t, h0, n)), ALU.mult))
    DVE.wait(cbm)
    bt = DVE.done(nc.vector.tensor_copy(b["bt"], cb_p[:, 2 * P:3 * P]))
    DVE.wait(xd)
    xe = DVE.done(nc.vector.tensor_tensor(heads(b["xe"]), heads(b["xd"][:, 0:S]),
                                          over(scol(core, "te", 0, h0, n)), ALU.mult))
    cbs = DVE.done(nc.vector.tensor_tensor(b["cb"].rearrange("p (t l) -> p t l", t=2),
                                           cb_p[:, 0:2 * P].rearrange("p (t l) -> p t l", t=2),
                                           wide(core, con1(core, "causal"), 2), ALU.mult))
    core.cb_read = cbs
    yield
    PE.wait(xe, bt, ea)
    mm = PE.done(nc.tensor.matmul(bank(0)[:, 0:S], b["bt"], b["xe"], start=True, stop=True))
    ACT.wait(mm)
    state = ACT.done(nc.scalar.copy(b["state"], bank(0)[:, 0:S]))
    POOL.wait(ea, *prior)
    cs = POOL.done(nc.gpsimd.tensor_tensor(heads(b["cs"]), heads(b["cs"]), wide(core, C[:, P:S], n), ALU.mult))
    DVE.wait(dec, cbs)
    w = DVE.done(nc.vector.tensor_tensor(heads(b["w"]), heads(b["w"]),
                                         b["cb"].unsqueeze(1).to_broadcast([P, n, S]), ALU.mult))
    yield
    y_p = bank(1)
    PE.wait(w, cs, state)
    for h in range(n):
        rows = slice((h % 2) * SP, (h % 2) * SP + SP)
        for t in range(2):
            o = y_p[rows, (h // 2) * S + t * P:(h // 2) * S + t * P + P]
            ins = nc.tensor.matmul(o, b["xd"][:, t * S + h * SP:t * S + h * SP + SP],
                                   b["w"][:, h * S + t * P:h * S + t * P + P],
                                   start=True, stop=(t == 0), skip_group_check=True)
            if t == 1:
                ins = nc.tensor.matmul(o, b["state"][:, h * SP:h * SP + SP], b["cs"][:, h * P:h * P + P],
                                       start=False, stop=True, skip_group_check=True)
    mm = PE.done(ins)
    yield
    yield
    DVE.wait(mm, *core.tail_done)
    y = core.tmp[:, 2 * side:2 * side + 2, :]
    for c in range(2):
        m = DVE.done(nc.vector.scalar_tensor_tensor(y[:, c, :], core.xbc[:, c0 + c, :],
                                                    par1(core, "ssm_d", c0 + c), y_p[:, c * S:c * S + S],
                                                    ALU.mult, ALU.add))
    DVE.wait(m)
    done.append(DVE.done(nc.vector.tensor_tensor(y, y, core.z[:, c0:c0 + 2, :], ALU.mult)))


def ssm_tail(core, g, done):
    nc, PE, ACT, DVE = core.nc, core.PE, core.ACT, core.DVE
    y, work = core.tmp[:, 0:4, :], core.tmp[:, 4:8, :]
    ACT.wait(*done, *core.tail_done)
    sq = ACT.done(nc.scalar.activation(work, y, FN.Square))
    yield
    yield
    PE.wait(sq, core.cb_read)
    out = core.bank(6)[:, 0:S]
    for c in range(4):
        ins = nc.tensor.matmul(out, core.ones[:, :], work[:, c, :], start=(c == 0), stop=(c == 3),
                               skip_group_check=True)
    rs = core.inv_sqrt(out, core.rs[:, 1, :], 512, PE.done(ins))
    yield
    DVE.wait(rs)
    for c in range(4):
        m = DVE.done(nc.vector.scalar_tensor_tensor(work[:, c, :], y[:, c, :], par1(core, "ssm_norm", 4 * g + c),
                                                    core.rs[:, 1, :], ALU.mult, ALU.mult))
    yield
    m2 = core.split_x(work, 8 + 4 * g, 4, m)
    core.tail_done = (m, m2, ACT.own.mark())


def branch(core, w, l, chunks, at, after):
    wl = w[bass.ds(l, 1)]
    one = lambda kc: (core.xh[:, bass.ds(at + kc, 1), :].rearrange("p o s -> p (o s)"),
                      core.xl[:, bass.ds(at + kc, 1), :].rearrange("p o s -> p (o s)"))
    st = core.st
    for kc in range(4):
        m = st.row_block(wl, kc * P, one(kc), kc == 0, False, after if kc == 0 else ())
    if chunks > 8:
        with core.prog.loop(chunks // 4 - 2) as i:
            for j in range(4):
                st.row_block(wl, i * (4 * P) + (4 + j) * P, one(i * 4 + (4 + j)), False, False)
    for kc in range(chunks - 4, chunks):
        m = st.row_block(wl, kc * P, one(kc), False, kc == chunks - 1)
    return m


def mixer1(core, io, l):
    nc, PE, ACT, DVE, POOL, st = core.nc, core.PE, core.ACT, core.DVE, core.POOL, core.st
    core.prog.join()
    w = io["w_in"][bass.ds(l, 1)]
    x = core.x(0, ND)
    u = core.norm_split(core.h[:, :, :], lambda c: par1(core, "mix_norm", c), ND, D, 0)
    PE.wait(u)
    POOL.settle()
    for j in range(2):
        m = POOL.done(nc.gpsimd.memset(core.pad_buf[:, j, 0:3], 0.0))
    ACT.wait(m)
    DVE.wait(m)
    bank, mark = st.unit(w, None, x, cols=(COL_DT, COL_B), extra=lambda *a: small_extra(core, *a))
    ready = []
    st.put_off.append(small_params(core, bank, mark, ready))
    cw = lambda name: (lambda c, j, k: core.pv[:, bass.ds(c * 4 + (PAR1[name][0] + 4 * j + k), 1)])
    dw, sw = cw("dn_cw"), cw("ssm_cw")
    project(core, w, COL_QKV, DCONV // 256, x,
                 lambda i, bank, mark: conv_unit(core, bank, mark, i * 2, 4, dw, None, core.qkv))
    cols_ready, = ready
    project(core, w, COL_ZD, DH * DK // 256, x, act_unit(core, FN.Silu, core.zd))
    st.drain()
    with ExitStack() as inner:
        core.dn = buffers(core, inner, "dn", dict(eg=1024, dec=1024, qd=1024, kbg=1024, kdec=1024, vb=1024,
                                                  kk=1024, aqk=1024, km=1024))
        core.dn["state"] = core.act_buf
        core.o = core.qkv
        core.prog.join()
        delta(core, cols_ready)
        core.prog.join()
    with ExitStack() as inner:
        core.z = core.sb("z", [P, SI // P, S], ctx=inner)
        core.sm = buffers(core, inner, "ssm", dict(w=2048, cs=1024, cb=512, bt=2 * P, xd=1024, xe=512))
        core.sm["state"] = core.act_buf
        core.xbc = core.qkv
        bias = lambda c, j: core.pv[:, bass.ds(c + (PAR1["ssm_cb"][0] + j), 1)]
        project(core, w, COL_XBC, SCONV // 256, x,
                     lambda i, bank, mark: conv_unit(core, bank, mark, i * 2, 4, sw, bias, core.xbc))
        project(core, w, COL_Z, SI // 256, x, act_unit(core, FN.Silu, core.z), peel=8)
        st.drain()
        core.prog.join()
        core.tail_done = ()
        ssm(core, cols_ready)
        core.prog.join()
    with ExitStack() as inner:
        gates = core.sb("gates", [P, 2 * ND, S], ctx=inner)
        project(core, w, COL_GS, 2 * D // 256, x, act_unit(core, FN.Sigmoid, gates), peel=8)
        st.drain()
        flat = lambda a: a.rearrange("p c s -> p (c s)")
        core.prog.join()
        m = branch(core, io["ssm_w_branch"], l, SI // P, 8, ())
        DVE.wait(m)
        for b in range(4):
            m = DVE.done(nc.vector.tensor_tensor(flat(core.tmp[:, 2 * b:2 * b + 2, :]), core.bank(4 + b),
                                                 flat(gates[:, 2 * b:2 * b + 2, :]), ALU.mult))
        m = branch(core, io["dn_w_branch"], l, DH, 24, (m,))
        DVE.wait(m)
        for b in range(4):
            gb = flat(gates[:, ND + 2 * b:ND + 2 * b + 2, :])
            m = DVE.done(nc.vector.tensor_tensor(gb, core.bank(4 + b), gb, ALU.mult))
        DVE.wait(m)
        m = DVE.done(nc.vector.tensor_tensor(flat(core.tmp[:, :, :]), flat(core.tmp[:, :, :]),
                                             flat(gates[:, ND:2 * ND, :]), ALU.add))
        m = core.split_x(core.tmp[:, :, :], 0, ND, m)
        m = branch(core, io["w_out"], l, ND, 0, (m,))
        core.add_sum(1.0, m)
        core.prog.join()


def small_extra(core, half, hi, lo, x):
    for c in range(4):
        kc = 4 * half + c
        wh, wl = (a[:, c * 256 + P + DH:c * 256 + 2 * P] for a in (hi, lo))
        for n, (a, b) in enumerate(((wh, x[0][:, kc, :]), (wh, x[1][:, kc, :]), (wl, x[0][:, kc, :]))):
            ins = core.nc.tensor.matmul(core.bank(7)[0:P - DH, 0:S], a, b, start=(kc == 0 and n == 0),
                                        stop=(kc == 7 and n == 2), skip_group_check=True)
    return ins


def layer1(core, io, l):
    nc = core.nc
    for _ in range(AHEAD):
        core.st.split()
    core.ACT.wait(core.DVE.own.mark(), core.ACT.own.mark())
    core.s_par.inc(nc.scalar.dma_start(core.pv[:, :], io["par1"][bass.ds(l, 1)].rearrange("o p n -> p (o n)")), 16)
    for e in (core.ACT, core.DVE):
        e.wait(core.s_par.mark())
    with ExitStack() as inner:
        core.hid_buf = core.sb("hid1", [P, 512], ctx=inner)
        m = core.ffn(io["ffn1_w_in"], io["ffn1_w_out"], l, lambda c: par1(core, "ffn1_norm", c))
        core.add_sum(0.5, m)
        core.prog.join()
    with ExitStack() as inner:
        core.qkv = core.sb("qkv", [P, 3 * DH, S], ctx=inner)
        core.pad_buf = core.sb("pad", [P, 2, 3 + S], ctx=inner)
        core.zd = core.sb("zd", [P, DH, S], ctx=inner)
        core.hd_raw = core.tmp[0:SH, :, :].rearrange("p c s -> p (c s)")
        core.hs = core.sb("heads_ssm", [SH, 5, S], ctx=inner)
        core.hd = core.sb("heads_dn", [DH, 6, S], ctx=inner)
        core.cols = core.sb("cols", [P, 6 * SH + 8 * DH], ctx=inner)
        mixer1(core, io, l)
    with ExitStack() as inner:
        core.hid_buf = core.sb("hid2", [P, 512], ctx=inner)
        m = core.ffn(io["ffn2_w_in"], io["ffn2_w_out"], l, lambda c: par1(core, "ffn2_norm", c), last=True)
        core.add_sum(0.5, m)
        core.prog.join()
    core.st.skip_banks_to_start()
    core.st.skip_blocks()
    core.prog.join()


def buffers(core, ctx, stage, sizes):
    return {name: core.sb(stage + "_" + name, [P, n], ctx=ctx) for name, n in sizes.items()}


def par2(core, name, i=0, n=1, rows=P):
    a, width = PAR2[name]
    assert i + n <= width
    return core.pv2[0:rows, a + i:a + i + n]


def con2(core, name, rows=slice(0, P)):
    a, n = CON2[name]
    return core.con2[rows, a:a + n]


def moba_bias(core, io):
    nc, PE, ACT, DVE, SP = core.nc, core.PE, core.ACT, core.DVE, core.SP
    with ExitStack() as inner:
        cont = core.sb("con_t5", [P, NCONT], ctx=inner)
        relb = core.sb("rel_bias", [32, AH], ctx=inner)
        line = core.sb("bias_line", [AH, S + P], ctx=inner)
        slid = core.sb("bias_slid", [P, AH, S], ctx=inner)
        core.s_par.inc(nc.sync.dma_start(cont[:, :], io["con_t5"]), 16)
        core.s_par.inc(nc.sync.dma_start(relb[:, :], io["rel_bias"]), 16)
        flip = cont[:, CONT["flip"][0]:CONT["flip"][0] + P]
        onehot = cont[0:32, CONT["bucket"][0]:CONT["bucket"][0] + S + P]
        for e in (PE, DVE):
            e.wait(core.s_par.mark())
        mm = PE.done(nc.tensor.matmul(core.bank(0)[0:AH, 0:S + P], relb[:, :], onehot, start=True, stop=True))
        DVE.wait(mm)
        m = DVE.done(nc.vector.tensor_copy(line[:, :], core.bank(0)[0:AH, 0:S + P]))
        DVE.wait(m)
        m = DVE.done(nc.vector.memset(line[:, S:S + P], NEG))
        SP.wait(m)
        scratch = io["scratch"]
        core.s_par.inc(nc.sync.dma_start(scratch, line[:, :]), 16)
        SP.wait(core.s_par.mark())
        src = bass.AP(scratch.tensor, scratch.offset, [[1, P], [S + P, AH], [1, S]])
        core.s_par.inc(nc.sync.dma_start(slid[:, :, :], src), 16)
        PE.wait(core.s_par.mark(), m)
        for h in range(AH):
            ins = nc.tensor.matmul(core.bank(h // 2)[:, (h % 2) * S:(h % 2) * S + S], flip, slid[:, h, :],
                                   start=True, stop=True, skip_group_check=True)
        mm = PE.done(ins)
        ACT.wait(mm)
        for h in range(AH):
            b = core.bank(h // 2)[:, (h % 2) * S:(h % 2) * S + S]
            ACT.done(nc.scalar.copy(core.t5[:, h, 0:S], b))
            ACT.done(nc.scalar.copy(core.t5[:, h, S:S + P], b[:, P:S]))
        core.prog.join()


def units(core, w, cols, x, use):
    for n, col in enumerate(cols):
        bank, mark = core.st.unit(w, col, x)
        use(n, bank, mark)


def copy_unit(core, dst):
    def use(n, bank, mark):
        core.ACT.wait(mark)
        core.st.s_ev.inc(core.nc.scalar.copy(dst[:, 2 * n:2 * n + 2, :].rearrange("p c s -> p (c s)"), bank))
    return use


def mixer2(core, io, l):
    nc, PE, ACT, DVE, POOL, st = core.nc, core.PE, core.ACT, core.DVE, core.POOL, core.st
    core.prog.join()
    w = io["w_in_2"][bass.ds(l, 1)]
    x = core.x(0, ND)
    flat = lambda a: a.rearrange("p c s -> p (c s)")
    with ExitStack() as inner:
        sb = lambda name, shape: core.sb(name, shape, ctx=inner)
        pa, pf = sb("proj_a", [P, 12, S]), sb("proj_f", [P, 9, S])
        va, vf, vm = sb("v_moba", [P, 2, 3 * P]), sb("v_fox", [P, 2, 3 * P]), sb("v_mla", [P, 2, S])
        qm, km, kr = sb("q_mla", [P, MH, S]), sb("k_mla", [P, MH, S]), sb("k_rope", [P, 2, S])
        fg, dec = sb("forget", [P, 2 * XH_]), sb("decay", [XH_, 4, S])
        u = core.norm_split(core.h[:, :, :], lambda c: par2(core, "mix_pre", c), ND, D, 0)
        PE.wait(u)
        units(core, w, [256 * n for n in range(6)], x, copy_unit(core, pa))
        units(core, w, [COL2_F + 256 * n for n in range(4)], x, copy_unit(core, pf))
        bank, mark = st.unit(w, None, x, cols=(COL2_KR - 64, COL2_F + 8 * P))
        ACT.wait(mark)
        ACT.done(nc.scalar.copy(kr[64:96, 0, :], bank[64:96, 0:S]))
        st.s_ev.inc(nc.scalar.copy(pf[:, 8, :], bank[:, S:2 * S]))

        def forget(hi, lo):
            for t in range(2):
                for kc in range(ND):
                    a, b = (v[:, kc, t * P:t * P + P] for v in x)
                    wh, wl = (v[:, kc * XH_:(kc + 1) * XH_] for v in (hi, lo))
                    for n, (p, q) in enumerate(((a, wh), (b, wh), (a, wl))):
                        ins = nc.tensor.matmul(core.bank(7)[:, t * XH_:t * XH_ + XH_], p, q,
                                               start=(kc == 0 and n == 0), stop=(kc == 7 and n == 2),
                                               skip_group_check=True)
            return ins
        parts = [((lambda r, a=a: r[:, a * 4 * XH_:(a + 1) * 4 * XH_].rearrange("p (c n) -> p c n", c=4)),
                  w[:, a * 512:a * 512 + 512, COL2_FG:COL2_FG + XH_].rearrange("o (c p) n -> p (o c) n", p=P))
                 for a in range(2)]
        mm = st.block(parts, forget)
        DVE.wait(mm)
        fgm = DVE.done(nc.vector.tensor_copy(fg[:, :], core.bank(7)[:, 0:2 * XH_]))
        cq = core.norm_split(pa[:, 9:11, :], lambda c: par2(core, "q_norm", c), 2, QR, 8,
                             (ACT.own.mark(), st.s_ev.mark(), fgm))
        ckv = core.norm_split(pa[:, 11:12, :], lambda c: par2(core, "kv_norm", c), 1, KVR, 10,
                              (cq, st.s_ev.mark()))
        q_p = core.banks(4, 2)
        for kc in range(2):
            def up_q(hi, lo, kc=kc):
                a, b = core.x(8 + kc)
                for h in range(MH):
                    wh, wl = (v[:, h * QKD:(h + 1) * QKD] for v in (hi, lo))
                    for n, (p, q) in enumerate(((wh, a), (wh, b), (wl, a))):
                        ins = nc.tensor.matmul(q_p[0:QKD, h * S:h * S + S], p, q,
                                               start=(kc == 0 and h % 2 == 0 and n == 0),
                                               stop=(kc == 1 and n == 2), skip_group_check=True)
                return ins
            half = MH * QKD // 2
            parts = [((lambda r, a=a: r[:, a * half:(a + 1) * half]),
                      io["w_uq_2"][bass.ds(l, 1), kc * P:kc * P + P, a * half:(a + 1) * half].rearrange(
                          "o p n -> p (o n)")) for a in range(2)]
            mq = st.block(parts, up_q, (cq,))
        k_p, v_p = core.banks(2, 2), core.bank(6)

        def up_kv(hi, lo):
            a, b = core.x(10)
            for h in range(MH):
                wh, wl = (v[:, h * P:(h + 1) * P] for v in (hi, lo))
                for n, (p, q) in enumerate(((wh, a), (wh, b), (wl, a))):
                    nc.tensor.matmul(k_p[:, h * S:h * S + S], p, q, start=(n == 0), stop=(n == 2),
                                     skip_group_check=True)
            for t in range(2):
                c = slice(t * P, t * P + P)
                wh, wl = (v[:, 0:MH * P].rearrange("p (h n) -> p h n", h=MH)[:, :, HD:P] for v in (hi, lo))
                for n, (p, q) in enumerate(((a[:, c], wh), (b[:, c], wh), (a[:, c], wl))):
                    ins = nc.tensor.matmul(v_p[:, t * S:t * S + S], p, q, start=(n == 0), stop=(n == 2),
                                           skip_group_check=True)
            return ins
        parts = [((lambda r, a=a: r[:, a * S:(a + 1) * S]),
                  io["w_ukv_2"][bass.ds(l, 1), :, a * S:(a + 1) * S].rearrange("o p n -> p (o n)"))
                 for a in range(2)]
        mkv = st.block(parts, up_kv, (ckv, st.s_ev.mark()))
        ACT.wait(mkv)
        ACT.done(nc.scalar.copy(km[0:HD, :, :], k_p[0:HD, :].rearrange("p (h s) -> p h s", h=MH)))
        ACT.done(nc.scalar.copy(flat(vm[:, :, :]), v_p))
        raw_q = ACT.done(nc.scalar.copy(qm[0:QKD, :, :], q_p[0:QKD, :].rearrange("p (h s) -> p h s", h=MH)))
        rr = slice(64, 96)
        PE.wait(raw_q)
        for n in range(2):
            nc.tensor.matmul(core.bank(4 + n)[0:QKD, :], con2(core, "rot", slice(0, QKD))[:, 0:QKD],
                             flat(qm[0:QKD, 2 * n:2 * n + 2, :]), start=True, stop=True)
        mr = PE.done(nc.tensor.matmul(core.bank(7)[rr, 0:S], con2(core, "rot", rr)[:, rr], kr[rr, 0, :],
                                      start=True, stop=True))
        DVE.wait(mr, raw_q)
        four = lambda a, rows: a.unsqueeze(1).to_broadcast([rows, MH, S])
        rq = core.tmp[0:QKD, 0:MH, :]
        m1 = DVE.done(nc.vector.tensor_tensor(rq, q_p[0:QKD, :].rearrange("p (h s) -> p h s", h=MH),
                                              four(con2(core, "sin", slice(0, QKD)), QKD), ALU.mult))
        m2 = DVE.done(nc.vector.tensor_tensor(qm[0:QKD, :, :], qm[0:QKD, :, :],
                                              four(con2(core, "cos", slice(0, QKD)), QKD), ALU.mult))
        m3 = DVE.done(nc.vector.tensor_tensor(kr[rr, 1, :], core.bank(7)[rr, 0:S], con2(core, "sin", rr), ALU.mult))
        m4 = DVE.done(nc.vector.tensor_tensor(kr[rr, 0, :], kr[rr, 0, :], con2(core, "cos", rr), ALU.mult))
        DVE.wait(m4)
        DVE.done(nc.vector.tensor_tensor(qm[0:QKD, :, :], qm[0:QKD, :, :], rq, ALU.add))
        for h in range(MH):
            mla = DVE.done(nc.vector.tensor_tensor(km[rr, h, :], kr[rr, 0, :], kr[rr, 1, :], ALU.add))
        PE.wait(fgm, mla)
        for t in range(2):
            ins = nc.tensor.transpose(core.bank(7)[0:XH_, t * P:t * P + P], fg[:, t * XH_:(t + 1) * XH_],
                                      core.ident())
        m = PE.done(ins)
        f, sc, cum, neg = (dec[:, i, :] for i in range(4))
        DVE.wait(m)
        m = DVE.done(nc.vector.tensor_scalar(f, core.bank(7)[0:XH_, 0:S], par2(core, "b_f", rows=XH_), None, ALU.add))
        ACT.wait(m)
        m = ACT.done(nc.scalar.activation(sc, f, FN.Abs))
        ACT.wait(m)
        m = ACT.done(nc.scalar.activation(sc, sc, FN.Exp, scale=-1.0))
        ACT.wait(m)
        m = ACT.done(nc.scalar.activation(sc, sc, FN.Ln, bias=1.0))
        DVE.wait(m)
        m = DVE.done(nc.vector.scalar_tensor_tensor(f, f, 0.0, sc, ALU.min, ALU.subtract))
        DVE.wait(m)
        m = DVE.done(nc.vector.tensor_tensor_scan(sc, core.one_row[:, :], f, 0.0, ALU.mult, ALU.add))
        DVE.wait(m)
        DVE.done(nc.vector.tensor_scalar(cum, sc, float(HD) ** 0.5, None, ALU.mult))
        m = DVE.done(nc.vector.tensor_scalar(neg, sc, -(float(HD) ** 0.5), None, ALU.mult))
        PE.wait(m, ACT.own.mark(), st.s_ev.mark(), mkv)
        for dst, src, c0, b0 in ((va, pa, 6, 0), (vf, pf, 6, 2)):
            for t in range(2):
                for c in range(3):
                    ins = nc.tensor.transpose(core.bank(b0 + t)[:, c * P:c * P + P],
                                              src[:, c0 + c, t * P:t * P + P], core.ident())
            mt = PE.done(ins)
            DVE.wait(mt)
            for t in range(2):
                vals = DVE.done(nc.vector.tensor_copy(dst[:, t, :], core.bank(b0 + t)[:, 0:3 * P]))
        core.prog.join()
        attend(core, inner, pa, pf, qm, km, va, vf, vm, cum, neg)
        core.prog.join()
        m = core.split_x(core.tmp[:, :, :], 0, ND, DVE.own.mark())
        m = branch2(core, io["w_o_2"], l, (m,))
        post(core, m, "mix_post", flat(pa[:, 0:ND, :]), pa)
        core.prog.join()


def attend(core, ctx, pa, pf, qm, km, va, vf, vm, cum, neg):
    nc, PE, ACT, DVE, POOL = core.nc, core.PE, core.ACT, core.DVE, core.POOL
    W = S + P
    sc = [core.sb(f"scores{i}", [P, 2, W], ctx=ctx) for i in range(2)]
    pt = core.sb("probs_t", [P, 2, W], ctx=ctx)
    st = [core.sb(f"softmax{i}", [P, 3, 4], ctx=ctx) for i in range(2)]
    pairs = ([("moba", c) for c in range(AH // 2)] + [("mla", c) for c in range(MH // 2)]
             + [("fox", c) for c in range(XH_ // 2)])
    done_sc, done_out = {}, {}

    def operands(kind, c, h):
        rows = slice(64 * h, 64 * h + 64)
        if kind == "mla":
            r = slice(0, QKD)
            return qm[r, 2 * c + h, :], km[r, 2 * c + h, :], lambda t: vm[:, t, (2 * c + h) * HD:(2 * c + h + 1) * HD]
        src, v = (pa, va) if kind == "moba" else (pf, vf)
        return src[rows, c, :], src[rows, 3 + c, :], lambda t: v[:, t, c * P + 64 * h:c * P + 64 * h + 64]

    def scores(n):
        kind, c = pairs[n]
        b = n % 2
        PE.wait(*done_sc.get(n - 2, ()))
        for h in range(2):
            q, k, _ = operands(kind, c, h)
            bank = core.bank(2 * b + h)
            for t, o, keys in ((1, 0, S), (0, S, P)):
                out = bank[:, o:o + keys]
                more = kind == "fox"
                ins = nc.tensor.matmul(out, q[:, t * P:t * P + P], k[:, 0:keys], start=True, stop=not more,
                                       skip_group_check=True)
                if more:
                    pick = core.ident(XH_)[:, 2 * c + h:2 * c + h + 1]
                    nc.tensor.matmul(out, cum[:, t * P:t * P + P], pick.to_broadcast([XH_, keys]), start=False,
                                     stop=False, skip_group_check=True)
                    ins = nc.tensor.matmul(out, pick.to_broadcast([XH_, P]), neg[:, 0:keys], start=False,
                                           stop=True, skip_group_check=True)
        mm = PE.done(ins)
        scale = float(QKD if kind == "mla" else HD) ** -0.5
        s, red = sc[b], st[b]
        DVE.wait(mm, *done_out.get(n - 2, ()))
        for h in range(2):
            bias = core.t5[:, 2 * c + h, :] if kind == "moba" else con2(core, "mask")
            m = DVE.done(nc.vector.scalar_tensor_tensor(s[:, h, :], core.bank(2 * b + h)[:, 0:W], scale, bias,
                                                        ALU.mult, ALU.add))
        DVE.wait(m)
        DVE.done(nc.vector.tensor_reduce(red[:, 0, 0:2], s[:, :, 0:S], AX_X, ALU.max))
        m = DVE.done(nc.vector.tensor_reduce(red[:, 0, 2:4], s[:, :, S:W], AX_X, ALU.max))
        DVE.wait(m)
        m = DVE.done(nc.vector.tensor_scalar(red[:, 0, :], red[:, 0, :], -1.0, None, ALU.mult))
        ACT.wait(m)
        for h in range(2):
            for t, o, keys in ((0, 0, S), (1, S, P)):
                a = 2 * t + h
                m = ACT.done(nc.scalar.activation(s[:, h, o:o + keys], s[:, h, o:o + keys], FN.Exp,
                                                  bias=red[:, 0, a:a + 1], accum_out=red[:, 1, a:a + 1]))
        DVE.wait(m)
        m = DVE.done(nc.vector.reciprocal(red[:, 2, :], red[:, 1, :]))
        DVE.wait(m)
        for h in range(2):
            for t, o, keys in ((0, 0, S), (1, S, P)):
                a = 2 * t + h
                m = DVE.done(nc.vector.tensor_scalar(s[:, h, o:o + keys], s[:, h, o:o + keys],
                                                     red[:, 2, a:a + 1], None, ALU.mult))
        done_sc[n] = (m,)

    def values(n):
        kind, c = pairs[n]
        b = n % 2
        s = sc[b]
        PE.wait(*done_sc[n], *done_out.get(n - 1, ()))
        for h in range(2):
            for i in range(3):
                ins = nc.tensor.transpose(core.bank(4 + h)[:, i * P:i * P + P], s[:, h, i * P:i * P + P],
                                          core.ident())
        mt = PE.done(ins)
        ACT.wait(mt)
        for h in range(2):
            m = ACT.done(nc.scalar.copy(pt[:, h, :], core.bank(4 + h)[:, 0:W]))
        PE.wait(m)
        out = core.bank(6 + b)
        for h in range(2):
            v = operands(kind, c, h)[2]
            rows = slice(64 * h, 64 * h + 64)
            for t in range(2):
                nc.tensor.matmul(out[rows, P:S], v(t), pt[:, h, t * P:t * P + P], start=(t == 0), stop=(t == 1),
                                 skip_group_check=True)
            ins = nc.tensor.matmul(out[rows, 0:P], v(0), pt[:, h, S:W], start=True, stop=True,
                                   skip_group_check=True)
        mm = PE.done(ins)
        DVE.wait(mm)
        m = DVE.done(nc.vector.tensor_copy(core.tmp[:, n, :], out[:, 0:S]))
        done_out[n] = (mm, m)

    for n in range(len(pairs) + 1):
        if n < len(pairs):
            scores(n)
        if n:
            values(n - 1)


def branch2(core, w, l, after):
    wl = w[bass.ds(l, 1)]
    for kc in range(ND):
        m = core.st.row_block(wl, kc * P, core.x(kc), kc == 0, kc == ND - 1, after if kc == 0 else ())
    return m


def post(core, after, gain, flat, y):
    nc, ACT, DVE = core.nc, core.ACT, core.DVE
    ACT.wait(after)
    m = ACT.done(nc.scalar.copy(flat, core.banks(4, 4)))
    rs, summed = core.inv_rms(y[:, 0:ND, :], ND, D, core.bank(0), core.rs[:, 0, :], (m, core.st.s_ev.mark()))
    DVE.wait(rs, m)
    for c in range(ND):
        m = DVE.done(nc.vector.scalar_tensor_tensor(y[:, c, :], y[:, c, :], par2(core, gain, c), core.rs[:, 0, :],
                                                    ALU.mult, ALU.mult))
    DVE.wait(m)
    return DVE.done(nc.vector.tensor_tensor(core.h[:, :, :], core.h[:, :, :], y[:, 0:ND, :], ALU.add))


def conv_chunks(core, pads):
    cw, cb = PAR2["cw"][0], PAR2["cb"][0]

    def stage(i, bank, mark, at, out):
        c = lambda j: i * 2 + (j + (NF if at else 0))
        conv_taps(core, bank, mark, KC2, lambda j, k: core.pv2[:, bass.ds(c(j) * KC2 + (cw + k), 1)],
                  lambda j: core.pv2[:, bass.ds(c(j) + cb, 1)], pads[:, at:at + 2, :],
                  out[:, :].rearrange("p (c s) -> p c s", c=2), (core.hid_free(), core.s_conv.mark()))
        yield
    return stage


def layer2(core, io, l):
    nc = core.nc
    for _ in range(AHEAD):
        core.st.split()
    core.ACT.wait(core.DVE.own.mark(), core.ACT.own.mark())
    core.s_par.inc(nc.scalar.dma_start(core.pv2[:, :], io["par2"][bass.ds(l, 1)].rearrange("o p n -> p (o n)")), 16)
    for e in (core.ACT, core.DVE):
        e.wait(core.s_par.mark())
    mixer2(core, io, l)
    with ExitStack() as inner:
        core.hid_buf = core.sb("hid3", [P, 512], ctx=inner)
        pads, core.up_buf = core.sb("pads2", [P, 4, 2 + S], ctx=inner), core.sb("conv_up", [P, 2 * S], ctx=inner)
        sums = core.sb("sums", [P, ND, S], ctx=inner)
        core.DVE.done(nc.vector.memset(pads[:, :, 0:2], 0.0))
        m = core.ffn(io["w_up_2"], io["w_down_2"], l, lambda c: par2(core, "ffn_pre", c),
                     conv=conv_chunks(core, pads), last=True)
        post(core, m, "ffn_post", sums[:, :, :].rearrange("p c s -> p (c s)"), sums)
        core.prog.join()
    core.st.skip_banks_to_start()
    core.st.skip_blocks()
    core.prog.join()


def first_constants():
    j, i = np.arange(P)[:, None], np.arange(P)[None, :]
    same = (j // DC) == (i // DC)
    masks = [j <= i, (j <= i) & same, (j < i) & same]
    for level in range(LEVELS):
        s = 1 << level
        masks.append((j // (2 * s) == i // (2 * s)) & (j % (2 * s) < s) & (i % (2 * s) >= s))
    return np.concatenate(masks, axis=1).astype(np.float32)


def columns(a):
    return np.asarray(a).reshape(a.shape[0], -1, P).transpose(0, 2, 1)


def rows(a):
    a = np.asarray(a)
    out = np.zeros((a.shape[0], P, 1), a.dtype)
    out[:, :a.shape[1], 0] = a
    return out


def taps(a):
    a = np.asarray(a)
    return a.reshape(a.shape[0], a.shape[1], -1, P).transpose(0, 3, 2, 1).reshape(a.shape[0], P, -1)


def first_params(v):
    return np.ascontiguousarray(np.concatenate([
        columns(v["ffn1_norm"]), columns(v["mix_norm"]), columns(v["ffn2_norm"]), taps(v["ssm_conv_w"]),
        columns(v["ssm_conv_b"]), columns(np.repeat(np.asarray(v["ssm_d"]), SP, axis=1)), columns(v["ssm_norm"]),
        taps(v["dn_conv_w"]), columns(v["dn_norm"]), rows(v["ssm_dt_bias"]), rows(v["ssm_a_log"]),
        rows(v["dn_dt_bias"]), rows(v["dn_a_log"])], axis=2))


def second_constants():
    q, k = np.arange(P)[:, None], np.arange(P)[None, :]
    own = np.where(k <= q, 0.0, NEG)
    mask = np.concatenate([np.zeros((P, P)), own, own], axis=1)
    half = ROPE // 2
    rot, cos, sin = np.zeros((P, P)), np.ones((P, S), np.float32), np.zeros((P, S), np.float32)
    i = np.arange(half)
    rot[64 + half + i, 64 + i], rot[64 + i, 64 + half + i] = -1.0, 1.0
    inv = np.float32(10000.0) ** (-i.astype(np.float32) / np.float32(half))
    ang = (np.arange(S, dtype=np.float32)[None, :] * inv[:, None]).astype(np.float32)
    cos[64:96], sin[64:96] = np.tile(np.cos(ang), (2, 1)), np.tile(np.sin(ang), (2, 1))
    return np.concatenate([mask, rot, cos, sin], axis=1).astype(np.float32)


def bucket_constants():
    n = np.maximum(S - 1 - np.arange(S + P), 0)
    far = 16 + (np.log(np.maximum(n, 1).astype(np.float32) / np.float32(16)) / np.float32(np.log(64.0))
                * np.float32(16)).astype(np.int32)
    bucket = np.where(n < 16, n, np.minimum(far, 31))
    onehot = np.arange(P)[:, None] == bucket[None, :]
    return np.concatenate([np.eye(P)[::-1], onehot], axis=1).astype(np.float32)


def second_params(v):
    return np.ascontiguousarray(np.concatenate([
        columns(v["ln_mix_pre_2"]), columns(v["ln_mix_post_2"]), columns(v["ln_ffn_pre_2"]),
        columns(v["ln_ffn_post_2"]), rows(v["b_f_2"]), columns(v["q_norm_2"]), columns(v["kv_norm_2"]),
        taps(v["conv_w_2"]), columns(v["conv_b_2"])], axis=2))


WEIGHTS = ("ffn1_w_in", "ffn1_w_out", "w_in", "ssm_w_branch", "dn_w_branch", "w_out", "ffn2_w_in", "ffn2_w_out",
           "w_in_2", "w_uq_2", "w_ukv_2", "w_o_2", "w_up_2", "w_down_2")


def program(nc, io, out, passes):
    with ExitStack() as ctx:
        k = Kernel(nc, ctx, passes)
        PE, ACT, DVE, POOL, SP = k.PE, k.ACT, k.DVE, k.POOL, k.SP
        token = k.tmp[:, :, :].rearrange("p c s -> p (c s)").rearrange("p (t d) -> p t d", t=2)
        k.one_row = k.sb("one_row", [XH_, S])
        ones = POOL.done(nc.gpsimd.memset(k.ones[:, :], 1.0))
        POOL.done(nc.gpsimd.memset(k.one_row[:, :], 1.0))
        POOL.done(nc.gpsimd.memset(k.eps[:, 0:1], EPS))
        POOL.done(nc.gpsimd.memset(k.eps[:, 1:2], -0.5 * float(np.log(DK))))
        k.s_par.inc(nc.sync.dma_start(token, io["x"].rearrange("o (t p) d -> p (o t) d", p=P)), 16)
        k.s_par.inc(nc.sync.dma_start(k.con0[:, :], io["con0"]), 16)
        for e in (PE, ACT, DVE, POOL):
            e.wait(k.s_par.mark(), POOL.own.mark())
        for c in range(ND):
            for t in range(2):
                ins = nc.tensor.transpose(k.banks(0, 4)[:, c * S + t * P:c * S + t * P + P],
                                          token[:, t, c * P:c * P + P], k.ident())
        turned = PE.done(ins)
        DVE.wait(turned)
        DVE.done(nc.vector.tensor_copy(k.h[:, :, :].rearrange("p c s -> p (c s)"), k.banks(0, 4)))
        k.prog.join()
        with ExitStack() as part:
            k.con1, k.pv, k.nega = (k.sb(n, s, ctx=part) for n, s in (
                ("con1", [P, NCON1]), ("pv", [P, NPAR1]), ("nega", [P, 2])))
            k.s_par = Sem(k.prog, "par1_landed")
            k.s_par.inc(nc.sync.dma_start(k.con1[:, :], io["con1"]), 16)
            for e in (ACT, DVE, POOL):
                e.wait(k.s_par.mark())
            with k.prog.loop(L) as l:
                layer1(k, io, l)
        rs, summed = k.inv_rms(k.h[:, :, :], ND, D, k.bank(7), k.rs[:, 0, :])
        DVE.wait(rs, summed)
        for c in range(ND):
            g = k.con0[:, CON0["final_norm"][0] + c:CON0["final_norm"][0] + c + 1]
            DVE.done(nc.vector.scalar_tensor_tensor(k.h[:, c, :], k.h[:, c, :], g, k.rs[:, 0, :], ALU.mult, ALU.mult))
        k.prog.join()
        with ExitStack() as part:
            k.con2, k.pv2, k.t5 = (k.sb(n, s, ctx=part) for n, s in (
                ("con2", [P, NCON2]), ("pv2", [P, NPAR2]), ("t5_bias", [P, AH, S + P])))
            SP.wait(*[s.mark() for s in k.prog.joined])
            k.s_par = Sem(k.prog, "par2_landed")
            k.s_par.inc(nc.sync.dma_start(k.con2[:, :], io["con2"]), 16)
            moba_bias(k, io)
            for e in (PE, ACT, DVE, POOL):
                e.wait(k.s_par.mark())
            with k.prog.loop(L) as l:
                layer2(k, io, l)
        PE.wait(DVE.own.mark())
        for t in range(2):
            for c in range(ND):
                ins = nc.tensor.transpose(k.banks(0, 4)[:, t * D + c * P:t * D + c * P + P],
                                          k.h[:, c, t * P:t * P + P], k.ident())
        turned = PE.done(ins)
        DVE.wait(turned)
        m = DVE.done(nc.vector.tensor_copy(token.rearrange("p t d -> p (t d)"), k.banks(0, 4)))
        SP.wait(m)
        s_out = Sem(k.prog, "out_stored")
        s_out.inc(nc.sync.dma_start(out.rearrange("o (t p) d -> p (o t) d", p=P), token), 16)
        SP.wait(s_out.mark())


def kernel(**inputs):
    import concourse.bacc as bacc
    from concourse.bass_utils import run_bass_kernel_spmd as run

    v = {n: np.asarray(a) for n, a in inputs.items()}
    arrays = {n: np.ascontiguousarray(v[n]) for n in WEIGHTS}
    arrays["x"] = np.ascontiguousarray(v["x"])
    arrays["rel_bias"] = np.ascontiguousarray(v["rel_bias_2"])
    arrays["par1"], arrays["par2"] = first_params(v), second_params(v)
    arrays["con0"] = np.ascontiguousarray(np.concatenate(
        [np.eye(P, dtype=np.float32), v["final_norm"].reshape(ND, P).T], axis=1))
    arrays["con1"], arrays["con2"], arrays["con_t5"] = first_constants(), second_constants(), bucket_constants()
    passes = {}
    for _ in range(2):
        nc = bacc.Bacc("TRN2", target_bir_lowering=False, num_devices=1, dynamic_dma_scratch_size=1024)
        io = {n: nc.dram_tensor("in_" + n, a.shape, F32, kind="ExternalInput").ap() for n, a in arrays.items()}
        io["scratch"] = nc.dram_tensor("bias_scratch", [AH, S + P], F32).ap()
        out = nc.dram_tensor("out", [1, S, D], F32, kind="ExternalOutput").ap()
        program(nc, io, out, passes)
    r = run(nc, [{"in_" + n: a for n, a in arrays.items()}], core_ids=[0])
    return r.results[0]["out"]
```

```python
from contextlib import ExitStack, contextmanager

import numpy as np
import concourse.bass as bass
from concourse import mybir

F32 = mybir.dt.float32
F32R = mybir.dt.float32r
ALU = mybir.AluOpType
FN = mybir.ActivationFunctionType
AX_X = mybir.AxisListType.X

P = 128
S = 256
D = 1024
ND = D // P
L = 2
FF = 2816
NF = FF // P
EPS = 1e-6
NEG = -1e30
SI, SG, SH, SP, SN = 2048, 4, 32, 64, 128
HG = SH // SG
SCONV = SI + 2 * SG * SN
DH, DK = 8, 128
DC = 64
DCONV = 3 * DH * DK
COL_Z, COL_XBC = 0, SI
COL_DT = COL_XBC + SCONV
COL_QKV = COL_DT + SH
COL_ZD = COL_QKV + DCONV
COL_B = COL_ZD + DH * DK
COL_A = COL_B + DH
COL_GS = COL_A + DH
COL_GD = COL_GS + D
AH, MH, XH_, HD = 6, 4, 6, 64
QR, KVR, ROPE = 256, 128, 32
QKD = 96
COL2_KR = 3 * AH * HD + QR + KVR
COL2_F = COL2_KR + ROPE
COL2_FG = COL2_F + 3 * XH_ * HD
KC2 = 3

def table(widths):
    at, out = 0, {}
    for name, n in widths:
        out[name] = (at, n)
        at += n
    return out, at


PAR1, NPAR1 = table([("ffn1_norm", ND), ("mix_norm", ND), ("ffn2_norm", ND), ("ssm_cw", 4 * SCONV // P),
                     ("ssm_cb", SCONV // P), ("ssm_d", SI // P), ("ssm_norm", SI // P),
                     ("dn_cw", 4 * DCONV // P), ("dn_norm", 1), ("ssm_dtb", 1), ("ssm_alog", 1),
                     ("dn_dtb", 1), ("dn_alog", 1)])
PAR2, NPAR2 = table([("mix_pre", ND), ("mix_post", ND), ("ffn_pre", ND), ("ffn_post", ND), ("b_f", 1),
                     ("q_norm", QR // P), ("kv_norm", 1), ("cw", KC2 * 2 * NF), ("cb", 2 * NF)])
CON0, NCON0 = table([("ident", P), ("final_norm", ND)])
LEVELS = 6
CON1, NCON1 = table([("causal", P), ("incl", P), ("strict", P), ("level", LEVELS * P)])
CON2, NCON2 = table([("mask", S + P), ("rot", P), ("cos", S), ("sin", S)])
CONT, NCONT = table([("flip", P), ("bucket", S + P)])


class Count:

    def __init__(self, const=0, terms=()):
        self.const, self.terms = const, tuple(t for t in terms if t[2])

    def __add__(self, n):
        return Count(self.const + n, self.terms)

    def value(self):
        v = self.const
        for _, reg, k in self.terms:
            v = reg * k + v
        return v


class Sem:

    def __init__(self, prog, name, virtual=False):
        self.sem = None if virtual else prog.ctx.enter_context(prog.nc.semaphore(name))
        self.name, self.count = name, Count()
        prog.sems.append(self)

    def inc(self, ins, n=1):
        ins.then_inc(self.sem, n)
        return self.later(n)

    def later(self, n):
        self.count = self.count + n
        return (self, self.count)

    def mark(self, ago=0):
        return (self, self.count + (-ago))


class Engine:

    def __init__(self, prog, eng, name):
        self.eng, self.own = eng, Sem(prog, "done_" + name)
        self.idle = Sem(prog, "idle_" + name)
        prog.engines.append(self)

    def done(self, ins):
        return self.own.inc(ins)

    def wait(self, *marks):
        for sem, count in marks:
            self.eng.wait_ge(sem.sem, count.value())


    def settle(self):
        self.eng.sem_inc(self.idle.sem, 1)


class Program:
    def __init__(self, nc, ctx, passes):
        self.nc, self.ctx, self.passes = nc, ctx, passes
        self.sems, self.engines, self.loops, self.joined = [], [], 0, []
        self.PE = Engine(self, nc.tensor, "pe")
        self.ACT = Engine(self, nc.scalar, "act")
        self.DVE = Engine(self, nc.vector, "dve")
        self.POOL = Engine(self, nc.gpsimd, "pool")
        self.SP = Engine(self, nc.sync, "sp")

    @contextmanager
    def loop(self, trips):
        me = self.loops
        self.loops += 1
        start = [s.count for s in self.sems]
        step = self.passes.get(me, [0] * len(start))
        at = self.ring_places()
        for e in self.engines:
            e.settle()
        with self.nc.Fori(0, trips) as i:
            for s, c, k in zip(self.sems, start, step):
                s.count = Count(c.const, c.terms + ((me, i, k),))
            yield i
            took = [s.count.const - c.const for s, c in zip(self.sems, start)]
            self.passes[me] = took
            assert at == self.ring_places(), "a pass must leave every ring where it found it"
        for s, c, k in zip(self.sems, start, took):
            s.count = Count(c.const + k * trips, c.terms)

    def join(self):
        marks = [s.mark() for s in self.joined]
        for e in (self.PE, self.ACT, self.DVE, self.POOL):
            e.wait(*marks)


RAW, SPL, OUTB = 4, 4, 4
AHEAD = 2
BLK = 1024


class Stream:

    def __init__(self, k):
        pr = self.prog = k.prog
        self.k = k
        self.raw = [k.sb(f"raw{i}", [P, BLK]) for i in range(RAW)]
        self.hi = [k.sb(f"w_hi{i}", [P, BLK], F32R) for i in range(SPL)]
        self.lo = [k.sb(f"w_lo{i}", [P, BLK], F32R) for i in range(SPL)]
        self.s_raw = [Sem(pr, f"raw{i}_landed") for i in range(RAW)]
        self.s_hi, self.s_mm, self.s_ev = (Sem(pr, n) for n in ("w_hi", "w_mm", "out_read"))
        self.s_lo = [Sem(pr, f"w_lo_{n}") for n in ("even", "odd")]
        self.want = [Sem(pr, f"raw{i}_wanted", True) for i in range(RAW)]
        self.loads = [Sem(pr, f"loads{i}", True) for i in range(2)]
        self.load_at = self.split_at = self.mm_at = self.out_at = 0
        self.put_off = []
        pr.ring_places = lambda: (self.load_at, self.split_at, self.mm_at, self.out_at)
        self.outs = Sem(pr, "outs", True)
        for sem, n in ((self.s_lo[0], RAW // 2), (self.s_lo[1], RAW // 2), (self.s_mm, SPL), (self.s_ev, OUTB)):
            pr.nc.gpsimd.sem_inc(sem.sem, n)
            sem.later(n)

    def load(self, parts):
        pr, s = self.prog, self.load_at
        pr.SP.wait((self.s_lo[s % 2], self.loads[s % 2].count + 1))
        pr.SP.settle()
        for view, src in parts:
            self.s_raw[s].inc(pr.nc.sync.dma_start(view(self.raw[s]), src), 16)
        self.loads[s % 2].later(1)
        self.load_at = (s + 1) % RAW

    def split(self):
        pr, s, b = self.prog, self.split_at, self.split_at % SPL
        self.want[s].later(32)
        pr.ACT.wait((self.s_raw[s], self.want[s].count), (self.s_mm, self.s_hi.count + 1))
        self.s_hi.inc(pr.nc.scalar.copy(self.hi[b][:, :], self.raw[s][:, :]))
        e = (pr.POOL, pr.DVE)[s % 2]
        e.wait(self.s_hi.mark())
        self.s_lo[s % 2].inc(e.eng.tensor_tensor(self.lo[b][:, :], self.raw[s][:, :],
                                                 self.hi[b][:, :].bitcast(F32), ALU.subtract))
        self.split_at = (s + 1) % RAW

    def block(self, parts, emit, after=(), ahead=True):
        pr, b = self.prog, self.mm_at
        odd = self.load_at % 2
        self.load(parts)
        made = (self.s_lo[odd], self.loads[odd].count + RAW // 2)
        if ahead:
            self.split()
        self.flush()
        pr.PE.wait(made, *after)
        self.s_mm.inc(emit(self.hi[b], self.lo[b]))
        self.mm_at = (b + 1) % SPL
        return self.s_mm.mark()

    def flush(self):
        put_off, self.put_off = self.put_off, []
        for stages in put_off:
            for _ in stages:
                self.put_off.append(stages)
                break

    def drain(self):
        while self.put_off:
            self.flush()

    def unit_parts(self, w, col, half, cols=None):
        rows = lambda a: w[:, half * 512 + a * 256:half * 512 + a * 256 + 256, :]
        if cols is None:
            return [((lambda r, a=a: r[:, a * 512:a * 512 + 512].rearrange("p (c n) -> p c n", c=2)),
                     rows(a)[:, :, bass.ds(col, 256)].rearrange("o (c p) n -> p (o c) n", p=P)) for a in range(2)]
        whole = w[:, half * 512:half * 512 + 512, :]
        return [((lambda r, a=a: r[:, :].rearrange("p (c n) -> p c n", c=4)[:, :, a * P:a * P + P]),
                 whole[:, :, cols[a]:cols[a] + P].rearrange("o (c p) n -> p (o c) n", p=P)) for a in range(2)]

    def unit(self, w, col, x, after=(), cols=None, extra=None):
        pr, nc = self.prog, self.prog.nc
        bank = self.k.bank(self.out_at)
        free = (self.s_ev, self.ev_due() + 1)
        for half in range(2):
            def emit(hi, lo, half=half):
                for t in range(2):
                    for c in range(4):
                        kc = 4 * half + c
                        wh = hi[:, c * 256 + t * P:c * 256 + t * P + P]
                        wl = lo[:, c * 256 + t * P:c * 256 + t * P + P]
                        out = bank[:, t * S:t * S + S]
                        xh, xl = x[0][:, kc, :], x[1][:, kc, :]
                        for n, (a, b) in enumerate(((wh, xh), (wh, xl), (wl, xh))):
                            ins = nc.tensor.matmul(out, a, b, start=(kc == 0 and t == 0 and n == 0),
                                                   stop=(kc == 7 and n == 2), skip_group_check=True)
                return extra(half, hi, lo, x) if extra else ins
            mark = self.block(self.unit_parts(w, col, half, cols), emit, (*(after[half] if after else ()), free))
        self.out_at = (self.out_at + 1) % OUTB
        self.outs.later(1)
        return bank, mark

    def row_block(self, w, row, x, first, final, after=(), ahead=True):
        nc, k = self.prog.nc, self.k

        def emit(hi, lo):
            for t in range(8):
                out = k.bank(4 + t // 2)[:, (t % 2) * S:(t % 2) * S + S]
                wh, wl = hi[:, t * P:t * P + P], lo[:, t * P:t * P + P]
                for n, (a, b) in enumerate(((wh, x[0]), (wh, x[1]), (wl, x[0]))):
                    ins = nc.tensor.matmul(out, a, b, start=(first and t % 2 == 0 and n == 0),
                                           stop=(final and n == 2), skip_group_check=True)
            return ins
        src = w[:, bass.ds(row, P), :].rearrange("o p n -> p (o n)")
        parts = [((lambda r, a=a: r[:, a * 512:a * 512 + 512]), src[:, a * 512:a * 512 + 512]) for a in range(2)]
        return self.block(parts, emit, after, ahead)

    def skip_banks_to_start(self):
        n = -self.out_at % OUTB
        if n:
            self.prog.POOL.settle()
            self.s_ev.inc(self.prog.nc.gpsimd.memset(self.k.tick[:, 4:5], 0.0), n)
            self.outs.later(n)
            self.out_at = 0

    def skip_blocks(self):
        pr, n = self.prog, -self.load_at % RAW
        if n:
            pr.POOL.settle()
            odd = [(i + self.load_at) % 2 for i in range(n)].count(1)
            for i, (s, by) in enumerate(((self.s_hi, n), (self.s_mm, n), (self.s_lo[0], n - odd), (self.s_lo[1], odd))):
                if by:
                    s.inc(pr.nc.gpsimd.memset(self.k.tick[:, i:i + 1], 0.0), by)
            for i, by in enumerate((n - odd, odd)):
                self.loads[i].later(by)
            self.load_at = self.split_at = 0
            self.mm_at = (self.mm_at + n) % SPL

    def latest(self):
        return self.k.bank((self.out_at - 1) % OUTB), self.s_mm.mark()

    def ev_due(self):
        return self.outs.count


class Kernel:
    def __init__(self, nc, ctx, passes):
        self.nc, self.ctx = nc, ctx
        self.prog = Program(nc, ctx, passes)
        self.PE, self.ACT, self.DVE, self.POOL, self.SP = (
            self.prog.PE, self.prog.ACT, self.prog.DVE, self.prog.POOL, self.prog.SP)
        self.psum = ctx.enter_context(nc.psum_tensor("psum", [P, 8, 512], F32))
        self.h = self.sb("h", [P, ND, S])
        self.xh = self.sb("x_hi", [P, 32, S], F32R)
        self.xl = self.sb("x_lo", [P, 32, S], F32R)
        self.tmp = self.sb("tmp", [P, ND, S])
        self.rs = self.sb("rs", [P, 2, S])
        self.ones = self.sb("ones", [P, P])
        self.eps = self.sb("eps", [P, 2])
        self.act_buf = self.sb("act", [P, 2 * S])
        self.tick = self.sb("tick", [P, 5])
        self.con0 = self.sb("con0", [P, NCON0])
        self.s_par = Sem(self.prog, "params_landed")
        self.st = Stream(self)
        self.s_hid = Sem(self.prog, "hidden_split")
        self.s_conv = Sem(self.prog, "conv_done")
        for sem in [e.own for e in self.prog.engines] + [self.s_hid, self.s_conv]:
            nc.gpsimd.sem_inc(sem.sem, 1)
            sem.later(1)
        self.prog.joined = [e.own for e in (self.PE, self.ACT, self.DVE, self.POOL)] + [
            self.s_hid, self.s_conv, self.st.s_hi, *self.st.s_lo, self.st.s_mm, self.st.s_ev]

    def sb(self, name, shape, dt=F32, ctx=None):
        return (ctx or self.ctx).enter_context(self.nc.sbuf_tensor(name, shape, dt))

    def bank(self, i):
        return self.psum[:, i, :]

    def banks(self, i, n):
        return self.psum[:, i:i + n, :].rearrange("p b n -> p (b n)")

    def ident(self, n=P):
        return self.con0[0:n, 0:n]

    def inv_rms(self, src, chunks, width, bank, out, after=(), each=None):
        nc, n = self.nc, min(2, chunks)
        self.ACT.wait(*after)
        self.PE.wait(*after)
        total = None
        for c in range(0, chunks, n):
            if each:
                self.ACT.wait(each[c // 2])
            sq = self.ACT.done(nc.scalar.activation(self.tmp[:, c:c + n, :], src[:, c:c + n, :], FN.Square))
            if total is not None:
                self.DVE.wait(sq, total)
                total = self.DVE.done(nc.vector.tensor_tensor(self.tmp[:, 0:n, :], self.tmp[:, 0:n, :],
                                                              self.tmp[:, c:c + n, :], ALU.add))
            else:
                total = sq
        self.PE.wait(total)
        for j in range(n):
            ins = nc.tensor.matmul(bank[:, 0:S], self.ones[:, :], self.tmp[:, j, :], start=(j == 0), stop=(j == n - 1))
        summed = self.PE.done(ins)
        return self.inv_sqrt(bank[:, 0:S], out, width, summed), summed

    def inv_sqrt(self, src, out, width, after, scale=None):
        return self.exp_half(out, self.ln_mean(src, out, width, after), scale)

    def ln_mean(self, src, out, width, after):
        self.ACT.wait(after)
        return self.ACT.done(self.nc.scalar.activation(out, src, FN.Ln, scale=1.0 / width, bias=self.eps[:, 0:1]))

    def exp_half(self, out, after, scale=None):
        nc = self.nc
        self.ACT.wait(after)
        if scale is None:
            return self.ACT.done(nc.scalar.activation(out, out, FN.Exp, scale=-0.5))
        return self.ACT.done(nc.scalar.activation(out, out, FN.Exp, scale=-0.5, bias=scale))

    def norm_split(self, src, gain, chunks, width, dst, after=(), each=None):
        nc = self.nc
        rs, summed = self.inv_rms(src, chunks, width, self.bank(7), self.rs[:, 0, :], after, each)
        self.DVE.wait(rs, summed)
        los, before = [], None
        for a in range(0, chunks, 2):
            n = min(2, chunks - a)
            for c in range(a, a + n):
                m = self.DVE.done(nc.vector.scalar_tensor_tensor(self.tmp[:, c, :], src[:, c, :], gain(c),
                                                                 self.rs[:, 0, :], ALU.mult, ALU.mult))
            self.ACT.wait(m)
            hi = self.ACT.done(nc.scalar.copy(self.xh[:, dst + a:dst + a + n, :], self.tmp[:, a:a + n, :]))
            if before:
                los.append(self.lo_part(dst, *before))
            before = (a, n, hi)
        los.append(self.lo_part(dst, *before))
        return (los[(len(los) - 1) // 2],), (los[-1],)

    def lo_part(self, dst, a, n, hi):
        self.DVE.wait(hi)
        return self.DVE.done(self.nc.vector.tensor_tensor(
            self.xl[:, dst + a:dst + a + n, :], self.tmp[:, a:a + n, :],
            self.xh[:, dst + a:dst + a + n, :].bitcast(F32), ALU.subtract))

    def split_x(self, src, dst, chunks, after):
        nc = self.nc
        self.ACT.wait(after)
        hi = self.ACT.done(nc.scalar.copy(self.xh[:, dst:dst + chunks, :], src))
        self.DVE.wait(hi, after)
        return self.DVE.done(nc.vector.tensor_tensor(self.xl[:, dst:dst + chunks, :], src,
                                                     self.xh[:, dst:dst + chunks, :].bitcast(F32), ALU.subtract))

    def split_pairs(self, src, dst, chunks, each):
        return [self.split_x(src[:, 2 * p:2 * p + 2, :], dst + 2 * p, 2, each[p]) for p in range(chunks // 2)]

    def x(self, a, n=None):
        return (self.xh[:, a:a + n, :], self.xl[:, a:a + n, :]) if n else (self.xh[:, a, :], self.xl[:, a, :])

    def down(self, w, l, after, last):
        row = lambda kc: (self.xh[:, bass.ds(8 + kc, 1), :].rearrange("p o s -> p (o s)"),
                          self.xl[:, bass.ds(8 + kc, 1), :].rearrange("p o s -> p (o s)"))
        wl = w[bass.ds(l, 1)]
        for kc in range(2):
            self.st.row_block(wl, kc * P, row(kc), kc == 0, False, after)
        self.st.drain()
        with self.prog.loop((NF - 6) // 4) as i:
            for j in range(4):
                self.st.row_block(wl, i * (4 * P) + (2 + j) * P, row(i * 4 + (2 + j)), False, False)
        for kc in range(NF - 4, NF):
            m = self.st.row_block(wl, kc * P, row(kc), False, kc == NF - 1,
                                  (self.s_hid.mark(),) if kc == NF - 2 else (),
                                  ahead=not (last and kc >= NF - AHEAD))
        return m

    def ffn(self, w_in, w_out, l, gain, conv=None, last=False, each=None):
        nc, st = self.nc, self.st
        ready = self.norm_split(self.h[:, :, :], gain, ND, D, 0, each=each)
        act = self.act_buf
        hid = self.hid_buf
        wl = w_in[bass.ds(l, 1)]
        x = self.x(0, ND)

        def pair(i, after=()):
            g, gm = st.unit(wl, i * 256, x, after)
            st.put_off.append(gate_chunks(i, g, gm))
            u, um = st.unit(wl, i * 256 + FF, x)
            st.put_off.append(value_chunks(i, u, um))

        def gate_chunks(i, g, gm):
            if conv:
                yield from conv(i, g, gm, 0, act)
                self.ACT.wait(self.DVE.own.mark(), self.s_conv.mark())
                self.ACT.done(nc.scalar.activation(act[:, :], act[:, :], FN.Gelu_apprx_tanh))
            else:
                self.ACT.wait(gm, self.hid_free())
                st.s_ev.inc(nc.scalar.activation(act[:, :], g, FN.Silu))
            yield

        def value_chunks(i, u, um):
            if conv:
                yield from conv(i, u, um, 2, self.up_buf)
                self.DVE.wait(self.ACT.own.mark(), self.DVE.own.mark(), self.s_conv.mark(), self.hid_free())
                f = self.DVE.done(nc.vector.tensor_tensor(hid[:, :], act[:, :], self.up_buf[:, :], ALU.mult))
            else:
                self.DVE.wait(st.s_ev.mark(), um, self.hid_free())
                f = st.s_ev.inc(nc.vector.tensor_tensor(hid[:, :], act[:, :], u, ALU.mult))
            c = bass.ds(i * 2 + 8, 2)
            out_h = self.xh[:, c, :].rearrange("p c s -> p (c s)")
            out_l = self.xl[:, c, :].rearrange("p c s -> p (c s)")
            self.ACT.wait(f)
            hi = self.ACT.done(nc.scalar.copy(out_h, hid[:, :]))
            self.DVE.wait(hi, f)
            self.s_hid.inc(nc.vector.tensor_tensor(out_l, hid[:, :], out_h.bitcast(F32), ALU.subtract))

        pair(0, ready)
        st.put_off = []
        with self.prog.loop((NF // 2 - 1) // 2) as i:
            st.put_off = [value_chunks(i * 2, *st.latest())]
            pair(i * 2 + 1)
            pair(i * 2 + 2)
            st.put_off = []
        st.put_off = [value_chunks(NF // 2 - 1, *st.latest())]
        return self.down(w_out, l, (self.s_hid.mark(),), last)

    def hid_free(self):
        return self.s_hid.mark()

    def add_sum(self, scale, after):
        nc, each = self.nc, []
        self.prog.join()
        self.DVE.wait(after)
        for b in range(4):
            hb = self.h[:, 2 * b:2 * b + 2, :].rearrange("p c s -> p (c s)")
            each.append(self.DVE.done(nc.vector.scalar_tensor_tensor(hb, self.bank(4 + b), scale, hb,
                                                                     ALU.mult, ALU.add)))
        return each


def par1(core, name, i=0, n=1, rows=P):
    a, width = PAR1[name]
    assert i + n <= width
    return core.pv[0:rows, a + i:a + i + n]


def con1(core, name, i=0, n=P):
    a = CON1[name][0]
    return core.con1[:, a + i:a + i + n]


def wide(core, mask, n):
    return mask.unsqueeze(1).to_broadcast([P, n, P])

def conv_taps(core, bank, mark, taps, weight, bias, pad, acc, free):
    nc, ACT, DVE = core.nc, core.ACT, core.DVE
    two = bank.rearrange("p (c s) -> p c s", c=2)
    ACT.wait(mark, *free)
    padded = ACT.done(nc.scalar.copy(pad[:, :, taps - 1:taps - 1 + S], two))
    for j in range(2):
        ins = nc.scalar.activation(acc[:, j, :], two[:, j, :], FN.Identity, scale=weight(j, taps - 1),
                                   bias=bias(j) if bias else 0.0)
        m = ACT.done(ins) if j == 0 else core.st.s_ev.inc(ins)
    DVE.wait(padded, m)
    before = (), ()
    for k in range(taps - 1):
        now = []
        for j in range(2):
            DVE.wait(*before[j])
            ins = nc.vector.scalar_tensor_tensor(acc[:, j, :], pad[:, j, k:k + S], weight(j, k), acc[:, j, :],
                                                 ALU.mult, ALU.add)
            now.append(((DVE.done(ins) if (j, k) != (1, taps - 2) else core.s_conv.inc(ins)),))
        before = now
    return now[0][0], now[1][0]


def conv_unit(core, bank, mark, c, taps, weight, bias, dst):
    acc = core.act_buf[:, :].rearrange("p (c s) -> p c s", c=2)
    free = core.s_conv.mark(), core.ACT.own.mark()
    summed = conv_taps(core, bank, mark, taps, lambda j, k: weight(c, j, k),
                       (lambda j: bias(c, j)) if bias else None, core.pad_buf, acc, free)
    yield
    core.ACT.wait(*summed)
    core.ACT.done(core.nc.scalar.activation(dst[:, bass.ds(c, 2), :], acc, FN.Silu))


def project(core, w, col, units, x, use, peel=4):
    st = core.st
    assert (units - peel) % 4 == 0

    def unit(u, at):
        bank, mark = st.unit(w, at, x)
        st.put_off.append(use(u, bank, mark))
    for u in range(peel):
        unit(u, col + u * 256)
    if units > peel:
        st.put_off = []
        with core.prog.loop((units - peel) // 4) as i:
            st.put_off = [use(i * 4 + (peel - 1), *st.latest())]
            for j in range(4):
                unit(i * 4 + (peel + j), i * 1024 + (col + (peel + j) * 256))
            st.put_off = []
        st.put_off = [use(units - 1, *st.latest())]


def act_unit(core, func, dst):
    def use(u, bank, mark):
        core.ACT.wait(mark)
        core.st.s_ev.inc(core.nc.scalar.activation(
            dst[:, bass.ds(u * 2, 2), :].rearrange("p c s -> p (c s)"), bank, func))
        yield
    return use


def softplus(core, x, scratch, rows, after):
    nc = core.nc
    core.ACT.wait(after)
    m = core.ACT.done(nc.scalar.activation(scratch, x, FN.Abs))
    core.ACT.wait(m)
    m = core.ACT.done(nc.scalar.activation(scratch, scratch, FN.Exp, scale=-1.0))
    core.ACT.wait(m)
    m = core.ACT.done(nc.scalar.activation(scratch, scratch, FN.Ln, bias=1.0))
    yield
    core.DVE.wait(m, after)
    return core.DVE.done(nc.vector.scalar_tensor_tensor(x, x, 0.0, scratch, ALU.max, ALU.add))


def spread_row(core, out, src, row, rows, after):
    core.PE.wait(*after)
    return core.nc.tensor.matmul(out, core.ident(rows)[:, row:row + 1].to_broadcast([rows, P]), src,
                                 start=True, stop=True, skip_group_check=True)


def small_params(core, bank, mark, ready):
    nc, PE, ACT, DVE = core.nc, core.PE, core.ACT, core.DVE
    raw, raw_a = core.hd_raw[:, 0:2 * S], core.hd_raw[0:DH, 2 * S:3 * S]
    ACT.wait(mark)
    ACT.done(nc.scalar.copy(raw_a, core.bank(7)[0:DH, 0:S]))
    mark = core.st.s_ev.inc(nc.scalar.copy(raw, bank[0:SH, :]))
    own = ACT.own.mark()
    yield
    DVE.wait(mark, own)
    hs, hd = core.hs, core.hd
    dt, la, ac, te, sc = (hs[:, i, :] for i in range(5))
    beta, g, eg, bg, ed, scd = (hd[:, i, :] for i in range(6))
    m1 = DVE.done(nc.vector.tensor_scalar(dt, raw[:, 0:S], par1(core, "ssm_dtb", rows=SH), None, ALU.add))
    m1 = yield from softplus(core, dt, sc, SH, m1)
    na = ACT.done(nc.scalar.activation(core.nega[0:SH, 0:1], par1(core, "ssm_alog", rows=SH), FN.Exp))
    nd = ACT.done(nc.scalar.activation(core.nega[0:DH, 1:2], par1(core, "dn_alog", rows=DH), FN.Exp))
    DVE.wait(na, nd, m1)
    m = DVE.done(nc.vector.tensor_scalar(la, dt, core.nega[0:SH, 0:1], -1.0, ALU.mult, ALU.mult))
    DVE.wait(m)
    for t in range(2):
        c = slice(t * P, t * P + P)
        m = DVE.done(nc.vector.tensor_tensor_scan(ac[:, c], core.ones[0:SH, :], la[:, c], 0.0, ALU.mult, ALU.add))
    yield
    ACT.wait(m)
    for t in range(2):
        c = slice(t * P, t * P + P)
        m = ACT.done(nc.scalar.activation(te[:, c], ac[:, c], FN.Exp, scale=-1.0,
                                          bias=ac[:, t * P + P - 1:t * P + P]))
    ssm = m
    bank_b, bank_a = raw[0:DH, S:2 * S], raw_a
    ACT.wait(mark, m1)
    mb = ACT.done(nc.scalar.activation(beta, bank_b, FN.Sigmoid))
    DVE.wait(mark)
    m = DVE.done(nc.vector.tensor_scalar(g, bank_a, par1(core, "dn_dtb", rows=DH), None, ALU.add))
    m = yield from softplus(core, g, scd, DH, m)
    DVE.wait(m)
    m = DVE.done(nc.vector.tensor_scalar(scd, g, core.nega[0:DH, 1:2], -1.0, ALU.mult, ALU.mult))
    DVE.wait(m)
    for c in range(S // DC):
        s = slice(c * DC, c * DC + DC)
        m = DVE.done(nc.vector.tensor_tensor_scan(g[:, s], core.ones[0:DH, 0:DC], scd[:, s], 0.0,
                                                  ALU.mult, ALU.add))
    yield
    ACT.wait(m)
    for c in range(S // DC):
        s = slice(c * DC, c * DC + DC)
        ACT.done(nc.scalar.activation(ed[:, s], g[:, s], FN.Exp, scale=-1.0,
                                      bias=g[:, c * DC + DC - 1:c * DC + DC]))
    me = ACT.done(nc.scalar.activation(eg, g, FN.Exp))
    DVE.wait(me, mb)
    m = DVE.done(nc.vector.tensor_tensor(bg, beta, eg, ALU.mult))
    yield
    PE.wait(m, ssm, me)
    PE.settle()
    out = core.bank(6)
    for n, a in enumerate((dt, ac, te)):
        for t in range(2):
            nc.tensor.transpose(out[:, (2 * n + t) * SH:(2 * n + t + 1) * SH], a[:, t * P:t * P + P],
                                core.ident(SH))
    for n, a in enumerate((g, beta, bg, ed)):
        for t in range(2):
            at = 6 * SH + (2 * n + t) * DH
            ins = nc.tensor.transpose(out[:, at:at + DH], a[:, t * P:t * P + P], core.ident(DH))
    m = PE.done(ins)
    yield
    DVE.wait(m)
    ready.append(DVE.done(nc.vector.tensor_copy(core.cols[:, :], out[:, 0:6 * SH + 8 * DH])))


def scol(core, what, t, h, n=1):
    at = (2 * ("dt", "ac", "te").index(what) + t) * SH + h
    return core.cols[:, at:at + n]


def dcol(core, what, t, h, n=1):
    at = 6 * SH + (2 * ("g", "beta", "bg", "ed").index(what) + t) * DH + h
    return core.cols[:, at:at + n]

def side_by_side(*chains):
    chains = list(chains)
    while chains:
        for chain in list(chains):
            for _ in chain:
                break
            else:
                chains.remove(chain)



def delta(core, cols_ready):
    def heads(side):
        for h0 in range(2 * side, DH, 4):
            yield from delta_heads(core, h0, side, cols_ready)
    side_by_side(heads(0), heads(1))


def delta_heads(core, h0, side, cols_ready):
    nc, PE, ACT, DVE, POOL = core.nc, core.PE, core.ACT, core.DVE, core.POOL
    W = 2 * S
    d = {name: a[:, side * W:side * W + W] for name, a in core.dn.items() if name != "state"}
    state = core.dn["state"][:, side * S:side * S + S]
    work = core.tmp[:, 4 * side:4 * side + 4, :]
    low, high = (work[:, 2 * i:2 * i + 2, :].rearrange("p c s -> p (c s)") for i in range(2))
    T, U, un, wt = low, high, d["dec"], low
    bank = lambda i: core.bank(4 * side + i)
    tile = lambda i: slice(i * P, i * P + P)
    four = lambda a: a.rearrange("p (n j) -> p n j", n=4)
    qkv = core.qkv
    q, k, v = (lambda h, n=n: qkv[:, n * DH + h0 + h, :] for n in range(3))
    two = lambda n: qkv[:, n * DH + h0:n * DH + h0 + 2, :]
    flat = lambda a: a.rearrange("p c s -> p (c s)")
    prior = (PE.own.mark(), ACT.own.mark(), DVE.own.mark(), POOL.own.mark())

    ACT.wait(*prior)
    for n in range(2):
        m = ACT.done(nc.scalar.activation(work[:, 2 * n:2 * n + 2, :], two(n), FN.Square))
    PE.wait(m, *prior)
    for n in range(4):
        ins = nc.tensor.matmul(bank(n // 2)[:, (n % 2) * S:(n % 2) * S + S], core.ones[:, :], work[:, n, :],
                               start=True, stop=True, skip_group_check=True)
    mm = PE.done(ins)
    yield
    ln = [core.ln_mean(bank(n), a, 1.0, mm) for n, a in enumerate((low, high))]
    yield
    for n, a in enumerate((low, high)):
        m = core.exp_half(a, ln[n], None if n else core.eps[:, 1:2])
        DVE.wait(m, *prior)
        normed = DVE.done(nc.vector.tensor_tensor(flat(two(n)), flat(two(n)), a, ALU.mult))
    PE.wait(m, normed, cols_ready)
    for h in range(2):
        c = slice(h * S, h * S + S)
        spread_row(core, bank(2)[:, c], core.hd[:, 1, :], h0 + h, DH, ())
        spread_row(core, bank(3)[:, c], core.hd[:, 0, :], h0 + h, DH, ())
    spread = PE.done(nc.tensor.transpose(bank(0)[:, tile(0)], k(0)[:, 0:P], core.ident()))
    for h in range(2):
        for t in range(2):
            c = slice(t * P, t * P + P)
            if h or t:
                nc.tensor.transpose(bank(0)[:, tile(2 * h + t)], k(h)[:, c], core.ident())
            ins = nc.tensor.transpose(bank(1)[:, tile(2 * h + t)], v(h)[:, c], core.ident())
    turned = PE.done(ins)
    yield
    ACT.wait(spread)
    eg = ACT.done(nc.scalar.activation(d["eg"], bank(2), FN.Exp))
    DVE.wait(eg, cols_ready)
    column = lambda name, i: dcol(core, name, i % 2, h0 + i // 2)
    for i in range(4):
        m = DVE.done(nc.vector.tensor_scalar(d["dec"][:, tile(i)], bank(2)[:, tile(i)], column("g", i), 0.0,
                                             ALU.subtract, ALU.min))
    ACT.wait(m)
    dec = ACT.done(nc.scalar.activation(d["dec"], d["dec"], FN.Exp))
    qd = DVE.done(nc.vector.tensor_tensor(d["qd"], flat(two(0)), d["eg"], ALU.mult))
    DVE.wait(turned)
    halves = lambda a: a.rearrange("p (h t j) -> p h t j", h=2, t=2)
    for name, scale, src in (("kbg", "bg", 0), ("kdec", "ed", 0), ("vb", "beta", 1)):
        by = dcol(core, scale, 0, 0, 2 * DH).rearrange("p (t h) -> p h t", t=2)[:, h0:h0 + 2, :]
        rows = DVE.done(nc.vector.tensor_tensor(halves(d[name]), halves(bank(src)),
                                                by.unsqueeze(3).to_broadcast([P, 2, 2, P]), ALU.mult))
    yield
    PE.wait(rows)
    for i in range(4):
        h, c = i // 2, slice((i % 2) * P, (i % 2) * P + P)
        ins = nc.tensor.matmul(bank(0)[:, tile(i)], k(h)[:, c], k(h)[:, c], start=True, stop=True,
                               skip_group_check=True)
    kk = PE.done(ins)
    for i in range(4):
        h, c = i // 2, slice((i % 2) * P, (i % 2) * P + P)
        ins = nc.tensor.matmul(bank(1)[:, tile(i)], k(h)[:, c], q(h)[:, c], start=True, stop=True,
                               skip_group_check=True)
    qk = PE.done(ins)
    yield
    DVE.wait(kk, dec)
    m = DVE.done(nc.vector.tensor_tensor(d["kk"], bank(0), d["dec"], ALU.mult))
    DVE.wait(qk)
    aqk = DVE.done(nc.vector.tensor_tensor(d["aqk"], bank(1), d["dec"], ALU.mult))
    DVE.wait(m)
    kk = DVE.done(nc.vector.tensor_tensor(d["kk"], d["kk"], bank(3), ALU.mult))
    yield

    def level_blocks(level, read):
        POOL.wait(kk, *read)
        return POOL.done(nc.gpsimd.tensor_tensor(four(d["km"]), four(d["kk"]),
                                                 wide(core, con1(core, "level", level * P), 4), ALU.mult))
    DVE.wait(kk)
    m = DVE.done(nc.vector.tensor_tensor(four(U), four(d["kk"]), wide(core, con1(core, "level"), 4), ALU.mult))
    DVE.wait(m)
    mu = DVE.done(nc.vector.tensor_tensor(four(U), wide(core, core.ident(), 4), four(U), ALU.subtract))
    lm = level_blocks(1, ())
    PE.wait(mu)
    for i in range(4):
        ins = nc.tensor.transpose(bank(2)[:, tile(i)], U[:, tile(i)], core.ident())
    mm = PE.done(ins)
    ACT.wait(mm, aqk)
    mt = ACT.done(nc.scalar.copy(T, bank(2)))
    yield
    for level in range(1, LEVELS):
        final = level == LEVELS - 1
        PE.wait(lm, mt)
        for i in range(4):
            ins = nc.tensor.matmul(bank(0)[:, tile(i)], d["km"][:, tile(i)], T[:, tile(i)], start=True, stop=True,
                                   skip_group_check=True)
        mp = PE.done(ins)
        if not final:
            lm = level_blocks(level + 1, (mp,))
        else:
            POOL.wait(aqk)
            aqk = POOL.done(nc.gpsimd.tensor_tensor(four(d["aqk"]), four(d["aqk"]),
                                                    wide(core, con1(core, "incl"), 4), ALU.mult))
        ACT.wait(mp, aqk if level == 1 else mp)
        m = ACT.done(nc.scalar.copy(d["dec"], bank(0)))
        yield
        PE.wait(m, mu)
        if not final:
            for i in range(4):
                ins = nc.tensor.matmul(bank(1)[:, tile(i)], U[:, tile(i)], d["dec"][:, tile(i)], start=True,
                                       stop=True, skip_group_check=True)
            mm = PE.done(ins)
            DVE.wait(mm)
            mt = DVE.done(nc.vector.tensor_tensor(T, T, bank(1), ALU.subtract))
        for i in range(4):
            ins = nc.tensor.matmul(bank(2)[:, tile(i)], d["dec"][:, tile(i)], U[:, tile(i)], start=True,
                                   stop=True, skip_group_check=True)
        mm = PE.done(ins)
        DVE.wait(mm)
        mu = DVE.done(nc.vector.tensor_tensor(U, U, bank(2), ALU.subtract))
        yield
    PE.wait(mu)
    for i in range(4):
        ins = nc.tensor.matmul(bank(0)[:, tile(i)], U[:, tile(i)], d["vb"][:, tile(i)], start=True, stop=True,
                               skip_group_check=True)
    mm = PE.done(ins)
    DVE.wait(mm)
    un_ready = DVE.done(nc.vector.tensor_copy(un, bank(0)))
    for i in range(4):
        ins = nc.tensor.matmul(bank(1)[:, tile(i)], d["kbg"][:, tile(i)], U[:, tile(i)], start=True, stop=True,
                               skip_group_check=True)
    mm = PE.done(ins)
    ACT.wait(mm)
    wt_ready = ACT.done(nc.scalar.copy(wt, bank(1)))
    yield
    new, st_ready, outs = un_ready, None, []
    for c in range(S // DC):
        t, off = c // 2, (c % 2) * DC
        rows = slice(off, off + DC)
        ws_p, s_p, o_p = bank(0)[:, 0:S], bank(0)[:, S:2 * S], bank(1 + c % 2)
        cs = lambda h: slice((2 * h + t) * P + off, (2 * h + t) * P + off + DC)
        hv = lambda h: slice(h * P, h * P + P)
        PE.wait(*(outs[c - 2:c - 1] if c >= 2 else (wt_ready,)))
        if c:
            PE.wait(st_ready)
            for h in range(2):
                ins = nc.tensor.matmul(ws_p[rows, hv(h)], wt[:, cs(h)], state[:, hv(h)], start=True, stop=True,
                                       skip_group_check=True)
            mm = PE.done(ins)
            for h in range(2):
                nc.tensor.matmul(o_p[:, h * DC:h * DC + DC], state[:, hv(h)], d["qd"][:, cs(h)],
                                 start=(h == 0), stop=False, skip_group_check=True)
            DVE.wait(mm)
            un_c = un[rows, :].rearrange("p (h t v) -> p h t v", h=2, t=2)[:, :, t, :]
            new = DVE.done(nc.vector.tensor_tensor(un_c, un_c, ws_p[rows, :].rearrange("p (h v) -> p h v", h=2),
                                                   ALU.subtract))
            yield
        PE.wait(new, aqk)
        if c < S // DC - 1:
            for h in range(2):
                ins = nc.tensor.matmul(s_p[:, hv(h)], d["kdec"][rows, tile(2 * h + t)], un[rows, tile(2 * h + t)],
                                       start=True, stop=True, skip_group_check=True)
            mm = PE.done(ins)
            DVE.wait(mm)
            for h in range(2):
                last = h * S + c * DC + DC - 1
                if c:
                    st_ready = DVE.done(nc.vector.scalar_tensor_tensor(
                        state[:, hv(h)], state[:, hv(h)], d["eg"][:, last:last + 1], s_p[:, hv(h)],
                        ALU.mult, ALU.add))
                else:
                    st_ready = DVE.done(nc.vector.tensor_copy(state[:, hv(h)], s_p[:, hv(h)]))
        for h in range(2):
            ins = nc.tensor.matmul(o_p[:, h * DC:h * DC + DC], un[rows, tile(2 * h + t)], d["aqk"][rows, cs(h)],
                                   start=(c == 0 and h == 0), stop=True, skip_group_check=True)
        mm = PE.done(ins)
        ACT.wait(mm, qd)
        outs.append(ACT.done(nc.scalar.copy(core.o[:, h0:h0 + 2, c * DC:c * DC + DC],
                                            o_p[:, 0:2 * DC].rearrange("p (h s) -> p h s", h=2))))
        yield
    ACT.wait(outs[-1])
    sq = ACT.done(nc.scalar.activation(work[:, 0:2, :], core.o[:, h0:h0 + 2, :], FN.Square))
    PE.wait(sq)
    for n in range(2):
        ins = nc.tensor.matmul(bank(3)[:, n * S:n * S + S], core.ones[:, :], work[:, n, :],
                               start=True, stop=True, skip_group_check=True)
    mm = PE.done(ins)
    yield
    m = core.ln_mean(bank(3), high, DK, mm)
    yield
    m = core.exp_half(high, m)
    yield
    DVE.wait(m, outs[-1])
    m = DVE.done(nc.vector.scalar_tensor_tensor(high, flat(core.o[:, h0:h0 + 2, :]), par1(core, "dn_norm"), high,
                                                ALU.mult, ALU.mult))
    DVE.wait(m)
    m = DVE.done(nc.vector.tensor_tensor(high, high, flat(core.zd[:, h0:h0 + 2, :]), ALU.mult))
    yield
    core.split_x(work[:, 2:4, :], 24 + h0, 2, m)


def ssm(core, cols_ready):
    tail = ()
    for g in range(SG):
        done = []
        side_by_side(*(ssm_heads(core, g, side, cols_ready, done) for side in range(2)), *tail)
        tail = (ssm_tail(core, g, done),)
    side_by_side(*tail)


def ssm_heads(core, g, side, cols_ready, done):
    nc, PE, ACT, DVE, POOL = core.nc, core.PE, core.ACT, core.DVE, core.POOL
    n = HG // 2
    h0, c0 = g * HG + side * n, 4 * g + 2 * side
    b = {name: a[:, side * a.shape[1] // 2:(side + 1) * a.shape[1] // 2] for name, a in core.sm.items()}
    bank = lambda i: core.bank(4 * side + i)
    nx = SI // P
    B, C = core.xbc[:, nx + g, :], core.xbc[:, nx + SG + g, :]
    ac_p = core.banks(4 * side, 2)
    PE.wait(cols_ready, *core.y_read[side])
    for h in range(n):
        ins = spread_row(core, ac_p[:, h * S:h * S + S], core.hs[:, 2, :], h0 + h, SH, ())
    spread = PE.done(ins)
    cb_p, xt_p = bank(2), bank(3)
    for t in range(2):
        c = slice(t * P, t * P + P)
        nc.tensor.matmul(cb_p[:, c], B[:, c], C[:, c], start=True, stop=True, skip_group_check=True)
    cbm = PE.done(nc.tensor.transpose(cb_p[:, 2 * P:3 * P], B[:, 0:P], core.ident()))
    for t in range(2):
        for c in range(2):
            ins = nc.tensor.transpose(xt_p[:, t * S + c * P:t * S + c * P + P],
                                      core.xbc[:, c0 + c, t * P:t * P + P], core.ident())
    turned = PE.done(ins)
    yield
    DVE.wait(spread)
    for h in range(n):
        for t in range(2):
            o = slice(h * S + t * P, h * S + t * P + P)
            m = DVE.done(nc.vector.tensor_scalar(b["w"][:, o], ac_p[:, o], scol(core, "ac", t, h0 + h), 0.0,
                                                 ALU.subtract, ALU.min))
    ACT.wait(m)
    heads = lambda a: a.rearrange("p (h s) -> p h s", h=n)
    ea = ACT.done(nc.scalar.activation(heads(b["cs"]), heads(ac_p)[:, :, P:S], FN.Exp))
    dec = ACT.done(nc.scalar.activation(b["w"], b["w"], FN.Exp))
    DVE.wait(turned)
    over = lambda a: a.unsqueeze(2).to_broadcast([P, n, SP])
    for t in range(2):
        c = slice(t * S, t * S + S)
        xd = DVE.done(nc.vector.tensor_tensor(heads(b["xd"][:, c]), heads(xt_p[:, c]),
                                              over(scol(core, "dt", t, h0, n)), ALU.mult))
    DVE.wait(cbm)
    bt = DVE.done(nc.vector.tensor_copy(b["bt"], cb_p[:, 2 * P:3 * P]))
    DVE.wait(xd)
    xe = DVE.done(nc.vector.tensor_tensor(heads(b["xe"]), heads(b["xd"][:, 0:S]),
                                          over(scol(core, "te", 0, h0, n)), ALU.mult))
    cbs = DVE.done(nc.vector.tensor_tensor(b["cb"].rearrange("p (t l) -> p t l", t=2),
                                           cb_p[:, 0:2 * P].rearrange("p (t l) -> p t l", t=2),
                                           wide(core, con1(core, "causal"), 2), ALU.mult))
    core.cb_read = cbs
    yield
    PE.wait(xe, bt, ea)
    mm = PE.done(nc.tensor.matmul(bank(0)[:, 0:S], b["bt"], b["xe"], start=True, stop=True))
    ACT.wait(mm)
    state = ACT.done(nc.scalar.copy(b["state"], bank(0)[:, 0:S]))
    POOL.wait(ea)
    cs = POOL.done(nc.gpsimd.tensor_tensor(heads(b["cs"]), heads(b["cs"]), wide(core, C[:, P:S], n), ALU.mult))
    DVE.wait(dec, cbs)
    w = DVE.done(nc.vector.tensor_tensor(heads(b["w"]), heads(b["w"]),
                                         b["cb"].unsqueeze(1).to_broadcast([P, n, S]), ALU.mult))
    yield
    y_p = bank(1)
    PE.wait(w, cs, state)
    for h in range(n):
        rows = slice((h % 2) * SP, (h % 2) * SP + SP)
        for t in range(2):
            o = y_p[rows, (h // 2) * S + t * P:(h // 2) * S + t * P + P]
            ins = nc.tensor.matmul(o, b["xd"][:, t * S + h * SP:t * S + h * SP + SP],
                                   b["w"][:, h * S + t * P:h * S + t * P + P],
                                   start=True, stop=(t == 0), skip_group_check=True)
            if t == 1:
                ins = nc.tensor.matmul(o, b["state"][:, h * SP:h * SP + SP], b["cs"][:, h * P:h * P + P],
                                       start=False, stop=True, skip_group_check=True)
    mm = PE.done(ins)
    yield
    yield
    DVE.wait(mm, *core.tail_done)
    y = core.tmp[:, 2 * side:2 * side + 2, :]
    for c in range(2):
        m = DVE.done(nc.vector.scalar_tensor_tensor(y[:, c, :], core.xbc[:, c0 + c, :],
                                                    par1(core, "ssm_d", c0 + c), y_p[:, c * S:c * S + S],
                                                    ALU.mult, ALU.add))
    core.y_read[side] = (m, *core.tail_done)
    DVE.wait(m)
    done.append(DVE.done(nc.vector.tensor_tensor(y, y, core.z[:, c0:c0 + 2, :], ALU.mult)))


def ssm_tail(core, g, done):
    nc, PE, ACT, DVE = core.nc, core.PE, core.ACT, core.DVE
    y, work = core.tmp[:, 0:4, :], core.tmp[:, 4:8, :]
    ACT.wait(*done, *core.tail_done)
    sq = ACT.done(nc.scalar.activation(work, y, FN.Square))
    yield
    yield
    PE.wait(sq, core.cb_read)
    out = core.bank(6)[:, 0:S]
    for c in range(4):
        ins = nc.tensor.matmul(out, core.ones[:, :], work[:, c, :], start=(c == 0), stop=(c == 3),
                               skip_group_check=True)
    rs = core.inv_sqrt(out, core.rs[:, 1, :], 512, PE.done(ins))
    yield
    DVE.wait(rs)
    for c in range(4):
        m = DVE.done(nc.vector.scalar_tensor_tensor(work[:, c, :], y[:, c, :], par1(core, "ssm_norm", 4 * g + c),
                                                    core.rs[:, 1, :], ALU.mult, ALU.mult))
    yield
    m2 = core.split_x(work, 8 + 4 * g, 4, m)
    core.tail_done = (m, m2, ACT.own.mark())


def branch(core, w, l, chunks, at, after, pairs=None):
    wl = w[bass.ds(l, 1)]
    one = lambda kc: (core.xh[:, bass.ds(at + kc, 1), :].rearrange("p o s -> p (o s)"),
                      core.xl[:, bass.ds(at + kc, 1), :].rearrange("p o s -> p (o s)"))
    st = core.st
    waits = lambda kc: (after if kc == 0 else ()) + ((pairs[kc // 2],) if pairs and kc % 2 == 0 else ())
    for kc in range(4):
        m = st.row_block(wl, kc * P, one(kc), kc == 0, False, waits(kc))
    if chunks > 8:
        with core.prog.loop(chunks // 4 - 2) as i:
            for j in range(4):
                st.row_block(wl, i * (4 * P) + (4 + j) * P, one(i * 4 + (4 + j)), False, False)
    for kc in range(chunks - 4, chunks):
        m = st.row_block(wl, kc * P, one(kc), False, kc == chunks - 1, waits(kc))
    return m


def mixer1(core, io, l, each):
    nc, PE, ACT, DVE, POOL, st = core.nc, core.PE, core.ACT, core.DVE, core.POOL, core.st
    w = io["w_in"][bass.ds(l, 1)]
    x = core.x(0, ND)
    ready = core.norm_split(core.h[:, :, :], lambda c: par1(core, "mix_norm", c), ND, D, 0, each=each)
    POOL.settle()
    for j in range(2):
        m = POOL.done(nc.gpsimd.memset(core.pad_buf[:, j, 0:3], 0.0))
    ACT.wait(m)
    DVE.wait(m)
    bank, mark = st.unit(w, None, x, ready, cols=(COL_DT, COL_B), extra=lambda *a: small_extra(core, *a))
    ready = []
    st.put_off.append(small_params(core, bank, mark, ready))
    cw = lambda name: (lambda c, j, k: core.pv[:, bass.ds(c * 4 + (PAR1[name][0] + 4 * j + k), 1)])
    dw, sw = cw("dn_cw"), cw("ssm_cw")
    project(core, w, COL_QKV, DCONV // 256, x,
                 lambda i, bank, mark: conv_unit(core, bank, mark, i * 2, 4, dw, None, core.qkv))
    cols_ready, = ready
    project(core, w, COL_ZD, DH * DK // 256, x, act_unit(core, FN.Silu, core.zd))
    st.drain()
    with ExitStack() as inner:
        core.dn = buffers(core, inner, "dn", dict(eg=1024, dec=1024, qd=1024, kbg=1024, kdec=1024, vb=1024,
                                                  kk=1024, aqk=1024, km=1024))
        core.dn["state"] = core.act_buf
        core.o = core.qkv
        core.prog.join()
        delta(core, cols_ready)
        core.prog.join()
    with ExitStack() as inner:
        core.z = core.sb("z", [P, SI // P, S], ctx=inner)
        core.sm = buffers(core, inner, "ssm", dict(w=2048, cs=1024, cb=512, bt=2 * P, xd=1024, xe=512))
        core.sm["state"] = core.act_buf
        core.xbc = core.qkv
        bias = lambda c, j: core.pv[:, bass.ds(c + (PAR1["ssm_cb"][0] + j), 1)]
        project(core, w, COL_XBC, SCONV // 256, x,
                     lambda i, bank, mark: conv_unit(core, bank, mark, i * 2, 4, sw, bias, core.xbc))
        project(core, w, COL_Z, SI // 256, x, act_unit(core, FN.Silu, core.z), peel=8)
        st.drain()
        core.prog.join()
        core.tail_done, core.y_read = (), [(), ()]
        ssm(core, cols_ready)
        core.prog.join()
    with ExitStack() as inner:
        gates = core.sb("gates", [P, 2 * ND, S], ctx=inner)
        project(core, w, COL_GS, 2 * D // 256, x, act_unit(core, FN.Sigmoid, gates), peel=8)
        st.drain()
        flat = lambda a: a.rearrange("p c s -> p (c s)")
        core.prog.join()
        m = branch(core, io["ssm_w_branch"], l, SI // P, 8, ())
        DVE.wait(m)
        for b in range(4):
            m = DVE.done(nc.vector.tensor_tensor(flat(core.tmp[:, 2 * b:2 * b + 2, :]), core.bank(4 + b),
                                                 flat(gates[:, 2 * b:2 * b + 2, :]), ALU.mult))
        m = branch(core, io["dn_w_branch"], l, DH, 24, (m,))
        DVE.wait(m)
        for b in range(4):
            gb = flat(gates[:, ND + 2 * b:ND + 2 * b + 2, :])
            m = DVE.done(nc.vector.tensor_tensor(gb, core.bank(4 + b), gb, ALU.mult))
        DVE.wait(m)
        both = [DVE.done(nc.vector.tensor_tensor(core.tmp[:, c:c + 2, :], core.tmp[:, c:c + 2, :],
                                                 gates[:, ND + c:ND + c + 2, :], ALU.add)) for c in range(0, ND, 2)]
        pairs = core.split_pairs(core.tmp, 0, ND, both)
        m = branch(core, io["w_out"], l, ND, 0, (m,), pairs)
        return core.add_sum(1.0, m)


def small_extra(core, half, hi, lo, x):
    for c in range(4):
        kc = 4 * half + c
        wh, wl = (a[:, c * 256 + P + DH:c * 256 + 2 * P] for a in (hi, lo))
        for n, (a, b) in enumerate(((wh, x[0][:, kc, :]), (wh, x[1][:, kc, :]), (wl, x[0][:, kc, :]))):
            ins = core.nc.tensor.matmul(core.bank(7)[0:P - DH, 0:S], a, b, start=(kc == 0 and n == 0),
                                        stop=(kc == 7 and n == 2), skip_group_check=True)
    return ins


def layer1(core, io, l):
    nc = core.nc
    core.ACT.wait(core.DVE.own.mark(), core.ACT.own.mark())
    core.s_par.inc(nc.scalar.dma_start(core.pv[:, :], io["par1"][bass.ds(l, 1)].rearrange("o p n -> p (o n)")), 16)
    for _ in range(AHEAD):
        core.st.split()
    for e in (core.ACT, core.DVE):
        e.wait(core.s_par.mark())
    with ExitStack() as inner:
        core.hid_buf = core.sb("hid1", [P, 512], ctx=inner)
        m = core.ffn(io["ffn1_w_in"], io["ffn1_w_out"], l, lambda c: par1(core, "ffn1_norm", c))
        each = core.add_sum(0.5, m)
    with ExitStack() as inner:
        core.qkv = core.sb("qkv", [P, 3 * DH, S], ctx=inner)
        core.pad_buf = core.sb("pad", [P, 2, 3 + S], ctx=inner)
        core.zd = core.sb("zd", [P, DH, S], ctx=inner)
        core.hd_raw = core.tmp[0:SH, :, :].rearrange("p c s -> p (c s)")
        core.hs = core.sb("heads_ssm", [SH, 5, S], ctx=inner)
        core.hd = core.sb("heads_dn", [DH, 6, S], ctx=inner)
        core.cols = core.sb("cols", [P, 6 * SH + 8 * DH], ctx=inner)
        each = mixer1(core, io, l, each)
    with ExitStack() as inner:
        core.hid_buf = core.sb("hid2", [P, 512], ctx=inner)
        m = core.ffn(io["ffn2_w_in"], io["ffn2_w_out"], l, lambda c: par1(core, "ffn2_norm", c),
                     last=True, each=each)
        core.add_sum(0.5, m)
        core.prog.join()
    core.st.skip_banks_to_start()
    core.st.skip_blocks()
    core.prog.join()


def buffers(core, ctx, stage, sizes):
    return {name: core.sb(stage + "_" + name, [P, n], ctx=ctx) for name, n in sizes.items()}


def par2(core, name, i=0, n=1, rows=P):
    a, width = PAR2[name]
    assert i + n <= width
    return core.pv2[0:rows, a + i:a + i + n]


def con2(core, name, rows=slice(0, P)):
    a, n = CON2[name]
    return core.con2[rows, a:a + n]


def moba_bias(core, io):
    nc, PE, ACT, DVE, SP = core.nc, core.PE, core.ACT, core.DVE, core.SP
    with ExitStack() as inner:
        cont = core.sb("con_t5", [P, NCONT], ctx=inner)
        relb = core.sb("rel_bias", [32, AH], ctx=inner)
        line = core.sb("bias_line", [AH, S + P], ctx=inner)
        slid = core.sb("bias_slid", [P, AH, S], ctx=inner)
        core.s_par.inc(nc.sync.dma_start(cont[:, :], io["con_t5"]), 16)
        core.s_par.inc(nc.sync.dma_start(relb[:, :], io["rel_bias"]), 16)
        flip = cont[:, CONT["flip"][0]:CONT["flip"][0] + P]
        onehot = cont[0:32, CONT["bucket"][0]:CONT["bucket"][0] + S + P]
        for e in (PE, DVE):
            e.wait(core.s_par.mark())
        mm = PE.done(nc.tensor.matmul(core.bank(0)[0:AH, 0:S + P], relb[:, :], onehot, start=True, stop=True))
        DVE.wait(mm)
        m = DVE.done(nc.vector.tensor_copy(line[:, :], core.bank(0)[0:AH, 0:S + P]))
        DVE.wait(m)
        m = DVE.done(nc.vector.memset(line[:, S:S + P], NEG))
        SP.wait(m)
        scratch = io["scratch"]
        core.s_par.inc(nc.sync.dma_start(scratch, line[:, :]), 16)
        SP.wait(core.s_par.mark())
        src = bass.AP(scratch.tensor, scratch.offset, [[1, P], [S + P, AH], [1, S]])
        core.s_par.inc(nc.sync.dma_start(slid[:, :, :], src), 16)
        PE.wait(core.s_par.mark(), m)
        for h in range(AH):
            ins = nc.tensor.matmul(core.bank(h // 2)[:, (h % 2) * S:(h % 2) * S + S], flip, slid[:, h, :],
                                   start=True, stop=True, skip_group_check=True)
        mm = PE.done(ins)
        ACT.wait(mm)
        for h in range(AH):
            b = core.bank(h // 2)[:, (h % 2) * S:(h % 2) * S + S]
            ACT.done(nc.scalar.copy(core.t5[:, h, 0:S], b))
            ACT.done(nc.scalar.copy(core.t5[:, h, S:S + P], b[:, P:S]))
        core.prog.join()


def units(core, w, cols, x, use, after=()):
    for n, col in enumerate(cols):
        bank, mark = core.st.unit(w, col, x, () if n else after)
        use(n, bank, mark)


def copy_unit(core, dst):
    def use(n, bank, mark):
        core.ACT.wait(mark)
        core.st.s_ev.inc(core.nc.scalar.copy(dst[:, 2 * n:2 * n + 2, :].rearrange("p c s -> p (c s)"), bank))
    return use


def mixer2(core, io, l):
    nc, PE, ACT, DVE, POOL, st = core.nc, core.PE, core.ACT, core.DVE, core.POOL, core.st
    core.prog.join()
    w = io["w_in_2"][bass.ds(l, 1)]
    x = core.x(0, ND)
    flat = lambda a: a.rearrange("p c s -> p (c s)")
    with ExitStack() as inner:
        sb = lambda name, shape: core.sb(name, shape, ctx=inner)
        pa, pf = sb("proj_a", [P, 12, S]), sb("proj_f", [P, 9, S])
        va, vf, vm = sb("v_moba", [P, 2, 3 * P]), sb("v_fox", [P, 2, 3 * P]), sb("v_mla", [P, 2, S])
        qm, km, kr = sb("q_mla", [P, MH, S]), sb("k_mla", [P, MH, S]), sb("k_rope", [P, 2, S])
        fg, dec = sb("forget", [P, 2 * XH_]), sb("decay", [XH_, 4, S])
        u = core.norm_split(core.h[:, :, :], lambda c: par2(core, "mix_pre", c), ND, D, 0)
        units(core, w, [256 * n for n in range(6)], x, copy_unit(core, pa), u)
        bank, mark = st.unit(w, None, x, cols=(COL2_KR - 64, COL2_F + 8 * P))
        ACT.wait(mark)
        ACT.done(nc.scalar.copy(kr[64:96, 0, :], bank[64:96, 0:S]))
        st.s_ev.inc(nc.scalar.copy(pf[:, 8, :], bank[:, S:2 * S]))

        def forget(hi, lo):
            for t in range(2):
                for kc in range(ND):
                    a, b = (v[:, kc, t * P:t * P + P] for v in x)
                    wh, wl = (v[:, kc * XH_:(kc + 1) * XH_] for v in (hi, lo))
                    for n, (p, q) in enumerate(((a, wh), (b, wh), (a, wl))):
                        ins = nc.tensor.matmul(core.bank(7)[:, t * XH_:t * XH_ + XH_], p, q,
                                               start=(kc == 0 and n == 0), stop=(kc == 7 and n == 2),
                                               skip_group_check=True)
            return ins
        parts = [((lambda r, a=a: r[:, a * 4 * XH_:(a + 1) * 4 * XH_].rearrange("p (c n) -> p c n", c=4)),
                  w[:, a * 512:a * 512 + 512, COL2_FG:COL2_FG + XH_].rearrange("o (c p) n -> p (o c) n", p=P))
                 for a in range(2)]
        mm = st.block(parts, forget)
        DVE.wait(mm)
        fgm = DVE.done(nc.vector.tensor_copy(fg[:, :], core.bank(7)[:, 0:2 * XH_]))
        cq, ckv = [], []
        f, sc, cum, neg = (dec[:, i, :] for i in range(4))

        def aside():
            cq.extend(core.norm_split(pa[:, 9:11, :], lambda c: par2(core, "q_norm", c), 2, QR, 8,
                                      (ACT.own.mark(), st.s_ev.mark(), fgm))[1])
            yield
            ckv.extend(core.norm_split(pa[:, 11:12, :], lambda c: par2(core, "kv_norm", c), 1, KVR, 10,
                                       (*cq, st.s_ev.mark()))[1])
            yield
            PE.wait(*ckv)
            for t in range(2):
                ins = nc.tensor.transpose(core.bank(7)[0:XH_, t * P:t * P + P], fg[:, t * XH_:(t + 1) * XH_],
                                          core.ident())
            m = PE.done(ins)
            yield
            DVE.wait(m)
            m = DVE.done(nc.vector.tensor_scalar(f, core.bank(7)[0:XH_, 0:S], par2(core, "b_f", rows=XH_), None,
                                                 ALU.add))
            gates.append(m)
            yield
            ACT.wait(m)
            m = ACT.done(nc.scalar.activation(sc, f, FN.Abs))
            ACT.wait(m)
            m = ACT.done(nc.scalar.activation(sc, sc, FN.Exp, scale=-1.0))
            ACT.wait(m)
            m = ACT.done(nc.scalar.activation(sc, sc, FN.Ln, bias=1.0))
            yield
            DVE.wait(m)
            m = DVE.done(nc.vector.scalar_tensor_tensor(f, f, 0.0, sc, ALU.min, ALU.subtract))
            DVE.wait(m)
            m = DVE.done(nc.vector.tensor_tensor_scan(sc, core.one_row[:, :], f, 0.0, ALU.mult, ALU.add))
            DVE.wait(m)
            DVE.done(nc.vector.tensor_scalar(cum, sc, float(HD) ** 0.5, None, ALU.mult))
            gates.append(DVE.done(nc.vector.tensor_scalar(neg, sc, -(float(HD) ** 0.5), None, ALU.mult)))
        gates = []
        st.put_off.append(aside())
        units(core, w, [COL2_F + 256 * n for n in range(4)], x, copy_unit(core, pf))
        st.drain()
        q_p = core.banks(4, 2)
        for kc in range(2):
            def up_q(hi, lo, kc=kc):
                a, b = core.x(8 + kc)
                for h in range(MH):
                    wh, wl = (v[:, h * QKD:(h + 1) * QKD] for v in (hi, lo))
                    for n, (p, q) in enumerate(((wh, a), (wh, b), (wl, a))):
                        ins = nc.tensor.matmul(q_p[0:QKD, h * S:h * S + S], p, q,
                                               start=(kc == 0 and h % 2 == 0 and n == 0),
                                               stop=(kc == 1 and n == 2), skip_group_check=True)
                return ins
            half = MH * QKD // 2
            parts = [((lambda r, a=a: r[:, a * half:(a + 1) * half]),
                      io["w_uq_2"][bass.ds(l, 1), kc * P:kc * P + P, a * half:(a + 1) * half].rearrange(
                          "o p n -> p (o n)")) for a in range(2)]
            mq = st.block(parts, up_q, cq)
        k_p, v_p = core.banks(2, 2), core.bank(6)

        def up_kv(hi, lo):
            a, b = core.x(10)
            for h in range(MH):
                wh, wl = (v[:, h * P:(h + 1) * P] for v in (hi, lo))
                for n, (p, q) in enumerate(((wh, a), (wh, b), (wl, a))):
                    nc.tensor.matmul(k_p[:, h * S:h * S + S], p, q, start=(n == 0), stop=(n == 2),
                                     skip_group_check=True)
            for t in range(2):
                c = slice(t * P, t * P + P)
                wh, wl = (v[:, 0:MH * P].rearrange("p (h n) -> p h n", h=MH)[:, :, HD:P] for v in (hi, lo))
                for n, (p, q) in enumerate(((a[:, c], wh), (b[:, c], wh), (a[:, c], wl))):
                    ins = nc.tensor.matmul(v_p[:, t * S:t * S + S], p, q, start=(n == 0), stop=(n == 2),
                                           skip_group_check=True)
            return ins
        parts = [((lambda r, a=a: r[:, a * S:(a + 1) * S]),
                  io["w_ukv_2"][bass.ds(l, 1), :, a * S:(a + 1) * S].rearrange("o p n -> p (o n)"))
                 for a in range(2)]
        mkv = st.block(parts, up_kv, (*ckv, st.s_ev.mark()))
        ACT.wait(mkv)
        ACT.done(nc.scalar.copy(km[0:HD, :, :], k_p[0:HD, :].rearrange("p (h s) -> p h s", h=MH)))
        ACT.done(nc.scalar.copy(flat(vm[:, :, :]), v_p))
        raw_q = ACT.done(nc.scalar.copy(qm[0:QKD, :, :], q_p[0:QKD, :].rearrange("p (h s) -> p h s", h=MH)))
        rr = slice(64, 96)
        PE.wait(raw_q)
        for n in range(2):
            nc.tensor.matmul(core.bank(4 + n)[0:QKD, :], con2(core, "rot", slice(0, QKD))[:, 0:QKD],
                             flat(qm[0:QKD, 2 * n:2 * n + 2, :]), start=True, stop=True)
        PE.wait(*gates)
        PE.settle()
        mr = PE.done(nc.tensor.matmul(core.bank(7)[rr, 0:S], con2(core, "rot", rr)[:, rr], kr[rr, 0, :],
                                      start=True, stop=True))
        DVE.wait(mr, raw_q)
        four = lambda a, rows: a.unsqueeze(1).to_broadcast([rows, MH, S])
        rq = core.tmp[0:QKD, 0:MH, :]
        m1 = DVE.done(nc.vector.tensor_tensor(rq, q_p[0:QKD, :].rearrange("p (h s) -> p h s", h=MH),
                                              four(con2(core, "sin", slice(0, QKD)), QKD), ALU.mult))
        m2 = DVE.done(nc.vector.tensor_tensor(qm[0:QKD, :, :], qm[0:QKD, :, :],
                                              four(con2(core, "cos", slice(0, QKD)), QKD), ALU.mult))
        m3 = DVE.done(nc.vector.tensor_tensor(kr[rr, 1, :], core.bank(7)[rr, 0:S], con2(core, "sin", rr), ALU.mult))
        m4 = DVE.done(nc.vector.tensor_tensor(kr[rr, 0, :], kr[rr, 0, :], con2(core, "cos", rr), ALU.mult))
        DVE.wait(m4)
        DVE.done(nc.vector.tensor_tensor(qm[0:QKD, :, :], qm[0:QKD, :, :], rq, ALU.add))
        for h in range(MH):
            mla = DVE.done(nc.vector.tensor_tensor(km[rr, h, :], kr[rr, 0, :], kr[rr, 1, :], ALU.add))
        PE.wait(mla, ACT.own.mark(), st.s_ev.mark(), mkv)
        for dst, src, c0, b0 in ((va, pa, 6, 0), (vf, pf, 6, 2)):
            for t in range(2):
                for c in range(3):
                    ins = nc.tensor.transpose(core.bank(b0 + t)[:, c * P:c * P + P],
                                              src[:, c0 + c, t * P:t * P + P], core.ident())
            mt = PE.done(ins)
            DVE.wait(mt)
            for t in range(2):
                vals = DVE.done(nc.vector.tensor_copy(dst[:, t, :], core.bank(b0 + t)[:, 0:3 * P]))
        core.prog.join()
        attend(core, inner, pa, pf, qm, km, va, vf, vm, cum, neg)
        core.prog.join()
        pairs = core.split_pairs(core.tmp, 0, ND, [DVE.own.mark()] * (ND // 2))
        m = branch2(core, io["w_o_2"], l, pairs)
        return post(core, m, "mix_post", pa)


def attend(core, ctx, pa, pf, qm, km, va, vf, vm, cum, neg):
    W = S + P
    bufs = [[core.sb(f"{name}{i}", shape, ctx=ctx) for name, shape in (
        ("scores", [P, 2, W]), ("probs_t", [P, 2, W]), ("softmax", [P, 3, 4]))] for i in range(2)]
    pairs = ([("moba", c) for c in range(AH // 2)] + [("mla", c) for c in range(MH // 2)]
             + [("fox", c) for c in range(XH_ // 2)])

    def operands(kind, c, h):
        rows = slice(64 * h, 64 * h + 64)
        if kind == "mla":
            r = slice(0, QKD)
            return qm[r, 2 * c + h, :], km[r, 2 * c + h, :], lambda t: vm[:, t, (2 * c + h) * HD:(2 * c + h + 1) * HD]
        src, v = (pa, va) if kind == "moba" else (pf, vf)
        return src[rows, c, :], src[rows, 3 + c, :], lambda t: v[:, t, c * P + 64 * h:c * P + 64 * h + 64]

    for n in range(0, len(pairs), 2):
        side_by_side(*(attend_pair(core, n + i, i, pairs[n + i], bufs[i], operands, cum, neg) for i in range(2)))


def attend_pair(core, n, side, pair, bufs, operands, cum, neg):
    nc, PE, ACT, DVE = core.nc, core.PE, core.ACT, core.DVE
    (kind, c), (s, pt, red) = pair, bufs
    W = S + P
    bank = lambda i: core.bank(4 * side + i)
    parts = [(2 * t + h, h, o, keys) for h in range(2) for t, o, keys in ((0, 0, S), (1, S, P))]
    PE.wait(ACT.own.mark(), DVE.own.mark())
    for h in range(2):
        q, k, _ = operands(kind, c, h)
        for t, o, keys in ((1, 0, S), (0, S, P)):
            out = bank(h)[:, o:o + keys]
            more = kind == "fox"
            ins = nc.tensor.matmul(out, q[:, t * P:t * P + P], k[:, 0:keys], start=True, stop=not more,
                                   skip_group_check=True)
            if more:
                pick = core.ident(XH_)[:, 2 * c + h:2 * c + h + 1]
                nc.tensor.matmul(out, cum[:, t * P:t * P + P], pick.to_broadcast([XH_, keys]), start=False,
                                 stop=False, skip_group_check=True)
                ins = nc.tensor.matmul(out, pick.to_broadcast([XH_, P]), neg[:, 0:keys], start=False,
                                       stop=True, skip_group_check=True)
    mm = PE.done(ins)
    yield
    scale = float(QKD if kind == "mla" else HD) ** -0.5
    DVE.wait(mm)
    for h in range(2):
        bias = core.t5[:, 2 * c + h, :] if kind == "moba" else con2(core, "mask")
        m = DVE.done(nc.vector.scalar_tensor_tensor(s[:, h, :], bank(h)[:, 0:W], scale, bias, ALU.mult, ALU.add))
    DVE.wait(m)
    DVE.done(nc.vector.tensor_reduce(red[:, 0, 0:2], s[:, :, 0:S], AX_X, ALU.max))
    m = DVE.done(nc.vector.tensor_reduce(red[:, 0, 2:4], s[:, :, S:W], AX_X, ALU.max))
    DVE.wait(m)
    m = DVE.done(nc.vector.tensor_scalar(red[:, 0, :], red[:, 0, :], -1.0, None, ALU.mult))
    yield
    ACT.wait(m)
    for a, h, o, keys in parts:
        m = ACT.done(nc.scalar.activation(s[:, h, o:o + keys], s[:, h, o:o + keys], FN.Exp,
                                          bias=red[:, 0, a:a + 1], accum_out=red[:, 1, a:a + 1]))
    yield
    DVE.wait(m)
    m = DVE.done(nc.vector.reciprocal(red[:, 2, :], red[:, 1, :]))
    DVE.wait(m)
    for a, h, o, keys in parts:
        m = DVE.done(nc.vector.tensor_scalar(s[:, h, o:o + keys], s[:, h, o:o + keys], red[:, 2, a:a + 1], None,
                                             ALU.mult))
    yield
    PE.wait(m)
    for h in range(2):
        for i in range(3):
            ins = nc.tensor.transpose(bank(h)[:, i * P:i * P + P], s[:, h, i * P:i * P + P], core.ident())
    mt = PE.done(ins)
    yield
    ACT.wait(mt)
    for h in range(2):
        m = ACT.done(nc.scalar.copy(pt[:, h, :], bank(h)[:, 0:W]))
    yield
    PE.wait(m)
    out = bank(2)
    for h in range(2):
        v = operands(kind, c, h)[2]
        rows = slice(64 * h, 64 * h + 64)
        for t in range(2):
            nc.tensor.matmul(out[rows, P:S], v(t), pt[:, h, t * P:t * P + P], start=(t == 0), stop=(t == 1),
                             skip_group_check=True)
        ins = nc.tensor.matmul(out[rows, 0:P], v(0), pt[:, h, S:W], start=True, stop=True, skip_group_check=True)
    mm = PE.done(ins)
    yield
    DVE.wait(mm)
    DVE.done(nc.vector.tensor_copy(core.tmp[:, n, :], out[:, 0:S]))


def branch2(core, w, l, pairs):
    wl = w[bass.ds(l, 1)]
    for kc in range(ND):
        m = core.st.row_block(wl, kc * P, core.x(kc), kc == 0, kc == ND - 1, (pairs[kc // 2],))
    return m


def post(core, after, gain, y):
    nc, DVE, POOL = core.nc, core.DVE, core.POOL
    core.prog.join()
    DVE.wait(after)
    each, added = [], []
    for b in range(4):
        each.append(DVE.done(nc.vector.tensor_copy(y[:, 2 * b:2 * b + 2, :].rearrange("p c s -> p (c s)"),
                                                   core.bank(4 + b))))
    rs, summed = core.inv_rms(y[:, 0:ND, :], ND, D, core.bank(0), core.rs[:, 0, :], each=each)
    DVE.wait(rs, summed)
    for b in range(4):
        two = slice(2 * b, 2 * b + 2)
        for c in range(2 * b, 2 * b + 2):
            m = DVE.done(nc.vector.scalar_tensor_tensor(y[:, c, :], y[:, c, :], par2(core, gain, c),
                                                        core.rs[:, 0, :], ALU.mult, ALU.mult))
        e = (POOL, DVE)[b % 2]
        e.wait(m)
        added.append(e.done(e.eng.tensor_tensor(core.h[:, two, :], core.h[:, two, :], y[:, two, :], ALU.add)))
    return added


def conv_chunks(core, pads):
    cw, cb = PAR2["cw"][0], PAR2["cb"][0]

    def stage(i, bank, mark, at, out):
        c = lambda j: i * 2 + (j + (NF if at else 0))
        conv_taps(core, bank, mark, KC2, lambda j, k: core.pv2[:, bass.ds(c(j) * KC2 + (cw + k), 1)],
                  lambda j: core.pv2[:, bass.ds(c(j) + cb, 1)], pads[:, at:at + 2, :],
                  out[:, :].rearrange("p (c s) -> p c s", c=2), (core.hid_free(), core.s_conv.mark()))
        yield
    return stage


def layer2(core, io, l):
    nc = core.nc
    core.ACT.wait(core.DVE.own.mark(), core.ACT.own.mark())
    core.s_par.inc(nc.scalar.dma_start(core.pv2[:, :], io["par2"][bass.ds(l, 1)].rearrange("o p n -> p (o n)")), 16)
    for _ in range(AHEAD):
        core.st.split()
    for e in (core.ACT, core.DVE):
        e.wait(core.s_par.mark())
    each = mixer2(core, io, l)
    with ExitStack() as inner:
        core.hid_buf = core.sb("hid3", [P, 512], ctx=inner)
        pads, core.up_buf = core.sb("pads2", [P, 4, 2 + S], ctx=inner), core.sb("conv_up", [P, 2 * S], ctx=inner)
        sums = core.sb("sums", [P, ND, S], ctx=inner)
        core.DVE.wait(*each)
        core.DVE.done(nc.vector.memset(pads[:, :, 0:2], 0.0))
        m = core.ffn(io["w_up_2"], io["w_down_2"], l, lambda c: par2(core, "ffn_pre", c),
                     conv=conv_chunks(core, pads), last=True, each=each)
        post(core, m, "ffn_post", sums)
        core.prog.join()
    core.st.skip_banks_to_start()
    core.st.skip_blocks()
    core.prog.join()


def first_constants():
    j, i = np.arange(P)[:, None], np.arange(P)[None, :]
    same = (j // DC) == (i // DC)
    masks = [j <= i, (j <= i) & same, (j < i) & same]
    for level in range(LEVELS):
        s = 1 << level
        masks.append((j // (2 * s) == i // (2 * s)) & (j % (2 * s) < s) & (i % (2 * s) >= s))
    return np.concatenate(masks, axis=1).astype(np.float32)


def columns(a):
    return np.asarray(a).reshape(a.shape[0], -1, P).transpose(0, 2, 1)


def rows(a):
    a = np.asarray(a)
    out = np.zeros((a.shape[0], P, 1), a.dtype)
    out[:, :a.shape[1], 0] = a
    return out


def taps(a):
    a = np.asarray(a)
    return a.reshape(a.shape[0], a.shape[1], -1, P).transpose(0, 3, 2, 1).reshape(a.shape[0], P, -1)


def first_params(v):
    return np.ascontiguousarray(np.concatenate([
        columns(v["ffn1_norm"]), columns(v["mix_norm"]), columns(v["ffn2_norm"]), taps(v["ssm_conv_w"]),
        columns(v["ssm_conv_b"]), columns(np.repeat(np.asarray(v["ssm_d"]), SP, axis=1)), columns(v["ssm_norm"]),
        taps(v["dn_conv_w"]), columns(v["dn_norm"]), rows(v["ssm_dt_bias"]), rows(v["ssm_a_log"]),
        rows(v["dn_dt_bias"]), rows(v["dn_a_log"])], axis=2))


def second_constants():
    q, k = np.arange(P)[:, None], np.arange(P)[None, :]
    own = np.where(k <= q, 0.0, NEG)
    mask = np.concatenate([np.zeros((P, P)), own, own], axis=1)
    half = ROPE // 2
    rot, cos, sin = np.zeros((P, P)), np.ones((P, S), np.float32), np.zeros((P, S), np.float32)
    i = np.arange(half)
    rot[64 + half + i, 64 + i], rot[64 + i, 64 + half + i] = -1.0, 1.0
    inv = np.float32(10000.0) ** (-i.astype(np.float32) / np.float32(half))
    ang = (np.arange(S, dtype=np.float32)[None, :] * inv[:, None]).astype(np.float32)
    cos[64:96], sin[64:96] = np.tile(np.cos(ang), (2, 1)), np.tile(np.sin(ang), (2, 1))
    return np.concatenate([mask, rot, cos, sin], axis=1).astype(np.float32)


def bucket_constants():
    n = np.maximum(S - 1 - np.arange(S + P), 0)
    far = 16 + (np.log(np.maximum(n, 1).astype(np.float32) / np.float32(16)) / np.float32(np.log(64.0))
                * np.float32(16)).astype(np.int32)
    bucket = np.where(n < 16, n, np.minimum(far, 31))
    onehot = np.arange(P)[:, None] == bucket[None, :]
    return np.concatenate([np.eye(P)[::-1], onehot], axis=1).astype(np.float32)


def second_params(v):
    return np.ascontiguousarray(np.concatenate([
        columns(v["ln_mix_pre_2"]), columns(v["ln_mix_post_2"]), columns(v["ln_ffn_pre_2"]),
        columns(v["ln_ffn_post_2"]), rows(v["b_f_2"]), columns(v["q_norm_2"]), columns(v["kv_norm_2"]),
        taps(v["conv_w_2"]), columns(v["conv_b_2"])], axis=2))


WEIGHTS = ("ffn1_w_in", "ffn1_w_out", "w_in", "ssm_w_branch", "dn_w_branch", "w_out", "ffn2_w_in", "ffn2_w_out",
           "w_in_2", "w_uq_2", "w_ukv_2", "w_o_2", "w_up_2", "w_down_2")


def program(nc, io, out, passes):
    with ExitStack() as ctx:
        k = Kernel(nc, ctx, passes)
        PE, ACT, DVE, POOL, SP = k.PE, k.ACT, k.DVE, k.POOL, k.SP
        token = k.tmp[:, :, :].rearrange("p c s -> p (c s)").rearrange("p (t d) -> p t d", t=2)
        k.one_row = k.sb("one_row", [XH_, S])
        ones = POOL.done(nc.gpsimd.memset(k.ones[:, :], 1.0))
        POOL.done(nc.gpsimd.memset(k.one_row[:, :], 1.0))
        POOL.done(nc.gpsimd.memset(k.eps[:, 0:1], EPS))
        POOL.done(nc.gpsimd.memset(k.eps[:, 1:2], -0.5 * float(np.log(DK))))
        k.s_par.inc(nc.sync.dma_start(token, io["x"].rearrange("o (t p) d -> p (o t) d", p=P)), 16)
        k.s_par.inc(nc.sync.dma_start(k.con0[:, :], io["con0"]), 16)
        for e in (PE, ACT, DVE, POOL):
            e.wait(k.s_par.mark(), POOL.own.mark())
        for c in range(ND):
            for t in range(2):
                ins = nc.tensor.transpose(k.banks(0, 4)[:, c * S + t * P:c * S + t * P + P],
                                          token[:, t, c * P:c * P + P], k.ident())
        turned = PE.done(ins)
        DVE.wait(turned)
        DVE.done(nc.vector.tensor_copy(k.h[:, :, :].rearrange("p c s -> p (c s)"), k.banks(0, 4)))
        k.prog.join()
        with ExitStack() as part:
            k.con1, k.pv, k.nega = (k.sb(n, s, ctx=part) for n, s in (
                ("con1", [P, NCON1]), ("pv", [P, NPAR1]), ("nega", [P, 2])))
            k.s_par = Sem(k.prog, "par1_landed")
            k.s_par.inc(nc.sync.dma_start(k.con1[:, :], io["con1"]), 16)
            for e in (ACT, DVE, POOL):
                e.wait(k.s_par.mark())
            with k.prog.loop(L) as l:
                layer1(k, io, l)
        rs, summed = k.inv_rms(k.h[:, :, :], ND, D, k.bank(7), k.rs[:, 0, :])
        DVE.wait(rs, summed)
        for c in range(ND):
            g = k.con0[:, CON0["final_norm"][0] + c:CON0["final_norm"][0] + c + 1]
            DVE.done(nc.vector.scalar_tensor_tensor(k.h[:, c, :], k.h[:, c, :], g, k.rs[:, 0, :], ALU.mult, ALU.mult))
        k.prog.join()
        with ExitStack() as part:
            k.con2, k.pv2, k.t5 = (k.sb(n, s, ctx=part) for n, s in (
                ("con2", [P, NCON2]), ("pv2", [P, NPAR2]), ("t5_bias", [P, AH, S + P])))
            SP.wait(*[s.mark() for s in k.prog.joined])
            k.s_par = Sem(k.prog, "par2_landed")
            k.s_par.inc(nc.sync.dma_start(k.con2[:, :], io["con2"]), 16)
            moba_bias(k, io)
            for e in (PE, ACT, DVE, POOL):
                e.wait(k.s_par.mark())
            with k.prog.loop(L) as l:
                layer2(k, io, l)
        PE.wait(DVE.own.mark())
        for t in range(2):
            for c in range(ND):
                ins = nc.tensor.transpose(k.banks(0, 4)[:, t * D + c * P:t * D + c * P + P],
                                          k.h[:, c, t * P:t * P + P], k.ident())
        turned = PE.done(ins)
        DVE.wait(turned)
        m = DVE.done(nc.vector.tensor_copy(token.rearrange("p t d -> p (t d)"), k.banks(0, 4)))
        SP.wait(m)
        s_out = Sem(k.prog, "out_stored")
        s_out.inc(nc.sync.dma_start(out.rearrange("o (t p) d -> p (o t) d", p=P), token), 16)
        SP.wait(s_out.mark())


def kernel(**inputs):
    import concourse.bacc as bacc
    from concourse.bass_utils import run_bass_kernel_spmd as run

    v = {n: np.asarray(a) for n, a in inputs.items()}
    arrays = {n: np.ascontiguousarray(v[n]) for n in WEIGHTS}
    arrays["x"] = np.ascontiguousarray(v["x"])
    arrays["rel_bias"] = np.ascontiguousarray(v["rel_bias_2"])
    arrays["par1"], arrays["par2"] = first_params(v), second_params(v)
    arrays["con0"] = np.ascontiguousarray(np.concatenate(
        [np.eye(P, dtype=np.float32), v["final_norm"].reshape(ND, P).T], axis=1))
    arrays["con1"], arrays["con2"], arrays["con_t5"] = first_constants(), second_constants(), bucket_constants()
    passes = {}
    for _ in range(2):
        nc = bacc.Bacc("TRN2", target_bir_lowering=False, num_devices=1, dynamic_dma_scratch_size=1024)
        io = {n: nc.dram_tensor("in_" + n, a.shape, F32, kind="ExternalInput").ap() for n, a in arrays.items()}
        io["scratch"] = nc.dram_tensor("bias_scratch", [AH, S + P], F32).ap()
        out = nc.dram_tensor("out", [1, S, D], F32, kind="ExternalOutput").ap()
        program(nc, io, out, passes)
    r = run(nc, [{"in_" + n: a for n, a in arrays.items()}], core_ids=[0])
    return r.results[0]["out"]
```
